# Optimizing a Trainium2 kernel written in Bass

```python
import math
import jax, jax.numpy as jnp
from jax import lax
import numpy as np

D_MODEL = 1024
BATCH = 1
SEQ = 256
DEPTH = 1

HEAD_DIM = 64
SWA_HEADS = 8
SWA_KV_HEADS = 2
SWA_WINDOW = 128
SWA_BLOCK = 128
RNN_WIDTH = D_MODEL
RNN_BLOCKS = 16
RNN_BLOCK_WIDTH = RNN_WIDTH // RNN_BLOCKS
RNN_CONV = 4
RGLRU_C = 8.0
MOBA_HEADS = 8
MOBA_BLOCK = 256
MOBA_TOPK = 3
NUM_BUCKETS = 32
MAX_DISTANCE = 2048
D_FF = 2816
FFN_CONV = 3

RMS_EPS = 1e-6
NEG_INF = -1e30
N_BRANCH = 3
SWA_Q = SWA_HEADS * HEAD_DIM
SWA_KV = SWA_KV_HEADS * HEAD_DIM
MOBA_W = MOBA_HEADS * HEAD_DIM
IN_WIDTHS = (SWA_Q, SWA_KV, SWA_KV, RNN_WIDTH, RNN_WIDTH, MOBA_W, MOBA_W, MOBA_W, N_BRANCH * D_MODEL)
IN_OFFSETS = tuple(sum(IN_WIDTHS[:i + 1]) for i in range(len(IN_WIDTHS) - 1))
D_IN = sum(IN_WIDTHS)
D_MIX = SWA_Q + RNN_WIDTH + MOBA_W


def rms_norm(x, gain):
    xf = x.astype(jnp.float32)
    y = xf * lax.rsqrt(jnp.mean(xf * xf, axis=-1, keepdims=True) + RMS_EPS)
    return (y * gain.astype(jnp.float32)).astype(x.dtype)

def t5_bucket(dist):
    dist = jnp.maximum(dist, 0)
    max_exact = NUM_BUCKETS // 2
    log_ratio = jnp.log(jnp.maximum(dist, 1).astype(jnp.float32) / max_exact) / math.log(MAX_DISTANCE / max_exact)
    large = max_exact + (log_ratio * (NUM_BUCKETS - max_exact)).astype(jnp.int32)
    large = jnp.minimum(large, NUM_BUCKETS - 1)
    return jnp.where(dist < max_exact, dist, large)

def causal_dwconv(x, w, b):
    k_width = w.shape[0]
    s = x.shape[1]
    xp = jnp.pad(x, ((0, 0), (k_width - 1, 0), (0, 0)))
    return sum(xp[:, k:k + s] * w[k] for k in range(k_width)) + b

def swa_attention(q, k, v, sinks, bias_a):
    b_sz, s_len = q.shape[:2]
    L = SWA_BLOCK
    nblk = s_len // L
    grp = SWA_HEADS // SWA_KV_HEADS
    qb = q.reshape(b_sz, nblk, L, SWA_KV_HEADS, grp, HEAD_DIM)

    def band(t):
        tp = jnp.pad(t, ((0, 0), (L, 0), (0, 0), (0, 0))).reshape(b_sz, nblk + 1, L, SWA_KV_HEADS, HEAD_DIM)
        return jnp.concatenate([tp[:, :-1], tp[:, 1:]], axis=2)

    kb, vb = band(k), band(v)
    s = jnp.einsum('bnqkgd,bnskd->bnkgqs', qb, kb).astype(jnp.float32) * (HEAD_DIM ** -0.5)
    qi = jnp.arange(L)
    sj = jnp.arange(2 * L)
    diff = qi[:, None] + L - sj[None, :]
    bias = bias_a[t5_bucket(diff)].astype(jnp.float32).transpose(2, 0, 1).reshape(SWA_KV_HEADS, grp, L, 2 * L)
    key_pos = jnp.arange(nblk)[:, None] * L - L + sj[None, :]
    valid = ((diff >= 0) & (diff < SWA_WINDOW))[None] & (key_pos >= 0)[:, None, :]
    s = jnp.where(valid[None, :, None, None], s + bias, NEG_INF)
    sink = sinks.astype(jnp.float32).reshape(SWA_KV_HEADS, grp)[:, :, None, None]
    m = jnp.maximum(jnp.max(s, axis=-1, keepdims=True), sink)
    p = jnp.exp(s - m)
    p = p / (jnp.sum(p, axis=-1, keepdims=True) + jnp.exp(sink - m))
    o = jnp.einsum('bnkgqs,bnskd->bnqkgd', p.astype(v.dtype), vb)
    return o.reshape(b_sz, s_len, SWA_Q)

def rg_lru(x, ga_w, ga_b, gx_w, gx_b, lam):
    b_sz, s_len, width = x.shape
    xb = x.reshape(b_sz, s_len, RNN_BLOCKS, RNN_BLOCK_WIDTH)
    r = jax.nn.sigmoid(jnp.einsum('bsnc,ncd->bsnd', xb, ga_w).reshape(b_sz, s_len, width) + ga_b)
    i = jax.nn.sigmoid(jnp.einsum('bsnc,ncd->bsnd', xb, gx_w).reshape(b_sz, s_len, width) + gx_b)
    log_a = -RGLRU_C * r.astype(jnp.float32) * jax.nn.softplus(-lam.astype(jnp.float32))
    a = jnp.exp(log_a)
    mult = jnp.sqrt(-jnp.expm1(2.0 * log_a))
    mult = jnp.where((jnp.arange(s_len) == 0)[None, :, None], 1.0, mult)
    u = mult * (i * x).astype(jnp.float32)

    def combine(left, right):
        a_l, b_l = left
        a_r, b_r = right
        return (a_l * a_r, a_r * b_l + b_r)

    _, h = lax.associative_scan(combine, (a, u), axis=1)
    return h.astype(x.dtype)

def moba_attention(q, k, v, bias_c):
    b_sz, s_len = q.shape[:2]
    MB = MOBA_BLOCK
    nb = -(-s_len // MB)
    s_pad = nb * MB
    pad = ((0, 0), (0, s_pad - s_len), (0, 0), (0, 0))
    q, k, v = jnp.pad(q, pad), jnp.pad(k, pad), jnp.pad(v, pad)
    topk = min(MOBA_TOPK, nb)
    kb = k.reshape(b_sz, nb, MB, MOBA_HEADS, HEAD_DIM)
    vb = v.reshape(b_sz, nb, MB, MOBA_HEADS, HEAD_DIM)
    k_mean = jnp.mean(kb.astype(jnp.float32), axis=2).astype(k.dtype)
    k_bh = kb.transpose(0, 3, 1, 2, 4)
    v_bh = vb.transpose(0, 3, 1, 2, 4)
    q_chunks = q.reshape(b_sz, nb, MB, MOBA_HEADS, HEAD_DIM).transpose(1, 0, 2, 3, 4)
    k_own = kb.transpose(1, 0, 2, 3, 4)
    v_own = vb.transpose(1, 0, 2, 3, 4)
    pos = jnp.arange(MB)
    own_diff = pos[:, None] - pos[None, :]
    own_mask = own_diff >= 0
    own_bias = bias_c[t5_bucket(own_diff)].astype(jnp.float32).transpose(0, 2, 1)
    b_ix = jnp.arange(b_sz)[:, None, None, None]
    h_ix = jnp.arange(MOBA_HEADS)[None, None, :, None]
    blk_ids = jnp.arange(nb)
    scale = HEAD_DIM ** -0.5

    def one_block(args):
        n, q_c, k_c, v_c = args
        gate = jnp.einsum('bqhd,bmhd->bqhm', q_c, k_mean).astype(jnp.float32)
        gate = jnp.where(blk_ids < n, gate, NEG_INF)
        _, sel = lax.top_k(gate, topk)
        sel_valid = sel < n
        k_sel = k_bh[b_ix, h_ix, sel]
        v_sel = v_bh[b_ix, h_ix, sel]
        s_sel = jnp.einsum('bqhd,bqhtsd->bqhts', q_c, k_sel).astype(jnp.float32) * scale
        dist = (n * MB + pos)[None, :, None, None, None] - (sel[..., None] * MB + pos)
        s_sel = s_sel + bias_c[t5_bucket(dist), h_ix[..., None]].astype(jnp.float32)
        s_sel = jnp.where(sel_valid[..., None], s_sel, NEG_INF).reshape(b_sz, MB, MOBA_HEADS, topk * MB)
        s_own = jnp.einsum('bqhd,bshd->bqhs', q_c, k_c).astype(jnp.float32) * scale + own_bias
        s_own = jnp.where(own_mask[:, None, :], s_own, NEG_INF)
        p = jax.nn.softmax(jnp.concatenate([s_sel, s_own], axis=-1), axis=-1).astype(v.dtype)
        p_sel = p[..., :topk * MB].reshape(b_sz, MB, MOBA_HEADS, topk, MB)
        p_own = p[..., topk * MB:]
        return jnp.einsum('bqhts,bqhtsd->bqhd', p_sel, v_sel) + jnp.einsum('bqhs,bshd->bqhd', p_own, v_c)

    o = lax.map(one_block, (blk_ids, q_chunks, k_own, v_own))
    return o.transpose(1, 0, 2, 3, 4).reshape(b_sz, s_pad, MOBA_W)[:, :s_len]

def first_inputs(seed: int = 0) -> dict:
    key = jax.random.key(seed)
    ks = jax.random.split(key, 32)
    f32 = jnp.float32

    def nrm(k, shape, fan_in, scale=1.0):
        return jax.random.normal(k, shape, f32) * (scale * fan_in ** -0.5)

    def gain(k, shape):
        return 1.0 + 0.05 * jax.random.normal(k, shape, f32)

    def small(k, shape, scale=0.02):
        return scale * jax.random.normal(k, shape, f32)

    a_init = jax.random.uniform(ks[16], (DEPTH, RNN_WIDTH), f32, 0.9, 0.999)
    w_branch = jnp.concatenate([
        nrm(ks[20], (DEPTH, SWA_Q, D_MODEL), SWA_Q),
        nrm(ks[21], (DEPTH, RNN_WIDTH, D_MODEL), RNN_WIDTH),
        nrm(ks[22], (DEPTH, MOBA_W, D_MODEL), MOBA_W)], axis=1)
    return {
        'x': jax.random.normal(ks[0], (BATCH, SEQ, D_MODEL), f32),
        'c': jax.random.normal(ks[1], (BATCH, D_MODEL), f32),
        'w_mod': nrm(ks[2], (DEPTH, D_MODEL, 6 * D_MODEL), D_MODEL, 0.5),
        'b_mod': small(ks[3], (DEPTH, 6 * D_MODEL)),
        'norm_mix': gain(ks[4], (DEPTH, D_MODEL)),
        'norm_ffn': gain(ks[5], (DEPTH, D_MODEL)),
        'w_in': nrm(ks[6], (DEPTH, D_MODEL, D_IN), D_MODEL),
        'qnorm_a': gain(ks[7], (DEPTH, HEAD_DIM)),
        'knorm_a': gain(ks[8], (DEPTH, HEAD_DIM)),
        'sinks': small(ks[9], (DEPTH, SWA_HEADS), 0.5),
        'rnn_conv_w': nrm(ks[10], (DEPTH, RNN_CONV, RNN_WIDTH), RNN_CONV),
        'rnn_conv_b': small(ks[11], (DEPTH, RNN_WIDTH)),
        'rnn_gate_a_w': nrm(ks[12], (DEPTH, RNN_BLOCKS, RNN_BLOCK_WIDTH, RNN_BLOCK_WIDTH), RNN_BLOCK_WIDTH),
        'rnn_gate_a_b': small(ks[13], (DEPTH, RNN_WIDTH)),
        'rnn_gate_x_w': nrm(ks[14], (DEPTH, RNN_BLOCKS, RNN_BLOCK_WIDTH, RNN_BLOCK_WIDTH), RNN_BLOCK_WIDTH),
        'rnn_gate_x_b': small(ks[15], (DEPTH, RNN_WIDTH)),
        'rnn_lambda': jnp.log(a_init) - jnp.log1p(-a_init),
        'qnorm_c': gain(ks[17], (DEPTH, HEAD_DIM)),
        'knorm_c': gain(ks[18], (DEPTH, HEAD_DIM)),
        'rel_bias': small(ks[19], (NUM_BUCKETS, SWA_HEADS + MOBA_HEADS), 0.5),
        'w_branch': w_branch,
        'w_out': nrm(ks[23], (DEPTH, D_MODEL, D_MODEL), D_MODEL),
        'w_up': nrm(ks[24], (DEPTH, D_MODEL, 2 * D_FF), D_MODEL),
        'ffn_conv_w': nrm(ks[25], (DEPTH, FFN_CONV, 2 * D_FF), FFN_CONV),
        'ffn_conv_b': small(ks[26], (DEPTH, 2 * D_FF)),
        'w_down': nrm(ks[27], (DEPTH, D_FF, D_MODEL), D_FF),
    }

def first_block(x, c, w_mod, b_mod, norm_mix, norm_ffn, w_in, qnorm_a, knorm_a, sinks,
              rnn_conv_w, rnn_conv_b, rnn_gate_a_w, rnn_gate_a_b, rnn_gate_x_w, rnn_gate_x_b,
              rnn_lambda, qnorm_c, knorm_c, rel_bias, w_branch, w_out, w_up, ffn_conv_w,
              ffn_conv_b, w_down):
    b_sz, s_len, _ = x.shape
    c_act = jax.nn.silu(c)
    bias_a = rel_bias[:, :SWA_HEADS]
    bias_c = rel_bias[:, SWA_HEADS:]
    for l in range(DEPTH):
        mod = (c_act @ w_mod[l] + b_mod[l])[:, None, :]
        shift_m, scale_m, gate_m, shift_f, scale_f, gate_f = jnp.split(mod, 6, axis=-1)

        h = rms_norm(x, norm_mix[l]) * (1.0 + scale_m) + shift_m
        z = h @ w_in[l]
        qa, ka, va, xr, yr, qc, kc, vc, g_logits = jnp.split(z, IN_OFFSETS, axis=-1)

        qa = rms_norm(qa.reshape(b_sz, s_len, SWA_HEADS, HEAD_DIM), qnorm_a[l])
        ka = rms_norm(ka.reshape(b_sz, s_len, SWA_KV_HEADS, HEAD_DIM), knorm_a[l])
        va = va.reshape(b_sz, s_len, SWA_KV_HEADS, HEAD_DIM)
        o_a = swa_attention(qa, ka, va, sinks[l], bias_a)

        xr = causal_dwconv(xr, rnn_conv_w[l], rnn_conv_b[l])
        hr = rg_lru(xr, rnn_gate_a_w[l], rnn_gate_a_b[l], rnn_gate_x_w[l], rnn_gate_x_b[l], rnn_lambda[l])
        o_b = hr * jax.nn.gelu(yr)

        qc = rms_norm(qc.reshape(b_sz, s_len, MOBA_HEADS, HEAD_DIM), qnorm_c[l])
        kc = rms_norm(kc.reshape(b_sz, s_len, MOBA_HEADS, HEAD_DIM), knorm_c[l])
        vc = vc.reshape(b_sz, s_len, MOBA_HEADS, HEAD_DIM)
        o_c = moba_attention(qc, kc, vc, bias_c)

        wb = w_branch[l]
        p_a = o_a @ wb[:SWA_Q]
        p_b = o_b @ wb[SWA_Q:SWA_Q + RNN_WIDTH]
        p_c = o_c @ wb[SWA_Q + RNN_WIDTH:]
        g = jax.nn.sigmoid(g_logits.reshape(b_sz, s_len, N_BRANCH, D_MODEL))
        merged = g[:, :, 0] * p_a + g[:, :, 1] * p_b + g[:, :, 2] * p_c
        x = x + gate_m * (merged @ w_out[l])

        h = rms_norm(x, norm_ffn[l]) * (1.0 + scale_f) + shift_f
        u = causal_dwconv(h @ w_up[l], ffn_conv_w[l], ffn_conv_b[l])
        u_gate, u_val = jnp.split(u, 2, axis=-1)
        x = x + gate_f * ((jax.nn.silu(u_gate) * u_val) @ w_down[l])
    return x


DEPTH_2 = 2

CHUNK = 64
MEM_LEN = 256
HEAD_GROUP = 64
A_WIDTH = 384
B_WIDTH = 320
C_WIDTH = 320
MIX_WIDTH = A_WIDTH + B_WIDTH + C_WIDTH
N_MIX_GROUPS = MIX_WIDTH // HEAD_GROUP
C_GROUPS = C_WIDTH // HEAD_GROUP
A_KERNEL = 31
B_KERNEL = 3
GMLP_BLOCK = 128
PROJ_WIDTH = 2 * A_WIDTH + 3 * B_WIDTH + 2 * C_WIDTH
X_HEADS = 4
X_HEAD_DIM = D_MODEL // X_HEADS
N_EXPERTS = 8
TOP_K = 2
D_EXPERT = 3584
N_DENSE = (DEPTH_2 + 1) // 2
N_MOE = DEPTH_2 // 2
EPS = 1e-6


def rmsnorm(x, g):
    xf = x.astype(jnp.float32)
    y = xf * lax.rsqrt(jnp.mean(xf * xf, axis=-1, keepdims=True) + EPS)
    return (y * g.astype(jnp.float32)).astype(x.dtype)

def layernorm(x, g, b):
    xf = x.astype(jnp.float32)
    mu = jnp.mean(xf, axis=-1, keepdims=True)
    xc = xf - mu
    var = jnp.mean(xc * xc, axis=-1, keepdims=True)
    y = xc * lax.rsqrt(var + EPS) * g.astype(jnp.float32) + b.astype(jnp.float32)
    return y.astype(x.dtype)

def causal_depthwise_conv(x, w):
    k, c = w.shape
    return lax.conv_general_dilated(
        x, w[:, None, :], window_strides=(1,), padding=[(k - 1, 0)],
        dimension_numbers=("NWC", "WIO", "NWC"), feature_group_count=c)

def chunk_spatial_gate(u, v, ws, bias):
    bsz, s, c = v.shape
    n_blocks = s // GMLP_BLOCK
    chunk_id = jnp.arange(GMLP_BLOCK) // CHUNK
    mask = chunk_id[:, None] >= chunk_id[None, :]
    ws = jnp.where(mask[None], ws, jnp.zeros((), ws.dtype))
    vb = v.reshape(bsz, n_blocks, GMLP_BLOCK, C_GROUPS, HEAD_GROUP)
    mixed = jnp.einsum("gij,bnjgc->bnigc", ws, vb) + bias.T[None, None, :, :, None]
    return u * mixed.reshape(bsz, s, c)

def hybrid_mixer(xn, w_in, conv_a_w, conv_a_b, ln_a_g, ln_a_b, conv_b_w,
                 ln_c_g, ln_c_b, gmlp_ws, gmlp_b, mix_out_g, w_mix_out):
    z = xn @ w_in
    splits = [A_WIDTH, 2 * A_WIDTH, 2 * A_WIDTH + B_WIDTH,
              2 * A_WIDTH + 2 * B_WIDTH, 2 * A_WIDTH + 3 * B_WIDTH]
    a_val, a_gate, b_gate, c_gate, b_in, c_z = jnp.split(z, splits, axis=-1)
    ya = a_val * jax.nn.sigmoid(a_gate)
    ya = causal_depthwise_conv(ya, conv_a_w) + conv_a_b
    ya = jax.nn.silu(layernorm(ya, ln_a_g, ln_a_b))
    yb = b_gate * causal_depthwise_conv(c_gate * b_in, conv_b_w)
    c_z = jax.nn.gelu(c_z)
    c_u, c_v = jnp.split(c_z, 2, axis=-1)
    c_v = layernorm(c_v, ln_c_g, ln_c_b)
    yc = chunk_spatial_gate(c_u, c_v, gmlp_ws, gmlp_b)
    y = jnp.concatenate([ya, yb, yc], axis=-1)
    bsz, s, _ = y.shape
    y = rmsnorm(y.reshape(bsz, s, N_MIX_GROUPS, HEAD_GROUP),
                mix_out_g.reshape(N_MIX_GROUPS, HEAD_GROUP)).reshape(bsz, s, MIX_WIDTH)
    return y @ w_mix_out

def memory_cross_attention(xn, memn, w_xq, w_xkv, w_xo):
    bsz, s, _ = xn.shape
    m = memn.shape[1]
    q = (xn @ w_xq).reshape(bsz, s, X_HEADS, X_HEAD_DIM)
    k, v = jnp.split(memn @ w_xkv, 2, axis=-1)
    k = k.reshape(bsz, m, X_HEADS, X_HEAD_DIM)
    v = v.reshape(bsz, m, X_HEADS, X_HEAD_DIM)
    scores = jnp.einsum("bshd,bmhd->bhsm", q, k).astype(jnp.float32) * (X_HEAD_DIM ** -0.5)
    p = jax.nn.softmax(scores, axis=-1).astype(v.dtype)
    o = jnp.einsum("bhsm,bmhd->bshd", p, v).reshape(bsz, s, D_MODEL)
    return o @ w_xo

def swiglu(x, w_gate, w_up, w_down):
    return (jax.nn.silu(x @ w_gate) * (x @ w_up)) @ w_down

def moe_swiglu(xn, w_router, w_gate, w_up, w_down):
    bsz, s, d = xn.shape
    xt = xn.reshape(-1, d)
    logits = (xt @ w_router).astype(jnp.float32)
    top_vals, top_idx = lax.top_k(logits, TOP_K)
    top_w = jax.nn.softmax(top_vals, axis=-1)
    combine = jnp.sum(jax.nn.one_hot(top_idx, N_EXPERTS, dtype=jnp.float32) * top_w[..., None], axis=1)
    combine = combine.astype(xn.dtype)
    y = jnp.zeros_like(xt)
    for e in range(N_EXPERTS):
        y = y + combine[:, e:e + 1] * swiglu(xt, w_gate[e], w_up[e], w_down[e])
    return y.reshape(bsz, s, d)

def second_inputs(seed: int = 0) -> dict:
    key = jax.random.key(seed)
    ks = jax.random.split(key, 32)
    f32 = jnp.float32

    def nrm(k, shape, scale):
        return jax.random.normal(k, shape, f32) * scale

    def gain(k, shape):
        return 1.0 + 0.02 * jax.random.normal(k, shape, f32)

    return {
        "x": nrm(ks[0], (BATCH, SEQ, D_MODEL), 1.0),
        "mem": nrm(ks[1], (BATCH, MEM_LEN, D_MODEL), 1.0),
        "norm_mix_g": gain(ks[2], (DEPTH_2, D_MODEL)),
        "w_in": nrm(ks[3], (DEPTH_2, D_MODEL, PROJ_WIDTH), D_MODEL ** -0.5),
        "conv_a_w": nrm(ks[4], (DEPTH_2, A_KERNEL, A_WIDTH), A_KERNEL ** -0.5),
        "conv_a_b": nrm(ks[5], (DEPTH_2, A_WIDTH), 0.02),
        "ln_a_g": gain(ks[6], (DEPTH_2, A_WIDTH)),
        "ln_a_b": nrm(ks[7], (DEPTH_2, A_WIDTH), 0.02),
        "conv_b_w": nrm(ks[8], (DEPTH_2, B_KERNEL, B_WIDTH), B_KERNEL ** -0.5),
        "ln_c_g": gain(ks[9], (DEPTH_2, C_WIDTH)),
        "ln_c_b": nrm(ks[10], (DEPTH_2, C_WIDTH), 0.02),
        "gmlp_ws": nrm(ks[11], (DEPTH_2, C_GROUPS, GMLP_BLOCK, GMLP_BLOCK), GMLP_BLOCK ** -0.5),
        "gmlp_b": 1.0 + nrm(ks[12], (DEPTH_2, C_GROUPS, GMLP_BLOCK), 0.1),
        "mix_out_g": gain(ks[13], (DEPTH_2, MIX_WIDTH)),
        "w_mix_out": nrm(ks[14], (DEPTH_2, MIX_WIDTH, D_MODEL), MIX_WIDTH ** -0.5),
        "norm_x_g": gain(ks[15], (DEPTH_2, D_MODEL)),
        "norm_mem_g": gain(ks[16], (DEPTH_2, D_MODEL)),
        "w_xq": nrm(ks[17], (DEPTH_2, D_MODEL, D_MODEL), D_MODEL ** -0.5),
        "w_xkv": nrm(ks[18], (DEPTH_2, D_MODEL, 2 * D_MODEL), D_MODEL ** -0.5),
        "w_xo": nrm(ks[19], (DEPTH_2, D_MODEL, D_MODEL), D_MODEL ** -0.5),
        "norm_ffn_g": gain(ks[20], (DEPTH_2, D_MODEL)),
        "ffn_w_gate": nrm(ks[21], (N_DENSE, D_MODEL, D_FF), D_MODEL ** -0.5),
        "ffn_w_up": nrm(ks[22], (N_DENSE, D_MODEL, D_FF), D_MODEL ** -0.5),
        "ffn_w_down": nrm(ks[23], (N_DENSE, D_FF, D_MODEL), D_FF ** -0.5),
        "moe_router": nrm(ks[24], (N_MOE, D_MODEL, N_EXPERTS), D_MODEL ** -0.5),
        "moe_w_gate": nrm(ks[25], (N_MOE, N_EXPERTS, D_MODEL, D_EXPERT), D_MODEL ** -0.5),
        "moe_w_up": nrm(ks[26], (N_MOE, N_EXPERTS, D_MODEL, D_EXPERT), D_MODEL ** -0.5),
        "moe_w_down": nrm(ks[27], (N_MOE, N_EXPERTS, D_EXPERT, D_MODEL), D_EXPERT ** -0.5),
        "norm_final_g": gain(ks[28], (D_MODEL,)),
    }

def second_block(x, mem, norm_mix_g, w_in, conv_a_w, conv_a_b, ln_a_g, ln_a_b, conv_b_w,
              ln_c_g, ln_c_b, gmlp_ws, gmlp_b, mix_out_g, w_mix_out, norm_x_g, norm_mem_g,
              w_xq, w_xkv, w_xo, norm_ffn_g, ffn_w_gate, ffn_w_up, ffn_w_down,
              moe_router, moe_w_gate, moe_w_up, moe_w_down, norm_final_g):
    h = x
    for layer in range(DEPTH_2):
        h = h + hybrid_mixer(rmsnorm(h, norm_mix_g[layer]), w_in[layer], conv_a_w[layer],
                             conv_a_b[layer], ln_a_g[layer], ln_a_b[layer], conv_b_w[layer],
                             ln_c_g[layer], ln_c_b[layer], gmlp_ws[layer], gmlp_b[layer],
                             mix_out_g[layer], w_mix_out[layer])
        h = h + memory_cross_attention(rmsnorm(h, norm_x_g[layer]), rmsnorm(mem, norm_mem_g[layer]),
                                       w_xq[layer], w_xkv[layer], w_xo[layer])
        hn = rmsnorm(h, norm_ffn_g[layer])
        i = layer // 2
        if layer % 2 == 0:
            h = h + swiglu(hn, ffn_w_gate[i], ffn_w_up[i], ffn_w_down[i])
        else:
            h = h + moe_swiglu(hn, moe_router[i], moe_w_gate[i], moe_w_up[i], moe_w_down[i])
    return rmsnorm(h, norm_final_g)


def setup_inputs(seed=0):
    out = dict(first_inputs(seed))
    for name, value in second_inputs(seed + 1).items():
        if name != "x":
            out[name + "_2"] = value
    return out


def reference(
    x, c, w_mod, b_mod, norm_mix, norm_ffn, w_in, qnorm_a, knorm_a, sinks, rnn_conv_w,
    rnn_conv_b, rnn_gate_a_w, rnn_gate_a_b, rnn_gate_x_w, rnn_gate_x_b, rnn_lambda, qnorm_c,
    knorm_c, rel_bias, w_branch, w_out, w_up, ffn_conv_w, ffn_conv_b, w_down, mem_2,
    norm_mix_g_2, w_in_2, conv_a_w_2, conv_a_b_2, ln_a_g_2, ln_a_b_2, conv_b_w_2, ln_c_g_2,
    ln_c_b_2, gmlp_ws_2, gmlp_b_2, mix_out_g_2, w_mix_out_2, norm_x_g_2, norm_mem_g_2, w_xq_2,
    w_xkv_2, w_xo_2, norm_ffn_g_2, ffn_w_gate_2, ffn_w_up_2, ffn_w_down_2, moe_router_2,
    moe_w_gate_2, moe_w_up_2, moe_w_down_2, norm_final_g_2,
):
    x = first_block(
        x, c, w_mod, b_mod, norm_mix, norm_ffn, w_in, qnorm_a, knorm_a, sinks, rnn_conv_w,
        rnn_conv_b, rnn_gate_a_w, rnn_gate_a_b, rnn_gate_x_w, rnn_gate_x_b, rnn_lambda, qnorm_c,
        knorm_c, rel_bias, w_branch, w_out, w_up, ffn_conv_w, ffn_conv_b, w_down,
    )
    return second_block(
        x, mem_2, norm_mix_g_2, w_in_2, conv_a_w_2, conv_a_b_2, ln_a_g_2, ln_a_b_2, conv_b_w_2,
        ln_c_g_2, ln_c_b_2, gmlp_ws_2, gmlp_b_2, mix_out_g_2, w_mix_out_2, norm_x_g_2,
        norm_mem_g_2, w_xq_2, w_xkv_2, w_xo_2, norm_ffn_g_2, ffn_w_gate_2, ffn_w_up_2,
        ffn_w_down_2, moe_router_2, moe_w_gate_2, moe_w_up_2, moe_w_down_2, norm_final_g_2,
    )


_drawn_inputs = setup_inputs


def setup_inputs(seed=0):
    import zlib

    import numpy as np

    out = dict(_drawn_inputs(seed))
    spreads = {}
    factors = {'norm_mix': 2.819,
     'qnorm_a': 4.773,
     'knorm_a': 8.0,
     'sinks': 5.302,
     'rnn_conv_b': 4.051,
     'rnn_gate_a_b': 8.0,
     'rnn_gate_x_b': 8.0,
     'qnorm_c': 6.119,
     'knorm_c': 8.0,
     'ffn_conv_b': 4.348,
     'ln_a_g_2': 3.002,
     'ln_a_b_2': 3.082,
     'ln_c_g_2': 3.085,
     'ln_c_b_2': 4.079,
     'norm_x_g_2': 7.356,
     'norm_mem_g_2': 4.947,
     'norm_final_g_2': 8.449,
     'norm_ffn_g_2': 3.677}
    for name, (base, spread) in spreads.items():
        noise = np.random.default_rng([zlib.crc32(name.encode()), seed]).standard_normal(out[name].shape)
        drawn = base * np.exp(spread * noise) if base else spread * noise
        out[name] = __import__('jax').numpy.asarray(drawn.astype(out[name].dtype))
    for name, factor in factors.items():
        out[name] = (out[name] * factor).astype(out[name].dtype)
    return out
```

```python
from contextlib import ExitStack

import numpy as np
import concourse.bass as bass
from concourse import mybir

ALU = mybir.AluOpType
ACT = mybir.ActivationFunctionType
F32 = mybir.dt.float32
F32R = mybir.dt.float32r
U32 = mybir.dt.uint32
I32 = mybir.dt.int32
AX_X = mybir.AxisListType.X

P = 128
T = 256
TB = T // P
D = 1024
DC = D // P
HD = 64
NHEAD = 16
FF = 2816
FC = FF // P
EPS = 1e-6
NEG = -1e30
WIN = 128
NE = 8
DE = 3584
JE = DE // 512
TAPS_A = 31
SLOT = 2048
RAW = 6
SPLIT = 3
PAIRS = 2
MOE_SLOTS = 6 * JE

QA, KA, VA, XR, YR, QC, KC, VC, GL = 0, 512, 640, 768, 1792, 2816, 3328, 3840, 4352
A_VAL, A_GATE, B_GATE, C_GATE, B_IN, C_U, C_V = 0, 384, 768, 1088, 1408, 1728, 2048

VEC = [("c", 8), ("b_mod", 48), ("norm_mix", 8), ("norm_ffn", 8), ("rnn_conv_w", 32), ("rnn_conv_b", 8),
       ("rnn_gate_a_b", 8), ("rnn_gate_x_b", 8), ("rnn_lambda", 8),
       ("ffn_conv_w", 132), ("ffn_conv_b", 44),
       ("norm_mix_g_2", 16), ("norm_x_g_2", 16), ("norm_mem_g_2", 16), ("norm_ffn_g_2", 16), ("norm_final_g_2", 8),
       ("conv_a_w_2", 186), ("conv_a_b_2", 6), ("ln_a_g_2", 6), ("ln_a_b_2", 6), ("mix_out_g_2", 16),
       ("conv_b_w_2", 18), ("ln_c_g_2", 6), ("ln_c_b_2", 6),
       ("qnorm_a", 1), ("knorm_a", 1), ("qnorm_c", 1), ("knorm_c", 1)]
PIECEWISE = ("conv_b_w_2", "ln_c_g_2", "ln_c_b_2")
DOUBLED = ("qnorm_a", "knorm_a", "qnorm_c", "knorm_c")
VROW = {}
_at = 0
for _n, _r in VEC:
    VROW[_n] = _at
    _at += _r
N_VEC = _at
NV = -(-_at // P)


def vec_dmas():
    n = 0
    for name, rows in VEC:
        r = VROW[name]
        n += 2 if name in DOUBLED else 3 if name in PIECEWISE else (r + rows - 1) // P - r // P + 1
    return n


N_VEC_DMAS = vec_dmas()

SUMS = ["mix", "ffn"] + [f"{k}{l}" for l in range(2) for k in ("mix", "v", "a", "y", "x", "ffn")]
ROOTS = SUMS[:1] + ["qk"] + SUMS[1:]
NORM = {"mix": 0, "ffn": 1, "mix0": 2, "x0": 3, "ffn0": 4, "mix1": 5, "x1": 6, "ffn1": 7}


def bucket_onehot():
    dist = np.arange(T)
    large = 16 + (np.log(np.maximum(dist, 1).astype(np.float32) / 16) / np.float32(np.log(2048 / 16)) * 16).astype(np.int32)
    bucket = np.where(dist < 16, dist, np.minimum(large, 31))
    out = np.zeros((32, T), np.float32)
    out[bucket, T - 1 - dist] = 1.0
    return out


def plan(w):
    groups = []

    def rows(src, k0, n):
        return src[k0 * P:(k0 + n) * P, :]

    def dense(stage, src, cols, reader, kchunks=DC, k0=0):
        slots = []
        for c0 in range(0, kchunks, 8):
            n = min(8, kchunks - c0)
            parts, at = [], 0
            for col, width in cols:
                parts.append((rows(src, k0 + c0, n), 0, n, col, width, at))
                at += width
            slots.append((parts, n))
        groups.append((stage, slots, reader))

    w_in = w["w_in"][0]
    for j in range(8):
        dense("mod1", w["w_mod"][0], [(j * 256, 256)], None)
    for j in range(2):
        dense("qa", w_in, [(QA + j * 256, 256)], "act")
    dense("ka", w_in, [(KA, 64), (KA, 64), (KA + 64, 64), (KA + 64, 64)], "act")
    for j in range(2):
        dense("qc", w_in, [(QC + j * 256, 256)], "act")
    for j in range(2):
        dense("kc", w_in, [(KC + j * 256, 256)], "act")
    dense("va", w_in, [(VA, 128)], "act")
    for j in range(2):
        dense("vc", w_in, [(VC + j * 256, 256)], "act")
    for j in range(4):
        dense("xr", w_in, [(XR + j * 256, 256)], "act")
    for j in range(4):
        dense("yr", w_in, [(YR + j * 256, 256)], "act")
    for j in range(8, 24):
        dense("mod2", w["w_mod"][0], [(j * 256, 256)], None)
    wb = w["w_branch"][0]
    for j in range(4):
        for b in range(3):
            dense("g", w_in, [(GL + b * D + j * 256, 256)], "act")
        parts = [(rows(wb, 0, 4), 0, 4, j * 256, 256, 0), (rows(wb, 12, 4), 4, 4, j * 256, 256, 0)]
        groups.append(("branch_ac", [(parts, 8)], "dve"))
        dense("branch_b", wb, [(j * 256, 256)], "dve", k0=4)
    for j in range(4):
        dense("w_out", w["w_out"][0], [(j * 256, 256)], "dve")
    for j in range(FC):
        dense("up", w["w_up"][0], [(j * P, P), (FF + j * P, P)], "dve")
    for j in range(4):
        dense("down", w["w_down"][0], [(j * 256, 256)], "dve", FC)
    for l in range(2):
        wi = w["w_in_2"][l]
        for t in range(3):
            dense(f"mixa{l}", wi, [(A_VAL + t * P, P), (A_GATE + t * P, P)], "dve")
        dense(f"mix_bg{l}", wi, [(B_GATE, 256)], "act")
        dense(f"mix_bgcg{l}", wi, [(B_GATE + 256, P), (C_GATE + 256, P)], "act")
        dense(f"mix_cg{l}", wi, [(C_GATE, 256)], "act")
        dense(f"mix_bin{l}", wi, [(B_IN, 256)], "dve")
        dense(f"mix_binuv{l}", wi, [(B_IN + 256, P), (C_V + 192, P)], "dve")
        dense(f"mix_u{l}", wi, [(C_U + 64, 256)], "act")
        dense(f"mix_v{l}", wi, [(C_V - 64, 256)], "act")
        for j in range(4):
            dense(f"mixout{l}", w["w_mix_out_2"][l], [(j * 256, 256)], "dve")
        for j in range(4):
            dense(f"xk{l}", w["w_xkv_2"][l], [(j * 256, 256)], "act")
        for j in range(4):
            dense(f"xv{l}", w["w_xkv_2"][l], [(D + j * 256, 256)], "act")
        for j in range(4):
            dense(f"xq{l}", w["w_xq_2"][l], [(j * 256, 256)], "act")
        for j in range(4):
            dense(f"xo{l}", w["w_xo_2"][l], [(j * 256, 256)], "dve")
        if l == 0:
            for j in range(FC):
                slot = [(w["ffn_w_gate_2"][0], 0, 8, j * P, P, 0), (w["ffn_w_up_2"][0], 0, 8, j * P, P, P)]
                groups.append(("up2", [(slot, 8)], "dve"))
            for j in range(4):
                dense("down2", w["ffn_w_down_2"][0], [(j * 256, 256)], "dve", FC)
    return groups


def build_program(nc, w, onehot, out, bias_dram):
    groups = plan(w)
    first_slot, slot_of, at = [], [], 0
    for _, slots, _ in groups:
        first_slot.append(at)
        at += len(slots)
    n_dense = at
    stage_groups = {}
    for g, (stage, _, _) in enumerate(groups):
        stage_groups.setdefault(stage, []).append(g)
    order, pair_seq, reads_at = [], {}, {}
    count = {"act": 0, "dve": 0}
    for g, (_, _, reader) in enumerate(groups):
        if reader:
            count[reader] += 1
            reads_at[g] = count[reader]
            pair_seq[g] = len(order)
            order.append(g)
    landed_at, total, size_of = {}, [0] * RAW, {}
    n = 0
    for _, slots, _ in groups:
        for parts, _ in slots:
            total[n % RAW] += 16 * len(parts)
            landed_at[n] = total[n % RAW]
            size_of[n] = 256 * max(p[1] + p[2] for p in parts)
            n += 1

    ctx = ExitStack()
    with ctx:
        def sb(name, shape, dt=F32):
            return ctx.enter_context(nc.sbuf_tensor(name, shape, dt))

        sems = {}

        def sem(name):
            if name not in sems:
                sems[name] = ctx.enter_context(nc.semaphore(name))
            return sems[name]

        raw = sb("raw", [P, RAW, SLOT])
        whi = sb("whi", [P, SPLIT, SLOT], F32R)
        wlo = sb("wlo", [P, SPLIT, SLOT], F32R)
        xT = sb("xT", [P, DC, T])
        hh = sb("hh", [P, DC, T], F32R)
        hl = sb("hl", [P, DC, T], F32R)
        oph = sb("oph", [P, 24, T], F32R)
        opl = sb("opl", [P, 24, T], F32R)
        work = sb("work", [P, DC, T])
        arena = sb("arena", [P, 5888])
        vec = sb("vec", [P, N_VEC])
        mod = sb("mod", [P, 48])
        gain = sb("gain", [P, DC])
        coef = sb("coef", [P, DC])
        tiny = sb("tiny", [P, 8, DC])
        cpair = sb("cpair", [P, DC, 2], F32R)
        cact = sb("cact", [P, DC])
        rt = sb("rt", [P, T])
        ident = sb("ident", [P, P])
        ones = sb("ones", [P, P])
        hsel = sb("hsel", [P, 162])
        spread = sb("spread", [P, 512])
        sinks = sb("sinks", [P, 8])
        consts = sb("consts", [P, 4])
        small = sb("small", [P, 2, 8])
        pair = ctx.enter_context(nc.psum_tensor("pair", [P, PAIRS, 2, 512], F32))
        misc = ctx.enter_context(nc.psum_tensor("misc", [P, 4, 512], F32))
        banks = pair[:, :, :, :].rearrange("p a b c -> p (a b) c")

        flag = sb("flag", [1, 1], I32)
        rw = sb("rw", [P, DC, NE])
        logit = sb("logit", [P, TB, NE])
        best = sb("best", [P, TB, 8])
        besti = sb("besti", [P, TB, 8], U32)
        topw = sb("topw", [P, TB, 4])
        pick = sb("pick", [P, 2, TB, NE])
        comb = sb("comb", [P, TB, NE])
        rankm = sb("rankm", [P, TB, NE + 2])

        block = ctx.enter_context(nc.Block())

        def aview(at, *shape):
            size = int(np.prod(shape))
            v = arena[:, at:at + size]
            if len(shape) == 1:
                return v
            names = "abc"[:len(shape)]
            return v.rearrange(f"p ({' '.join(names)}) -> p {' '.join(names)}",
                               **{k: s for k, s in zip(names, shape)})

        stage_rows = aview(0, NV, P)
        oh = arena[0:32, 2048:2048 + T]
        relb = arena[0:32, 2400:2400 + NHEAD]
        brow = arena[0:NHEAD, 2560:2560 + 512]
        x_tok = work[:, :, :].rearrange("p a b -> p (a b)").rearrange("p (i d) -> p i d", i=TB)
        qa, ka, qc, kc = aview(0, 4, T), aview(1024, 2, T), aview(1536, 4, T), aview(2560, 4, T)
        va, vc = aview(3584, TB, 128), aview(3840, TB, 512)
        qk = aview(0, 14, T)
        qk_sq = aview(4864, 2, 2, T)
        s_buf = [work[:, 0:2, :].rearrange("p a b -> p (a b)")[:, 0:384],
                 work[:, 2:4, :].rearrange("p a b -> p (a b)")[:, 0:384]]
        pt_buf = [work[:, 4:6, :].rearrange("p a b -> p (a b)")[:, 0:384],
                  aview(4864, 384)]
        bias_buf = [work[:, 6, :].rearrange("p (a b) -> p a b", a=2), work[:, 7, :].rearrange("p (a b) -> p a b", a=2)]
        flip = work[:, 0:2, :].rearrange("p a b -> p (a b)")[:, 384:512]
        xrp, yg = aview(0, DC, T + 3), aview(2080, DC, T)
        gw = aview(4128, 2, DC, HD)
        xc = aview(5152, 2, T)
        wmul = aview(4128, 4, T)
        tmp2 = aview(5152, 2, T)
        g_sig = aview(0, 2, 6, T)
        mrg = aview(3072, 2, 2, T)
        mrg2 = aview(4096, 2, 2, T)
        acc = aview(0, 3, 2, T)
        sg = aview(1536, 3, T)
        uf = aview(2304, 3, T)
        y8 = aview(0, DC, T)
        yap = aview(2048, 3, T + 30)
        cg = aview(2048 + 858, 3, T)
        prod = aview(2048 + 858 + 768, 3, T + 2)
        vb = aview(2048 + 858 + 768 + 774, 3, T)
        sgm = aview(5216, 2, T)
        vcb = cg
        wflat = work[:, :, :].rearrange("p a b -> p (a b)")
        vtok = wflat[:, 0:768].rearrange("p (i f) -> p i f", i=TB)
        wst = wflat[:, 768:768 + 640].rearrange("p (g j) -> p g j", g=5)
        wsl = wflat[:, 1408:1408 + 640].rearrange("p (g j) -> p g j", g=5)
        gb = aview(5216, 3, P)
        sq3 = cg
        m_tok = aview(0, TB, D)
        xk, xv = aview(1536, DC, T), aview(3584, TB, D)
        xq = work
        xp = aview(0, 2, 2, T)
        xpt = aview(1024, 2, T)

        hn_tok = aview(0, TB, D)
        place = wflat[:, 128:384].rearrange("p (i s) -> p i s", i=TB)
        place_w = wflat[:, 384:640].rearrange("p (i s) -> p i s", i=TB)
        comb_t = wflat[:, 640:1152].rearrange("p (b t) -> p b t", b=2)
        ye = aview(2048, D)
        sil, sh = aview(3072, 2, 512), aview(4096, 2, 512)
        ohf, olf = oph[:, :, :].rearrange("p a b -> p (a b)"), opl[:, :, :].rearrange("p a b -> p (a b)")
        xg_hi, xg_lo = [ohf[:, b * D:(b + 1) * D] for b in range(2)], [olf[:, b * D:(b + 1) * D] for b in range(2)]
        h_hi = [ohf[:, 2 * D + b * 512:2 * D + (b + 1) * 512] for b in range(2)]
        h_lo = [olf[:, 2 * D + b * 512:2 * D + (b + 1) * 512] for b in range(2)]
        iota = wflat[:, 0:P]
        tri = rt[:, 0:P]

        def exps(h):
            return 3 * (h + 1) if h < 8 else 24 + 2 * (h - 7)

        def gate_last(j):
            return 1 if j == 0 else 6 * j - 1

        @block.sync
        def _(sp):
            n = 0
            for _, slots, _ in groups:
                for parts, _ in slots:
                    if n >= RAW:
                        sp.wait_ge(sem("lo_ready"), n - RAW + 1)
                    dst = raw[:, n % RAW, :].rearrange("p (c m) -> p c m", m=256)
                    for src, c0, nc_, col, width, at_ in parts:
                        sp.dma_start(dst[:, c0:c0 + nc_, at_:at_ + width],
                                     src.rearrange("(c p) m -> p c m", p=P)[:, :, col:col + width])\
                          .then_inc(sem(f"landed{n % RAW}"), 16)
                    n += 1
            wg, wu, wd = (w[x][0] for x in ("moe_w_gate_2", "moe_w_up_2", "moe_w_down_2"))

            def source(e, k):
                j, r = (0, k) if k < 4 else ((k - 4) // 6 + 1, (k - 4) % 6)
                if j < JE and r < 4:
                    src = (wg, wu)[r // 2][e, (r % 2) * 512:(r % 2 + 1) * 512, j * 512:(j + 1) * 512]
                    return src.rearrange("(c p) m -> p c m", p=P), 512
                half = r - 4 if j < JE else r
                row = (j - 1) * 512 + half * 256
                return wd[e, row:row + 256, :].rearrange("(c p) m -> p c m", p=P), D

            def load(E, e, k):
                r = (n_dense + k) % RAW
                sp.wait_ge(sem("lo_ready"), E * MOE_SLOTS + (n_dense + k - RAW + 1))
                src, width = source(e, k % MOE_SLOTS)
                sp.dma_start(raw[:, r, :].rearrange("p (c m) -> p c m", m=width), src).then_inc(sem(f"landed{r}"), 16)

            def moe_pass(p):
                with sp.Fori(0, NE - 1) as e:
                    for k in range(2, MOE_SLOTS):
                        load(e + NE * p, e, k)
                    for k in (0, 1):
                        load(e + NE * p, e + 1, k + MOE_SLOTS)
                for k in range(2, MOE_SLOTS):
                    load(NE - 1 + NE * p, NE - 1, k)
                for k in (0, 1):
                    load(NE - 1 + NE * p, 0, k + MOE_SLOTS)

            load(0, 0, 0)
            load(0, 0, 1)
            moe_pass(0)
            sp.wait_ge(sem("overflow_known"), 1)
            over = sp.value_load(flag[0:1, 0:1], min_val=0, max_val=1)
            with sp.If(over > 0):
                moe_pass(1)
            sp.wait_ge(sem("out_written"), 16 * TB)

        @block.gpsimd
        def _(pool):
            pool.dma_start(x_tok, w["x"][0].rearrange("(i p) d -> p i d", p=P)).then_inc(sem("x_landed"), 16)
            st = {"chain": 0}

            def link(ins):
                st["chain"] += 1
                ins.then_inc(sem("pool_chain"), 1)
                pool.wait_ge(sem("pool_chain"), st["chain"])

            link(pool.memset(stage_rows, 0.0))
            pool.memset(brow, NEG).then_inc(sem("rows_cleared"), 1)
            pool.wait_ge(sem("rows_cleared"), 1)
            link(pool.memset(ident[:], 0.0))
            link(pool.affine_select(out=ident[:], in_=ident[:], compare_op=ALU.not_equal, fill=1.0, base=0,
                                    pattern=[[-1, P]], channel_multiplier=1))
            link(pool.memset(ones[:], 1.0))
            link(pool.memset(hsel[:], 0.0))
            link(pool.memset(hsel[0:64, 0:162:32], 1.0))
            link(pool.memset(hsel[64:128, 1:162:32], 1.0))
            link(pool.memset(consts[:, 1:2], 1e-30))
            link(pool.memset(spread[:], 1.0))
            for b in range(4):
                rows = spread[32 * b:32 * b + 32, :]
                link(pool.affine_select(out=rows, in_=rows, compare_op=ALU.is_ge, fill=0.0, base=512 * b,
                                        pattern=[[1, 512]], channel_multiplier=-64))
                link(pool.affine_select(out=rows, in_=rows, compare_op=ALU.is_ge, fill=0.0, base=63 - 512 * b,
                                        pattern=[[-1, 512]], channel_multiplier=64))
            pool.memset(consts[:, 0:1], EPS).then_inc(sem("consts_ready"), 1)
            pool.dma_start(oh, onehot).then_inc(sem("table_landed"), 16)
            pool.dma_start(relb, w["rel_bias"]).then_inc(sem("table_landed"), 16)
            pool.dma_start(sinks[:], w["sinks"].partition_broadcast(P) if False else
                           bass.AP(w["sinks"].tensor, 0, [[0, P], [1, 8]])).then_inc(sem("sinks_landed"), 16)
            for name, rows in VEC:
                r = VROW[name]
                if name in DOUBLED:
                    for half in (0, 64):
                        pool.dma_start(stage_rows[r % P:r % P + 1, r // P, half:half + 64], w[name])\
                            .then_inc(sem("vec_landed"), 16)
                    continue
                if name in PIECEWISE:
                    per = rows // 3
                    src = w[name] if len(w[name].shape) == 2 else w[name].rearrange("l k c -> (l k) c")
                    pieces = [(0, 128, 0), (128, 256, 0), (256, 320, 0)] if name == "conv_b_w_2" else \
                        [(0, 64, 64), (64, 192, 0), (192, 320, 0)]
                    for i, (a, b, o) in enumerate(pieces):
                        q = r + i * per
                        pool.dma_start(stage_rows[q % P:q % P + per, q // P, o:o + b - a], src[:, a:b])\
                            .then_inc(sem("vec_landed"), 16)
                    continue
                flat = w[name]
                dims = "abc"[:len(flat.shape) - 1]
                if len(flat.shape) == 1:
                    flat = flat.rearrange("(r p) -> r p", p=P)
                elif len(flat.shape) == 2:
                    flat = flat.rearrange("a (r p) -> (a r) p", p=P)
                else:
                    flat = flat.rearrange("a b (r p) -> (a b r) p", p=P)
                done = 0
                while done < rows:
                    q = r + done
                    k = min(rows - done, P - q % P)
                    pool.dma_start(stage_rows[q % P:q % P + k, q // P, :], flat[done:done + k, :])\
                        .then_inc(sem("vec_landed"), 16)
                    done += k
            pool.wait_ge(sem("brow_ready"), 2)
            pool.dma_start(bias_dram, brow).then_inc(sem("brow_stored"), 16)
            pool.wait_ge(sem("brow_stored"), 16)
            pool.wait_ge(sem("h_lo"), DC)
            link(pool.memset(flip, 0.0))
            pool.affine_select(out=flip, in_=flip, compare_op=ALU.not_equal, fill=1.0, base=1 - P, pattern=[[1, P]],
                               channel_multiplier=1).then_inc(sem("flip_ready"), 1)
            for h in range(NHEAD):
                if h >= 2:
                    pool.wait_ge(sem("att_scores"), h - 1)
                pool.dma_start(bias_buf[h % 2], bass.AP(bias_dram.tensor, h * 512, [[1, P], [P, 2], [1, P]]))\
                    .then_inc(sem(f"bias_landed{h % 2}"), 16)
            pool.wait_ge(sem("att_out_lo"), 8)
            pool.memset(xrp[:, :, 0:3], 0.0).then_inc(sem("xr_padded"), 1)
            for k, name in enumerate(("rnn_gate_a_w", "rnn_gate_x_w")):
                for half in range(2):
                    src = w[name][0].rearrange("(t h) c d -> h c t d", h=2)
                    pool.dma_start(gw[64 * half:64 * half + 64, k], src[half]).then_inc(sem("gate_w_landed"), 16)
            for l in range(2):
                pool.wait_ge(sem("dve_read"), reads_at[stage_groups[("down", "down2")[l]][-1]])
                link(pool.memset(yap[:, :, 0:30], 0.0))
                pool.memset(prod[:, :, 0:2], 0.0).then_inc(sem("mix_padded"), 1)
                pool.wait_ge(sem("h_lo"), DC * (NORM[f"mix{l}"] + 1))
                pool.dma_start(wsl, w["gmlp_ws_2"][l].rearrange("g i j -> i g j")).then_inc(sem("ws_landed"), 16)
                pool.wait_ge(sem("ws_landed"), 16 * (l + 1))
                pool.wait_ge(sem("mix_padded"), l + 1)
                pool.memset(wsl[0:64, :, 64:128], 0.0).then_inc(sem("ws_masked"), 1)
                pool.wait_ge(sem("mix_v_normed"), 3 * (l + 1))
                for k in range(3):
                    for half in range(2):
                        g = 2 * k - 1 + half
                        if g < 0:
                            continue
                        pool.dma_start(gb[64 * half:64 * half + 64, k, :],
                                       bass.AP(w["gmlp_b_2"].tensor, (l * 5 + g) * P, [[0, 64], [1, P]]))\
                            .then_inc(sem("gb_landed"), 16)
                pool.wait_ge(sem("dve_read"), reads_at[stage_groups[f"mixout{l}"][-1]])
                pool.dma_start(m_tok, w["mem_2"][0].rearrange("(i p) d -> p i d", p=P)).then_inc(sem("mem_landed"), 16)
            pool.dma_start(rw[:], w["moe_router_2"][0].rearrange("(c p) e -> p c e", p=P)).then_inc(sem("router_landed"), 16)
            pool.wait_ge(sem("h_lo"), DC * (NORM["ffn1"] + 1))
            pool.wait_ge(sem("ws_masked"), 2)
            pool.memset(tri, 1.0).then_inc(sem("moe_consts"), 1)
            pool.wait_ge(sem("moe_consts"), 1)
            pool.affine_select(out=tri, in_=tri, compare_op=ALU.is_gt, fill=0.0, base=0, pattern=[[1, P]],
                               channel_multiplier=-1).then_inc(sem("moe_consts"), 1)
            pool.wait_ge(sem("moe_consts"), 2)
            pool.wait_ge(sem("hn_turned"), 4)
            pool.wait_ge(sem("logits_done"), 1)
            pool.iota(iota, pattern=[[1, P]], base=0, channel_multiplier=0,
                      allow_small_or_imprecise_dtypes=True).then_inc(sem("moe_consts"), 1)

        @block.scalar
        def _(act):
            st = {"hi": 0}

            def link(ins):
                st["c"] = st.get("c", 0) + 1
                ins.then_inc(sem("act_chain"), 1)
                act.wait_ge(sem("act_chain"), st["c"])

            def ahead(n):
                while st["hi"] <= min(n, n_dense - 1):
                    s = st["hi"]
                    act.wait_ge(sem(f"landed{s % RAW}"), landed_at[s])
                    if s >= SPLIT:
                        act.wait_ge(sem("slot_used"), s - SPLIT + 1)
                    size = size_of[s]
                    act.copy(whi[:, s % SPLIT, 0:size], raw[:, s % RAW, 0:size]).then_inc(sem("hi_ready"), 1)
                    st["hi"] += 1

            def group(g):
                last = first_slot[g] + len(groups[g][1]) - 1
                ahead(last + 2)
                act.wait_ge(sem("slot_used"), last + 1)
                return pair[:, pair_seq[g] % PAIRS, :, 0:T]

            def norm(name, src, shift=None):
                k = NORM[name]
                for c in range(0, DC, 4):
                    act.activation(work[:, c:c + 4, :], src[:, c:c + 4, :], ACT.Square).then_inc(sem("sq_ready"), 1)
                act.wait_ge(sem("squares_summed"), SUMS.index(name) + 1)
                act.activation(rt[:], misc[:, 0, 0:T], ACT.Sqrt, bias=consts[:, 0:1], scale=1.0 / D)\
                    .then_inc(sem("root_ready"), 1)
                for c in range(DC):
                    act.wait_ge(sem("h_scaled"), DC * k + c + 1)
                    if shift is None:
                        act.copy(hh[:, c], work[:, c]).then_inc(sem("h_hi"), 1)
                    else:
                        act.activation(hh[:, c], work[:, c], ACT.Identity, bias=mod[:, shift + c:shift + c + 1])\
                            .then_inc(sem("h_hi"), 1)

            act.wait_ge(sem("consts_ready"), 1)
            act.wait_ge(sem("vec_ready"), NV)
            act.activation(cact[:], vec[:, 0:DC], ACT.Silu).then_inc(sem("act_start"), 1)
            act.wait_ge(sem("act_start"), 1)
            act.copy(cpair[:, :, 0], cact[:]).then_inc(sem("act_start"), 1)
            for b in range(4):
                act.wait_ge(sem("pe_start"), NV + 1 + b + 1)
                act.copy(xT[:, 2 * b:2 * b + 2, :], banks[:, b, :].rearrange("p (c t) -> p c t", c=2))\
                    .then_inc(sem("act_start"), 1)
            act.wait_ge(sem("act_start"), 6)
            act.activation(tiny[:, 0], vec[:, VROW["rnn_lambda"]:VROW["rnn_lambda"] + DC], ACT.Abs)\
                .then_inc(sem("act_start"), 1)
            act.wait_ge(sem("act_start"), 7)
            act.activation(tiny[:, 1], tiny[:, 0], ACT.Exp, scale=-1.0).then_inc(sem("act_start"), 1)
            for g in stage_groups["mod1"]:
                ahead(first_slot[g] + 2)
            norm("mix", xT, shift=0)

            tiles = [("qa", qa), ("ka", ka), ("qc", qc), ("kc", kc)]
            act.wait_ge(sem("brow_stored"), 16)
            i = 0
            for stage, dst in tiles:
                for j, g in enumerate(stage_groups[stage]):
                    ps = group(g)
                    if i >= 2:
                        act.wait_ge(sem("qk_ss"), i - 1)
                    act.activation(qk_sq[:, i % 2], ps, ACT.Square).then_inc(sem("qk_sq"), 1)
                    act.copy(dst[:, 2 * j:2 * j + 2, :], ps).then_inc(sem("act_read"), 1)
                    i += 1
            for j, g in enumerate(stage_groups["va"]):
                ps = group(g)
                act.copy(va, ps[:, :, 0:P]).then_inc(sem("act_read"), 1)
            for j, g in enumerate(stage_groups["vc"]):
                ps = group(g)
                act.copy(vc[:, :, j * 256:(j + 1) * 256], ps).then_inc(sem("act_read"), 1)

            act.wait_ge(sem("qk_ss"), 7)
            act.activation(rt[:], misc[:, 0, 0:T], ACT.Sqrt, bias=consts[:, 0:1], scale=1.0 / HD)\
                .then_inc(sem("root_ready"), 1)
            ahead(first_slot[stage_groups["xr"][0]] + 2)

            def expo(h):
                b, s = h % 2, small[:, h % 2]
                act.wait_ge(sem("att_negmax"), h + 1)
                if h >= 2:
                    act.wait_ge(sem("att_pt"), h - 1)
                act.activation(s_buf[b][:, 0:P], misc[:, b, 0:P], ACT.Exp, bias=s[:, 2:3], accum_out=s[:, 4:5])\
                    .then_inc(sem("att_exp"), 1)
                act.activation(s_buf[b][:, P:384], misc[:, b, P:384], ACT.Exp, bias=s[:, 3:4], accum_out=s[:, 5:6])\
                    .then_inc(sem("att_exp"), 1)
                if h < 8:
                    act.activation(s[:, 6:8], s[:, 2:4], ACT.Exp, bias=sinks[:, h:h + 1]).then_inc(sem("att_exp"), 1)

            def turned(h):
                act.wait_ge(sem("att_pt"), h + 1)
                if h >= 2:
                    act.wait_ge(sem("att_o"), h - 1)
                act.copy(pt_buf[h % 2], misc[:, 2, 0:384]).then_inc(sem("att_pt_sb"), 1)
                if h % 2:
                    act.wait_ge(sem("att_o"), h + 1)
                    i = h // 2
                    chunk = i if i < 4 else 8 + i
                    act.copy(oph[:, chunk], banks[:, i % 2, 0:T]).then_inc(sem("att_out_hi"), 1)

            expo(0)
            for h in range(NHEAD):
                if h + 1 < NHEAD:
                    expo(h + 1)
                turned(h)

            act.wait_ge(sem("att_out_lo"), 8)
            for j, g in enumerate(stage_groups["xr"]):
                ps = group(g)
                act.copy(xrp[:, 2 * j:2 * j + 2, 3:3 + T], ps).then_inc(sem("act_read"), 1)
            for j, g in enumerate(stage_groups["yr"]):
                ps = group(g)
                act.activation(yg[:, 2 * j:2 * j + 2, :], ps, ACT.Gelu_apprx_tanh).then_inc(sem("act_read"), 1)
            for t in range(DC):
                act.wait_ge(sem("rnn_gates"), t + 1)
                act.activation(xrp[:, t, 3:3 + T], misc[:, t % 2, 0:T], ACT.Sigmoid,
                               bias=vec[:, VROW["rnn_gate_a_b"] + t:VROW["rnn_gate_a_b"] + t + 1]).then_inc(sem("rnn_r"), 1)
                act.activation(work[:, t], misc[:, t % 2, T:2 * T], ACT.Sigmoid,
                               bias=vec[:, VROW["rnn_gate_x_b"] + t:VROW["rnn_gate_x_b"] + t + 1]).then_inc(sem("rnn_i"), 1)
            act.wait_ge(sem("coef_ready"), 1)
            act.wait_ge(sem("rnn_r"), DC)
            for half in range(2):
                if half == 0:
                    act.wait_ge(sem("rnn_ix"), DC)
                else:
                    act.wait_ge(sem("rnn_ob_lo"), 1)
                for t in range(4):
                    u = 4 * half + t
                    act.activation(wmul[:, t], xrp[:, u, 3:3 + T], ACT.Tanh, scale=coef[:, u:u + 1]).then_inc(sem("rnn_tanh"), 1)
                for t in range(4):
                    u = 4 * half + t
                    act.wait_ge(sem("rnn_tanh"), u + 1)
                    act.activation(xrp[:, u, 3:3 + T], xrp[:, u, 3:3 + T], ACT.Exp, scale=coef[:, u:u + 1])\
                        .then_inc(sem("rnn_a"), 1)
                act.wait_ge(sem("rnn_w"), 4 * (half + 1))
                act.activation(wmul, wmul, ACT.Sqrt, scale=-1.0, bias=consts[:, 1:2]).then_inc(sem("rnn_mult"), 1)
                act.wait_ge(sem("rnn_ob"), half + 1)
                act.copy(oph[:, 4 + 4 * half:8 + 4 * half, :], work[:, 4 * half:4 * half + 4, :]).then_inc(sem("rnn_ob_hi"), 1)
            for g in stage_groups["mod2"]:
                ahead(first_slot[g] + 2)
            act.wait_ge(sem("rnn_ob_lo"), 2)
            gi = iter(stage_groups["g"])
            for j in range(4):
                for b in range(3):
                    ps = group(next(gi))
                    if j >= 2:
                        act.wait_ge(sem("merged_f"), j - 1)
                    act.activation(g_sig[:, j % 2, 2 * b:2 * b + 2, :], ps, ACT.Sigmoid).then_inc(sem("act_read"), 1)
                gb_ = stage_groups["branch_b"][j]
                ahead(first_slot[gb_] + 2)
                act.wait_ge(sem("merged_f"), j + 1)
                act.copy(oph[:, 16 + 2 * j:18 + 2 * j, :], mrg[:, j % 2]).then_inc(sem("merged_hi"), 1)
            for g in stage_groups["w_out"]:
                ahead(first_slot[g] + 2)
            act.wait_ge(sem("dve_read"), reads_at[stage_groups["w_out"][-1]])
            norm("ffn", xT, shift=24)
            ups = stage_groups["up"]
            fw, fb = VROW["ffn_conv_w"], VROW["ffn_conv_b"]
            for j in range(FC + 2):
                if j < FC:
                    ps = group(ups[j])
                    if j >= 3:
                        act.wait_ge(sem("u_ready"), j - 2)
                    for m in range(2):
                        act.activation(acc[:, j % 3, m], ps[:, m], ACT.Identity,
                                       scale=vec[:, fw + 88 + 22 * m + j:fw + 89 + 22 * m + j],
                                       bias=vec[:, fb + 22 * m + j:fb + 22 * m + j + 1]).then_inc(sem("up_tap2"), 1)
                if 1 <= j <= FC:
                    act.wait_ge(sem("dve_read"), reads_at[ups[j - 1]])
                    act.activation(sg[:, (j - 1) % 3], acc[:, (j - 1) % 3, 0], ACT.Silu).then_inc(sem("up_silu"), 1)
                if j >= 2:
                    act.wait_ge(sem("u_ready"), j - 1)
                    act.copy(oph[:, j - 2], uf[:, (j - 2) % 3]).then_inc(sem("u_hi"), 1)
            for g in stage_groups["down"]:
                ahead(first_slot[g] + 4)
            for l in range(2):
                act.wait_ge(sem("dve_read"), reads_at[stage_groups[("down", "down2")[l]][-1]])
                norm(f"mix{l}", xT)
                for t, g in enumerate(stage_groups[f"mixa{l}"]):
                    ps = group(g)
                    if t == 2:
                        act.wait_ge(sem("dve_read"), reads_at[stage_groups[f"mixa{l}"][0]])
                    act.activation(sgm[:, t % 2], ps[:, 1], ACT.Sigmoid).then_inc(sem("ya_sig"), 1)
                ps = group(stage_groups[f"mix_bg{l}"][0])
                act.copy(y8[:, 3:5, :], ps).then_inc(sem("act_read"), 1)
                ps = group(stage_groups[f"mix_bgcg{l}"][0])
                act.copy(y8[0:64, 5, :], ps[0:64, 0]).then_inc(sem("mix_bg2"), 1)
                act.copy(cg[:, 2, :], ps[:, 1]).then_inc(sem("act_read"), 1)
                ps = group(stage_groups[f"mix_cg{l}"][0])
                act.copy(cg[:, 0:2, :], ps).then_inc(sem("act_read"), 1)
                ahead(first_slot[stage_groups[f"mix_bin{l}"][0]] + 2)
                ps = group(stage_groups[f"mix_binuv{l}"][0])
                act.activation(y8[64:128, 5, :], ps[64:128, 0], ACT.Gelu_apprx_tanh)
                act.activation(vb[:, 2], ps[:, 1], ACT.Gelu_apprx_tanh).then_inc(sem("mix_v2"), 1)
                ps = group(stage_groups[f"mix_u{l}"][0])
                act.activation(y8[:, 6:8, :], ps, ACT.Gelu_apprx_tanh).then_inc(sem("act_read"), 1)
                ps = group(stage_groups[f"mix_v{l}"][0])
                act.activation(vb[:, 0:2], ps, ACT.Gelu_apprx_tanh).then_inc(sem("act_read"), 1)
                ahead(first_slot[stage_groups[f"mixout{l}"][0]] + 2)
                act.wait_ge(sem("centred"), 6 * l + 3)
                act.activation(sq3, vb, ACT.Square).then_inc(sem("v_sq"), 1)
                act.wait_ge(sem("squares_summed"), SUMS.index(f"v{l}") + 1)
                act.activation(rt[:], misc[:, 1, 0:T], ACT.Sqrt, bias=consts[:, 0:1], scale=1.0 / 320).then_inc(sem("root_ready"), 1)
                for i in range(TB):
                    act.wait_ge(sem("v_turned"), 2 * l + i + 1)
                    act.copy(vtok[:, i, :], misc[:, 2 + i, 0:384]).then_inc(sem("vtok_ready"), 1)
                act.wait_ge(sem("ws_turned"), l + 1)
                act.copy(wst[:, 0:4, :], misc[:, 0, :].rearrange("p (g j) -> p g j", g=4)).then_inc(sem("wst_ready"), 1)
                act.copy(wst[:, 4, :], misc[:, 1, 0:P]).then_inc(sem("wst_ready"), 1)
                act.wait_ge(sem("centred"), 6 * l + 6)
                act.activation(sq3, y8[:, 0:3, :], ACT.Square).then_inc(sem("a_sq"), 1)
                act.wait_ge(sem("squares_summed"), SUMS.index(f"a{l}") + 1)
                act.activation(rt[:], misc[:, 1, 0:T], ACT.Sqrt, bias=consts[:, 0:1], scale=1.0 / 384).then_inc(sem("root_ready"), 1)
                la = VROW["ln_a_b_2"] + 3 * l
                for t in range(3):
                    act.wait_ge(sem("a_scaled"), 3 * l + t + 1)
                    act.activation(y8[:, t], y8[:, t], ACT.Silu, bias=vec[:, la + t:la + t + 1]).then_inc(sem("a_done"), 1)
                act.wait_ge(sem("a_done"), 3 * (l + 1))
                act.wait_ge(sem("c_done"), 3 * (l + 1))
                act.wait_ge(sem("b_done"), 3 * (l + 1))
                act.activation(work[:], y8, ACT.Square).then_inc(sem("y_sq"), 1)
                act.wait_ge(sem("squares_summed"), SUMS.index(f"y{l}") + 1)
                act.activation(rt[:], misc[:, 0, 0:T], ACT.Sqrt, bias=consts[:, 0:1], scale=1.0 / 64)\
                    .then_inc(sem("root_ready"), 1)
                for c in range(DC):
                    act.wait_ge(sem("y_scaled"), DC * l + c + 1)
                    act.copy(hh[:, c], work[:, c]).then_inc(sem("y_hi"), 1)
                for g in stage_groups[f"mixout{l}"]:
                    ahead(first_slot[g] + 2)
                act.wait_ge(sem("mem_landed"), 16 * (l + 1))
                for i in range(TB):
                    act.activation(work[:, 4 * i:4 * i + 4, :].rearrange("p a b -> p (a b)"), m_tok[:, i], ACT.Square,
                                   accum_out=tiny[:, 0, i:i + 1]).then_inc(sem("mem_sq"), 1)
                act.wait_ge(sem("mem_sq"), 2 * (l + 1))
                act.activation(tiny[:, 1, 0:2], tiny[:, 0, 0:2], ACT.Sqrt, bias=consts[:, 0:1], scale=1.0 / D)\
                    .then_inc(sem("mem_rt"), 1)
                mg = VROW["norm_mem_g_2"] + DC * l
                for c in range(DC):
                    act.wait_ge(sem("mem_turned"), 4 * l + c // 2 + 1)
                    act.activation(oph[:, c], misc[:, c // 2, (c % 2) * T:(c % 2 + 1) * T], ACT.Copy,
                                   scale=vec[:, mg + c:mg + c + 1]).then_inc(sem("mem_hi"), 1)
                for j, g in enumerate(stage_groups[f"xk{l}"]):
                    ps = group(g)
                    act.copy(xk[:, 2 * j:2 * j + 2, :], ps).then_inc(sem("act_read"), 1)
                for j, g in enumerate(stage_groups[f"xv{l}"]):
                    ps = group(g)
                    act.copy(xv[:, :, j * 256:(j + 1) * 256], ps).then_inc(sem("act_read"), 1)
                norm(f"x{l}", xT)
                act.wait_ge(sem("h_lo"), DC * (NORM[f"x{l}"] + 1))
                for j, g in enumerate(stage_groups[f"xq{l}"]):
                    ps = group(g)
                    act.copy(xq[:, 2 * j:2 * j + 2, :], ps).then_inc(sem("act_read"), 1)
                ahead(first_slot[stage_groups[f"xo{l}"][0]] + 2)
                def xexp(h):
                    b = h % 2
                    act.wait_ge(sem("x_negmax"), 4 * l + h + 1)
                    if h >= 2:
                        act.wait_ge(sem("x_pt"), 4 * l + h - 1)
                    for i in range(TB):
                        act.activation(xp[:, b, i], misc[:, b, i * T:(i + 1) * T], ACT.Exp, bias=small[:, b, 2 + i:3 + i],
                                       scale=1.0 / 16, accum_out=small[:, b, 4 + i:5 + i]).then_inc(sem("x_exp"), 1)

                xexp(0)
                for h in range(4):
                    if h + 1 < 4:
                        xexp(h + 1)
                    b = h % 2
                    act.wait_ge(sem("x_pt"), 4 * l + h + 1)
                    act.copy(xpt.rearrange("p a b -> p (a b)"), misc[:, 2, :]).then_inc(sem("x_pt_sb"), 1)
                    act.wait_ge(sem("x_o"), 4 * l + h + 1)
                    act.copy(hh[:, 2 * h:2 * h + 2, :], misc[:, 3, :].rearrange("p (a b) -> p a b", a=2)).then_inc(sem("xo_hi"), 1)
                for g in stage_groups[f"xo{l}"]:
                    ahead(first_slot[g] + 2)
                act.wait_ge(sem("dve_read"), reads_at[stage_groups[f"xo{l}"][-1]])
                norm(f"ffn{l}", xT)
                if l == 0:
                    ups2 = stage_groups["up2"]
                    for j in range(FC + 1):
                        if j < FC:
                            ps = group(ups2[j])
                            if j >= 3:
                                act.wait_ge(sem("dve_read"), reads_at[ups2[j - 3]])
                            act.activation(sg[:, j % 3], ps[:, 0], ACT.Silu).then_inc(sem("up2_silu"), 1)
                        if j >= 1:
                            act.wait_ge(sem("dve_read"), reads_at[ups2[j - 1]])
                            act.copy(oph[:, j - 1], uf[:, (j - 1) % 3]).then_inc(sem("u2_hi"), 1)
                    for g in stage_groups["down2"]:
                        ahead(first_slot[g] + 4)
            ahead(n_dense - 1)
            for q in range(4):
                act.wait_ge(sem("hn_turned"), q + 1)
                act.copy(hn_tok[:, q // 2, (q % 2) * 512:(q % 2 + 1) * 512], banks[:, q, :]).then_inc(sem("hn_tok"), 1)
            act.wait_ge(sem("top_gap"), 1)
            act.activation(topw[:, :, 1], topw[:, :, 0], ACT.Exp).then_inc(sem("top_exp"), 1)

            def moe_hi(E, k):
                r, q = (n_dense + k) % RAW, (n_dense + k) % SPLIT
                act.wait_ge(sem(f"landed{r}"), E * (16 * JE) + (total[r] + 16 * (k // RAW + 1)))
                act.wait_ge(sem("slot_used"), E * MOE_SLOTS + (n_dense + k - SPLIT + 1))
                act.copy(whi[:, q, :], raw[:, r, :]).then_inc(sem("hi_ready"), 1)

            def moe_expert(e, u, p):
                E, Q = e + NE * p, e + (NE + 1) * p
                st["k"] = 2

                def upto(k):
                    while st["k"] <= k:
                        moe_hi(E, st["k"])
                        st["k"] += 1

                def hidden_hi(j):
                    act.wait_ge(sem("m_hT"), E * JE + (j + 1))
                    act.copy(h_hi[j % 2], misc[:, 1 if j == JE - 1 else 0, :]).then_inc(sem("m_hhi"), 1)

                for j in range(JE):
                    upto(gate_last(j) + 2)
                    act.wait_ge(sem("slot_used"), E * MOE_SLOTS + (n_dense + gate_last(j) + 1))
                    act.activation(sil[:, j % 2], pair[:, j % 2, 0, :], ACT.Silu).then_inc(sem("m_sil"), 1)
                    if j >= 1:
                        hidden_hi(j - 1)
                    if j == 4:
                        act.wait_ge(sem("m_ct"), E + 1)
                        act.copy(comb_t[:, u], misc[:, 1, 0:T]).then_inc(sem("m_c"), 1)
                upto(MOE_SLOTS - 1)
                for half in range(2):
                    act.wait_ge(sem("m_x"), Q * 2 + (3 + half))
                    act.copy(xg_hi[1 - u][:, half * 512:(half + 1) * 512], misc[:, 1 - half, :]).then_inc(sem("m_xhi"), 1)
                hidden_hi(JE - 1)
                upto(MOE_SLOTS + 1)
                act.wait_ge(sem("slot_used"), E * MOE_SLOTS + (n_dense + MOE_SLOTS))
                act.copy(ye, misc[:, 2:4, :].rearrange("p a b -> p (a b)")).then_inc(sem("m_yc"), 1)

            def moe_pass(p):
                for half in range(2):
                    act.wait_ge(sem("m_x"), 2 * (NE + 1) * p + half + 1)
                    act.copy(xg_hi[0][:, half * 512:(half + 1) * 512], misc[:, 1 - half, :]).then_inc(sem("m_xhi"), 1)
                with act.Fori(0, NE // 2) as i:
                    for u in range(2):
                        moe_expert(2 * i + u, u, p)

            moe_hi(0, 0)
            moe_hi(0, 1)
            moe_pass(0)
            act.wait_ge(sem("overflow_known"), 1)
            over = act.value_load(flag[0:1, 0:1], min_val=0, max_val=1)
            with act.If(over > 0):
                moe_pass(1)
            act.wait_ge(sem("moe_added"), 1)
            for c in range(0, DC, 4):
                act.activation(work[:, c:c + 4, :], xT[:, c:c + 4, :], ACT.Square).then_inc(sem("fin_act"), 1)
            act.wait_ge(sem("fin_pe"), 1)
            act.activation(rt[:], misc[:, 0, 0:T], ACT.Sqrt, bias=consts[:, 0:1], scale=1.0 / D).then_inc(sem("fin_act"), 1)
            for i in range(TB):
                for b in range(2):
                    act.wait_ge(sem("fin_pe"), 1 + 2 * i + b + 1)
                    act.copy(hn_tok[:, i, b * 512:(b + 1) * 512], banks[:, 2 * i + b, :]).then_inc(sem("fin_act"), 1)
                act.wait_ge(sem("fin_act"), 3 + 2 * i + 2)
                act.dma_start(out[0].rearrange("(i p) d -> p i d", p=P)[:, i, :], hn_tok[:, i, :])\
                    .then_inc(sem("out_written"), 16)

        @block.tensor
        def _(pe):
            def three(out_, w_hi, w_lo, x_hi, x_lo, start, stop, weights_move=False):
                for i, (a, b) in enumerate(((w_hi, x_hi), (w_hi, x_lo), (w_lo, x_hi))):
                    lhs, rhs = (b, a) if weights_move else (a, b)
                    ins = pe.matmul(out_, lhs, rhs, start=start and i == 0, stop=stop and i == 2)
                return ins

            def free_pair(g):
                q = pair_seq[g]
                if q >= PAIRS:
                    before = order[q - PAIRS]
                    pe.wait_ge(sem(f"{groups[before][2]}_read"), reads_at[before])

            def dense_group(g, xh, xl, weights_move=False, width=256, chunk0=0, each_chunk=None):
                free_pair(g)
                q = pair_seq[g] % PAIRS
                slots = groups[g][1]
                done = 0
                for k, (_, nch) in enumerate(slots):
                    n = first_slot[g] + k
                    pe.wait_ge(sem("lo_ready"), n + 1)
                    for m in range(2):
                        for c in range(nch):
                            x = chunk0 + done + c
                            if each_chunk is not None and m == 0:
                                pe.wait_ge(*each_chunk(x))
                            wh, wl = whi[:, n % SPLIT, c * 256:(c + 1) * 256], wlo[:, n % SPLIT, c * 256:(c + 1) * 256]
                            start, stop = done + c == 0, k == len(slots) - 1 and c == nch - 1
                            if weights_move:
                                tok = slice(m * P, (m + 1) * P)
                                ins = three(pair[:, q, m, 0:width], wh[:, 0:width], wl[:, 0:width], xh[:, x, tok],
                                            xl[:, x, tok], start, stop, True)
                            else:
                                col = slice(m * P, (m + 1) * P)
                                ins = three(pair[:, q, m, 0:T], wh[:, col], wl[:, col], xh[:, x], xl[:, x], start, stop)
                    ins.then_inc(sem("slot_used"), 1)
                    done += nch

            def mod_group(g):
                n = first_slot[g]
                j = (stage_groups["mod1"] + stage_groups["mod2"]).index(g)
                pe.wait_ge(sem("lo_ready"), n + 1)
                for m in range(2):
                    col = 2 * (2 * j + m)
                    for c in range(DC):
                        for part, buf in enumerate((whi, wlo)):
                            ins = pe.matmul(misc[:, 3, col:col + 2], buf[:, n % SPLIT, c * 256 + m * P:c * 256 + (m + 1) * P],
                                            cpair[:, c, :], start=(c == 0 and part == 0), stop=(c == DC - 1 and part == 1))
                ins.then_inc(sem("slot_used"), 1)

            def norm(k):
                for c in range(DC):
                    if c % 4 == 0:
                        pe.wait_ge(sem("sq_ready"), 2 * k + c // 4 + 1)
                    ins = pe.matmul(misc[:, 0, 0:T], ones[:], work[:, c], start=(c == 0), stop=(c == DC - 1))
                ins.then_inc(sem("squares_summed"), 1)

            def h_chunk(k):
                return lambda c: (sem("h_lo"), DC * k + c + 1)

            pe.wait_ge(sem("consts_ready"), 1)
            pe.wait_ge(sem("vec_landed"), 16 * N_VEC_DMAS)
            for v in range(NV):
                pe.transpose(misc[:, v // 4, (v % 4) * P:(v % 4 + 1) * P], stage_rows[:, v, :], ident[:])\
                    .then_inc(sem("pe_start"), 1)
            pe.wait_ge(sem("table_landed"), 32)
            pe.matmul(misc[0:NHEAD, 2, 0:T], relb, oh, start=True, stop=True).then_inc(sem("pe_start"), 1)
            pe.wait_ge(sem("x_landed"), 16)
            for c in range(DC):
                for i in range(TB):
                    ins = pe.transpose(banks[:, c // 2, (c % 2) * T + i * P:(c % 2) * T + (i + 1) * P],
                                       x_tok[:, i, c * P:(c + 1) * P], ident[:])
                if c % 2:
                    ins.then_inc(sem("pe_start"), 1)
            pe.wait_ge(sem("c_lo"), 1)
            for g in stage_groups["mod1"]:
                mod_group(g)
            norm(0)
            qk_groups = stage_groups["qa"] + stage_groups["ka"] + stage_groups["qc"] + stage_groups["kc"]

            def qk_squares(i):
                pe.wait_ge(sem("qk_sq"), i + 1)
                for m in range(2):
                    t = 2 * i + m
                    ins = pe.matmul(misc[:, 0, 0:T], hsel[:, 32 - 2 * t:160 - 2 * t], qk_sq[:, i % 2, m],
                                    start=(t == 0), stop=(t == 13))
                ins.then_inc(sem("qk_ss"), 1)

            for i, g in enumerate(qk_groups):
                dense_group(g, hh, hl, each_chunk=h_chunk(0) if i == 0 else None)
                if i >= 1:
                    qk_squares(i - 1)
            dense_group(stage_groups["va"][0], hh, hl, weights_move=True, width=P)
            qk_squares(6)
            for g in stage_groups["vc"]:
                dense_group(g, hh, hl, weights_move=True)
            pe.wait_ge(sem("qk_rs"), 1)
            for t in range(14):
                if t % 2 == 0 and t >= 8:
                    pe.wait_ge(sem("qk_normed"), t - 6)
                rows = slice(32 * (t // 4), 32 * (t // 4) + 32)
                ins = pe.matmul(misc[:, (t // 2) % 4, (t % 2) * T:(t % 2 + 1) * T], spread[rows, (t % 4) * P:(t % 4 + 1) * P],
                                rt[rows, :], start=True, stop=True)
                if t % 2:
                    ins.then_inc(sem("qk_spread"), 1)

            def operands(h):
                half = slice(64 * (h % 2), 64 * (h % 2) + 64)
                if h < 8:
                    return qa[half, h // 2], ka[half, h // 4], va[:, :, 64 * (h // 4):64 * (h // 4) + 64]
                h -= 8
                return qc[half, h // 2], kc[half, h // 2], vc[:, :, 64 * h:64 * h + 64]

            def scores(h):
                q, k, _ = operands(h)
                if h >= 2:
                    pe.wait_ge(sem("att_exp"), exps(h - 2))
                pe.wait_ge(sem(f"bias_landed{h % 2}"), 16 * (h // 2 + 1))
                for i, (qb, kb) in enumerate(((0, 0), (1, 0), (1, 1))):
                    s = misc[:, h % 2, i * P:(i + 1) * P]
                    pe.matmul(s, q[:, qb * P:(qb + 1) * P], k[:, kb * P:(kb + 1) * P], start=True, stop=False)
                    ins = pe.matmul(s, flip, bias_buf[h % 2][:, 1 - (qb - kb), :], start=False, stop=True)
                ins.then_inc(sem("att_scores"), 1)

            pe.wait_ge(sem("qk_normed"), 14)
            pe.wait_ge(sem("flip_ready"), 1)
            pe.wait_ge(sem("act_read"), reads_at[stage_groups["vc"][1]])
            scores(0)
            scores(1)
            for h in range(NHEAD):
                pe.wait_ge(sem("att_p"), 2 * (h + 1))
                if h >= 1:
                    pe.wait_ge(sem("att_pt_sb"), h)
                for i in range(3):
                    ins = pe.transpose(misc[:, 2, i * P:(i + 1) * P], s_buf[h % 2][:, i * P:(i + 1) * P], ident[:])
                ins.then_inc(sem("att_pt"), 1)
                if h + 2 < NHEAD:
                    scores(h + 2)
                pe.wait_ge(sem("att_pt_sb"), h + 1)
                i = h // 2
                if h % 2 == 0 and i >= 2:
                    pe.wait_ge(sem("att_out_lo"), i - 1)
                _, _, v = operands(h)
                half = slice(64 * (h % 2), 64 * (h % 2) + 64)
                pe.matmul(banks[half, i % 2, 0:T], v[:, 0], pt_buf[h % 2][:, 0:T], start=True, stop=False)
                pe.matmul(banks[half, i % 2, P:T], v[:, 1], pt_buf[h % 2][:, T:384], start=False, stop=True)\
                    .then_inc(sem("att_o"), 1)

            pe.wait_ge(sem("att_out_lo"), 8)
            for g in stage_groups["xr"] + stage_groups["yr"]:
                dense_group(g, hh, hl)
            pe.wait_ge(sem("gate_w_landed"), 64)
            for t in range(DC):
                pe.wait_ge(sem("rnn_xc"), t + 1)
                if t >= 2:
                    pe.wait_ge(sem("rnn_i"), t - 1)
                for k in range(2):
                    for half in range(2):
                        p = slice(64 * half, 64 * half + 64)
                        ins = pe.matmul(misc[p, t % 2, k * T:(k + 1) * T], gw[p, k, t, :], xc[p, t % 2], start=True, stop=True)
                ins.then_inc(sem("rnn_gates"), 1)
            for g in stage_groups["mod2"]:
                mod_group(g)
            pe.wait_ge(sem("rnn_ob_lo"), 2)
            gi = iter(stage_groups["g"])
            for j in range(4):
                for b in range(3):
                    dense_group(next(gi), hh, hl)
                g = stage_groups["branch_ac"][j]
                free_pair(g)
                n, q = first_slot[g], pair_seq[g] % PAIRS
                pe.wait_ge(sem("lo_ready"), n + 1)
                for m in range(2):
                    for c in range(DC):
                        x, at = (c, 0) if c < 4 else (8 + c, T)
                        col = slice(c * 256 + m * P, c * 256 + (m + 1) * P)
                        ins = three(pair[:, q, m, at:at + T], whi[:, n % SPLIT, col], wlo[:, n % SPLIT, col],
                                    oph[:, x], opl[:, x], c % 4 == 0, c % 4 == 3)
                ins.then_inc(sem("slot_used"), 1)
                dense_group(stage_groups["branch_b"][j], oph, opl, chunk0=4)
            for i, g in enumerate(stage_groups["w_out"]):
                if i == 0:
                    pe.wait_ge(sem("merged_lo"), 4)
                dense_group(g, oph, opl, chunk0=16)
            norm(1)
            for i, g in enumerate(stage_groups["up"]):
                dense_group(g, hh, hl, each_chunk=h_chunk(1) if i == 0 else None)
            for i, g in enumerate(stage_groups["down"]):
                dense_group(g, oph, opl, each_chunk=(lambda c: (sem("u_lo"), c + 1)) if i == 0 else None)

            for l in range(2):
                k0 = NORM[f"mix{l}"]
                norm(k0)
                first = True
                for stage in ("mixa", "mix_bg", "mix_bgcg", "mix_cg", "mix_bin", "mix_binuv", "mix_u", "mix_v"):
                    for g in stage_groups[f"{stage}{l}"]:
                        dense_group(g, hh, hl, each_chunk=h_chunk(k0) if first else None)
                        first = False
                pe.wait_ge(sem("act_read"), reads_at[stage_groups[f"mix_v{l}"][0]])

                def over_v(src, bank, name):
                    pe.matmul(misc[:, bank, 0:T], ones[64:128, :], src[64:128, 0], start=True, stop=False)
                    pe.matmul(misc[:, bank, 0:T], ones[:], src[:, 1], start=False, stop=False)
                    pe.matmul(misc[:, bank, 0:T], ones[:], src[:, 2], start=False, stop=True).then_inc(sem(name), 1)

                over_v(vb, 0, "means_summed")
                pe.wait_ge(sem("v_sq"), l + 1)
                over_v(sq3, 1, "squares_summed")
                pe.wait_ge(sem("mix_v_normed"), 3 * (l + 1))
                for i in range(TB):
                    for t in range(3):
                        ins = pe.transpose(misc[:, 2 + i, t * P:(t + 1) * P], vb[:, t, i * P:(i + 1) * P], ident[:])
                    ins.then_inc(sem("v_turned"), 1)
                pe.wait_ge(sem("ws_masked"), l + 1)
                for g in range(5):
                    dst = misc[:, 0, g * P:(g + 1) * P] if g < 4 else misc[:, 1, 0:P]
                    ins = pe.transpose(dst, wsl[:, g, :], ident[:])
                ins.then_inc(sem("ws_turned"), 1)
                pe.wait_ge(sem("wst_ready"), 2 * (l + 1))
                pe.wait_ge(sem("vtok_ready"), 2 * (l + 1))
                for g in range(5):
                    k, p = (g + 1) // 2, 64 * ((g + 1) % 2)
                    for i in range(TB):
                        at = (k % 2) * T + i * P
                        ins = pe.matmul(misc[p:p + 64, 2 + k // 2, at:at + P], vtok[:, i, 64 + 64 * g:128 + 64 * g],
                                        wst[:, g, :], start=True, stop=True)
                ins.then_inc(sem("c_mixed"), 1)
                pe.wait_ge(sem("conv_taps"), 93 * (l + 1))
                for t in range(3):
                    ins = pe.matmul(misc[:, 0, 0:T], ones[:], y8[:, t], start=(t == 0), stop=(t == 2))
                ins.then_inc(sem("means_summed"), 1)
                pe.wait_ge(sem("a_sq"), l + 1)
                for t in range(3):
                    ins = pe.matmul(misc[:, 1, 0:T], ones[:], sq3[:, t], start=(t == 0), stop=(t == 2))
                ins.then_inc(sem("squares_summed"), 1)
                pe.wait_ge(sem("y_sq"), l + 1)
                for c in range(DC):
                    ins = pe.matmul(misc[:, 0, 0:T], hsel[:, 32 - 2 * c:160 - 2 * c], work[:, c],
                                    start=(c == 0), stop=(c == DC - 1))
                ins.then_inc(sem("squares_summed"), 1)
                pe.wait_ge(sem("y_rs"), l + 1)
                for c in range(DC):
                    rows = slice(32 * (c // 4), 32 * (c // 4) + 32)
                    ins = pe.matmul(misc[:, c // 2, (c % 2) * T:(c % 2 + 1) * T], spread[rows, (c % 4) * P:(c % 4 + 1) * P],
                                    rt[rows, :], start=True, stop=True)
                    if c % 2:
                        ins.then_inc(sem("y_spread"), 1)
                for i, g in enumerate(stage_groups[f"mixout{l}"]):
                    dense_group(g, hh, hl, each_chunk=(lambda c: (sem("y_lo"), DC * l + c + 1)) if i == 0 else None)
                pe.wait_ge(sem("mem_scaled"), 2 * (l + 1))
                for c in range(DC):
                    for i in range(TB):
                        ins = pe.transpose(misc[:, c // 2, (c % 2) * T + i * P:(c % 2) * T + (i + 1) * P],
                                           m_tok[:, i, c * P:(c + 1) * P], ident[:])
                    if c % 2:
                        ins.then_inc(sem("mem_turned"), 1)
                for i, g in enumerate(stage_groups[f"xk{l}"]):
                    dense_group(g, oph, opl, each_chunk=(lambda c: (sem("mem_lo"), DC * l + c + 1)) if i == 0 else None)
                for g in stage_groups[f"xv{l}"]:
                    dense_group(g, oph, opl, weights_move=True)
                k1 = NORM[f"x{l}"]
                norm(k1)
                for i, g in enumerate(stage_groups[f"xq{l}"]):
                    dense_group(g, hh, hl, each_chunk=h_chunk(k1) if i == 0 else None)

                def x_scores(h):
                    if h >= 2:
                        pe.wait_ge(sem("x_exp"), 2 * (4 * l + h - 1))
                    for i in range(TB):
                        for c in range(2):
                            ins = pe.matmul(misc[:, h % 2, i * T:(i + 1) * T], xq[:, 2 * h + c, i * P:(i + 1) * P],
                                            xk[:, 2 * h + c, :], start=(c == 0), stop=(c == 1))
                    ins.then_inc(sem("x_scores"), 1)

                pe.wait_ge(sem("act_read"), reads_at[stage_groups[f"xq{l}"][-1]])
                x_scores(0)
                x_scores(1)
                for h in range(4):
                    b = h % 2
                    pe.wait_ge(sem("x_p"), 2 * (4 * l + h + 1))
                    if h >= 1:
                        pe.wait_ge(sem("x_pt_sb"), 4 * l + h)
                    for mc in range(2):
                        for i in range(TB):
                            at = mc * T + i * P
                            ins = pe.transpose(misc[:, 2, at:at + P], xp[:, b, i, mc * P:(mc + 1) * P], ident[:])
                    ins.then_inc(sem("x_pt"), 1)
                    if h + 2 < 4:
                        x_scores(h + 2)
                    pe.wait_ge(sem("x_pt_sb"), 4 * l + h + 1)
                    if h >= 1:
                        pe.wait_ge(sem("xo_lo"), 4 * l + h)
                    for dt in range(2):
                        for mc in range(2):
                            ins = pe.matmul(misc[:, 3, dt * T:(dt + 1) * T], xv[:, mc, h * T + dt * P:h * T + (dt + 1) * P],
                                            xpt[:, mc, :], start=(mc == 0), stop=(mc == 1))
                    ins.then_inc(sem("x_o"), 1)
                for i, g in enumerate(stage_groups[f"xo{l}"]):
                    dense_group(g, hh, hl, each_chunk=(lambda c: (sem("xo_lo"), 4 * l + c // 2 + 1)) if i == 0 else None)
                norm(NORM[f"ffn{l}"])
                if l == 0:
                    for i, g in enumerate(stage_groups["up2"]):
                        dense_group(g, hh, hl, each_chunk=h_chunk(NORM["ffn0"]) if i == 0 else None)
                    for i, g in enumerate(stage_groups["down2"]):
                        dense_group(g, oph, opl, each_chunk=(lambda c: (sem("u2_lo"), c + 1)) if i == 0 else None)

            pe.wait_ge(sem("h_lo"), DC * (NORM["ffn1"] + 1))
            for i in range(TB):
                for c in range(DC):
                    ins = pe.transpose(banks[:, 2 * i + c // 4, (c % 4) * P:(c % 4 + 1) * P], work[:, c, i * P:(i + 1) * P], ident[:])
                    if c % 4 == 3:
                        ins.then_inc(sem("hn_turned"), 1)
            pe.wait_ge(sem("router_landed"), 16)
            for i in range(TB):
                for c in range(DC):
                    ins = pe.matmul(misc[:, 1, i * NE:(i + 1) * NE], work[:, c, i * P:(i + 1) * P], rw[:, c, :],
                                    start=(c == 0), stop=(c == DC - 1))
            ins.then_inc(sem("logits_done"), 1)
            pe.wait_ge(sem("picked"), 1)
            pe.wait_ge(sem("moe_consts"), 2)
            sel = pick[:, 0]
            pe.matmul(misc[:, 0, 0:NE], tri, sel[:, 0], start=True, stop=True)
            pe.matmul(misc[:, 0, NE:2 * NE], tri, sel[:, 1], start=True, stop=False)
            pe.matmul(misc[:, 0, NE:2 * NE], ones[:], sel[:, 0], start=False, stop=True)
            pe.matmul(misc[:, 0, 16:16 + NE], ones[:], sel[:, 0], start=True, stop=False)
            pe.matmul(misc[:, 0, 16:16 + NE], ones[:], sel[:, 1], start=False, stop=True).then_inc(sem("ranked"), 1)
            pe.wait_ge(sem("hn_tok"), 4)

            def gather(Q):
                pe.wait_ge(sem("m_gt"), Q + 1)
                for half in range(2):
                    for c in range(4):
                        f = (4 * half + c) * P
                        for i in range(TB):
                            ins = pe.matmul(misc[:, 1 - half, c * P:(c + 1) * P], hn_tok[:, i, f:f + P], place[:, i, :],
                                            start=(i == 0), stop=(i == 1))
                    ins.then_inc(sem("m_x"), 1)

            def scatter(S, cb, E):
                pe.wait_ge(sem("m_yc"), E)
                pe.wait_ge(sem("m_c"), E)
                for r in range(4):
                    for m in range(2):
                        f = (2 * r + m) * P
                        ins = pe.matmul(banks[:, r, m * T:(m + 1) * T], ye[:, f:f + P], comb_t[:, cb], start=True, stop=True)
                    ins.then_inc(sem("m_s"), 1)

            def moe_expert(e, u, p):
                E, Q = e + NE * p, e + (NE + 1) * p

                def gate_or_up(j, kind):
                    for half in range(2):
                        k = (0 if j == 0 else 6 * j - 2) + 2 * kind + half
                        q = (n_dense + k) % SPLIT
                        pe.wait_ge(sem("lo_ready"), E * MOE_SLOTS + (n_dense + k + 1))
                        for c in range(4):
                            x = slice((4 * half + c) * P, (4 * half + c + 1) * P)
                            col = slice(c * 512, (c + 1) * 512)
                            ins = three(pair[:, j % 2, kind, :], whi[:, q, col], wlo[:, q, col], xg_hi[u][:, x], xg_lo[u][:, x],
                                        half == 0 and c == 0, half == 1 and c == 3, True)
                        ins.then_inc(sem("slot_used"), 1)

                def turn(j):
                    pe.wait_ge(sem("m_mul"), E * JE + (j + 3))
                    bank = 1 if j == JE - 1 else 0
                    if j == JE - 1:
                        pe.wait_ge(sem("m_xlo"), Q * 2 + 3)
                    for c in range(4):
                        ins = pe.transpose(misc[:, bank, c * P:(c + 1) * P], sh[:, j % 2, c * P:(c + 1) * P], ident[:])
                    ins.then_inc(sem("m_hT"), 1)

                def down(j):
                    pe.wait_ge(sem("m_hlo"), E * JE + (j + 1))
                    if j == 0:
                        pe.wait_ge(sem("m_yc"), E + 1)
                    for half in range(2):
                        k = (6 * j + 8 if j < JE - 1 else 6 * j + 4) + half
                        q = (n_dense + k) % SPLIT
                        pe.wait_ge(sem("lo_ready"), E * MOE_SLOTS + (n_dense + k + 1))
                        for c in range(2):
                            x = slice((2 * half + c) * P, (2 * half + c + 1) * P)
                            for m in range(2):
                                col = slice(c * D + m * 512, c * D + (m + 1) * 512)
                                ins = three(misc[:, 2 + m, :], whi[:, q, col], wlo[:, q, col], h_hi[j % 2][:, x], h_lo[j % 2][:, x],
                                            j == 0 and half == 0 and c == 0, j == JE - 1 and half == 1 and c == 1, True)
                        ins.then_inc(sem("slot_used"), 1)

                for j in range(JE):
                    if j == 0:
                        pe.wait_ge(sem("m_xlo"), Q * 2 + 2)
                        pe.wait_ge(sem("m_added"), Q * 4 + 4)
                        pe.wait_ge(sem("m_mul"), E * JE + 2)
                    elif j == 1:
                        pe.wait_ge(sem("m_mul"), E * JE + 1)
                    else:
                        pe.wait_ge(sem("m_mul"), E * JE + (j + 1))
                    gate_or_up(j, 0)
                    if j >= 1:
                        turn(j - 1)
                    gate_or_up(j, 1)
                    if j >= 1:
                        down(j - 1)
                    if j == 3:
                        pe.wait_ge(sem("m_gw"), E + 1)
                        for i in range(TB):
                            ins = pe.transpose(misc[:, 1, i * P:(i + 1) * P], place_w[:, i, :], ident[:])
                        ins.then_inc(sem("m_ct"), 1)
                pe.wait_ge(sem("m_c"), E + 2)
                pe.wait_ge(sem("m_hlo"), E * JE + (JE - 1))
                gather(Q + 1)
                turn(JE - 1)
                scatter(Q, 1 - u, E + 1)
                down(JE - 1)

            def moe_pass(p):
                gather((NE + 1) * p)
                with pe.Fori(0, NE // 2) as i:
                    for u in range(2):
                        moe_expert(2 * i + u, u, p)
                pe.wait_ge(sem("m_mul"), NE * (p + 1) * JE + 2)
                pe.wait_ge(sem("m_added"), 4 * ((NE + 1) * p + NE) + 4)
                scatter(0, 1, NE * (p + 1) + 1)

            moe_pass(0)
            pe.wait_ge(sem("overflow_known"), 1)
            over = pe.value_load(flag[0:1, 0:1], min_val=0, max_val=1)
            with pe.If(over > 0):
                pe.wait_ge(sem("m_added"), 4 * (NE + 1) + 4)
                moe_pass(1)
            for c in range(DC):
                if c % 4 == 0:
                    pe.wait_ge(sem("fin_act"), c // 4 + 1)
                ins = pe.matmul(misc[:, 0, 0:T], ones[:], work[:, c], start=(c == 0), stop=(c == DC - 1))
            ins.then_inc(sem("fin_pe"), 1)
            for i in range(TB):
                for c in range(DC):
                    pe.wait_ge(sem("fin_scaled"), c + 1)
                    ins = pe.transpose(banks[:, 2 * i + c // 4, (c % 4) * P:(c % 4 + 1) * P], work[:, c, i * P:(i + 1) * P], ident[:])
                    if c % 4 == 3:
                        ins.then_inc(sem("fin_pe"), 1)

        @block.vector
        def _(dve):
            st = {"lo": 0, "chain": 0}

            def link(ins):
                st["chain"] += 1
                ins.then_inc(sem("dve_chain"), 1)
                dve.wait_ge(sem("dve_chain"), st["chain"])

            def ahead(n):
                while st["lo"] <= min(n, n_dense - 1):
                    s = st["lo"]
                    dve.wait_ge(sem("hi_ready"), s + 1)
                    size = size_of[s]
                    dve.tensor_tensor(wlo[:, s % SPLIT, 0:size], raw[:, s % RAW, 0:size],
                                      whi[:, s % SPLIT, 0:size].bitcast(F32), ALU.subtract).then_inc(sem("lo_ready"), 1)
                    st["lo"] += 1

            def group(g):
                last = first_slot[g] + len(groups[g][1]) - 1
                ahead(last + 2)
                dve.wait_ge(sem("slot_used"), last + 1)
                return pair[:, pair_seq[g] % PAIRS, :, 0:T]

            def col(name, i):
                return vec[:, VROW[name] + i:VROW[name] + i + 1]

            def low(dst, src, hi, name):
                dve.tensor_tensor(dst, src, hi.bitcast(F32), ALU.subtract).then_inc(sem(name), 1)

            def norm(name, src, gains, shift=None):
                k = NORM[name]
                dve.wait_ge(sem("root_ready"), ROOTS.index(name) + 1)
                link(dve.reciprocal(rt[:], rt[:]))
                for c in range(DC):
                    dve.scalar_tensor_tensor(work[:, c], src[:, c], gains(c), rt[:], ALU.mult, ALU.mult)\
                        .then_inc(sem("h_scaled"), 1)
                for c in range(DC):
                    dve.wait_ge(sem("h_hi"), DC * k + c + 1)
                    if shift is None:
                        low(hl[:, c], work[:, c], hh[:, c], "h_lo")
                    else:
                        dve.scalar_tensor_tensor(hl[:, c], work[:, c], mod[:, shift + c:shift + c + 1],
                                                 hh[:, c].bitcast(F32), ALU.add, ALU.subtract).then_inc(sem("h_lo"), 1)

            def add_modulated(g, j, gate):
                ps = group(g)
                for m in range(2):
                    t = 2 * j + m
                    ins = dve.scalar_tensor_tensor(xT[:, t], ps[:, m], mod[:, gate + t:gate + t + 1], xT[:, t], ALU.mult, ALU.add)
                    ins.then_inc(sem("dve_read" if m else "res_half"), 1)

            for v in range(NV):
                dve.wait_ge(sem("pe_start"), NV)
                k = min(P, N_VEC - v * P)
                dve.tensor_copy(vec[:, v * P:v * P + k], misc[:, v // 4, (v % 4) * P:(v % 4) * P + k])\
                    .then_inc(sem("vec_ready"), 1)
            dve.wait_ge(sem("vec_ready"), NV)
            for name in ("qnorm_a", "qnorm_c"):
                link(dve.tensor_scalar(col(name, 0), col(name, 0), HD ** -0.5, None, ALU.mult))
            dve.wait_ge(sem("act_start"), 2)
            dve.tensor_tensor(cpair[:, :, 1], cact[:], cpair[:, :, 0].bitcast(F32), ALU.subtract).then_inc(sem("c_lo"), 1)
            dve.wait_ge(sem("pe_start"), NV + 1)
            dve.wait_ge(sem("consts_ready"), 1)
            link(dve.tensor_copy(brow[:, 0:T], misc[0:NHEAD, 2, 0:T]))
            dve.memset(brow[0:8, 0:WIN], NEG).then_inc(sem("brow_ready"), 2)
            dve.wait_ge(sem("act_start"), 8)
            link(dve.tensor_scalar(tiny[:, 2], tiny[:, 1], 2.0, None, ALU.add))
            link(dve.reciprocal(tiny[:, 3], tiny[:, 2]))
            link(dve.tensor_tensor(tiny[:, 4], tiny[:, 1], tiny[:, 3], ALU.mult))
            link(dve.tensor_tensor(tiny[:, 5], tiny[:, 4], tiny[:, 4], ALU.mult))
            link(dve.tensor_scalar(tiny[:, 6], tiny[:, 5], 1.0 / 19, 1.0 / 17, ALU.mult, ALU.add))
            for d in (15, 13, 11, 9, 7, 5, 3, 1):
                link(dve.tensor_tensor(tiny[:, 7], tiny[:, 6], tiny[:, 5], ALU.mult))
                link(dve.tensor_scalar(tiny[:, 6], tiny[:, 7], 1.0 / d, None, ALU.add))
            link(dve.tensor_tensor(tiny[:, 7], tiny[:, 6], tiny[:, 4], ALU.mult))
            lam = vec[:, VROW["rnn_lambda"]:VROW["rnn_lambda"] + DC]
            link(dve.tensor_scalar(tiny[:, 2], lam, -1.0, 0.0, ALU.mult, ALU.max))
            link(dve.scalar_tensor_tensor(tiny[:, 3], tiny[:, 7], 2.0, tiny[:, 2], ALU.mult, ALU.add))
            dve.tensor_scalar(coef[:], tiny[:, 3], -8.0, None, ALU.mult).then_inc(sem("coef_ready"), 1)
            bm = VROW["b_mod"]

            def modulation(gs, j0):
                for i, g in enumerate(gs):
                    ahead(first_slot[g] + 2)
                n = first_slot[gs[-1]]
                dve.wait_ge(sem("slot_used"), n + 1)
                a, b = 2 * j0, 2 * (j0 + len(gs))
                ps = misc[:, 3, 2 * a:2 * b].rearrange("p (t two) -> p t two", two=2)
                link(dve.tensor_tensor(mod[:, a:b], vec[:, bm + a:bm + b], ps[:, :, 0], ALU.add))
                link(dve.tensor_tensor(mod[:, a:b], mod[:, a:b], ps[:, :, 1], ALU.add))

            modulation(stage_groups["mod1"], 0)
            nm = VROW["norm_mix"]
            link(dve.scalar_tensor_tensor(gain[:], mod[:, 8:16], 1.0, vec[:, nm:nm + DC], ALU.add, ALU.mult))
            norm("mix", xT, lambda c: gain[:, c:c + 1], shift=0)
            for stage in ("qa", "ka", "qc", "kc", "va", "vc"):
                for g in stage_groups[stage]:
                    ahead(first_slot[g] + 2)
            dve.wait_ge(sem("root_ready"), ROOTS.index("qk") + 1)
            dve.reciprocal(rt[:], rt[:]).then_inc(sem("qk_rs"), 1)
            names = ["qnorm_a"] * 4 + ["knorm_a"] * 2 + ["qnorm_c"] * 4 + ["knorm_c"] * 4
            dve.wait_ge(sem("act_read"), reads_at[stage_groups["kc"][-1]])
            for t in range(14):
                dve.wait_ge(sem("qk_spread"), t // 2 + 1)
                dve.scalar_tensor_tensor(qk[:, t], qk[:, t], col(names[t], 0), misc[:, (t // 2) % 4, (t % 2) * T:(t % 2 + 1) * T],
                                         ALU.mult, ALU.mult).then_inc(sem("qk_normed"), 1)

            def peak(h):
                b, s = h % 2, small[:, h % 2]
                dve.wait_ge(sem("att_scores"), h + 1)
                if h >= 2:
                    dve.wait_ge(sem("att_p"), 2 * (h - 1))
                dve.tensor_reduce(s[:, 0:1], misc[:, b, 0:P], AX_X, ALU.max).then_inc(sem("att_max"), 1)
                dve.tensor_reduce(s[:, 1:2], misc[:, b, P:384], AX_X, ALU.max).then_inc(sem("att_max"), 1)
                dve.wait_ge(sem("att_max"), 2 * h + 2)
                if h < 8:
                    dve.tensor_scalar(s[:, 2:4], s[:, 0:2], sinks[:, h:h + 1], -1.0, ALU.max, ALU.mult).then_inc(sem("att_negmax"), 1)
                else:
                    dve.tensor_scalar(s[:, 2:4], s[:, 0:2], -1.0, None, ALU.mult).then_inc(sem("att_negmax"), 1)

            def normalised(h):
                b, s = h % 2, small[:, h % 2]
                dve.wait_ge(sem("att_exp"), exps(h))
                if h < 8:
                    link(dve.tensor_tensor(s[:, 4:6], s[:, 4:6], s[:, 6:8], ALU.add))
                link(dve.reciprocal(s[:, 6:8], s[:, 4:6]))
                dve.tensor_scalar(s_buf[b][:, 0:P], s_buf[b][:, 0:P], s[:, 6:7], None, ALU.mult).then_inc(sem("att_p"), 1)
                dve.tensor_scalar(s_buf[b][:, P:384], s_buf[b][:, P:384], s[:, 7:8], None, ALU.mult).then_inc(sem("att_p"), 1)
                if h % 2 == 0 and h >= 2:
                    out_low(h // 2 - 1)

            def out_low(i):
                chunk = i if i < 4 else 8 + i
                dve.wait_ge(sem("att_out_hi"), i + 1)
                low(opl[:, chunk], banks[:, i % 2, 0:T], oph[:, chunk], "att_out_lo")

            ahead(first_slot[stage_groups["xr"][0]] + 2)
            dve.wait_ge(sem("sinks_landed"), 16)
            peak(0)
            for h in range(NHEAD):
                if h + 1 < NHEAD:
                    peak(h + 1)
                normalised(h)
            out_low(7)
            for stage in ("xr", "yr"):
                for g in stage_groups[stage]:
                    ahead(first_slot[g] + 2)
            dve.wait_ge(sem("act_read"), reads_at[stage_groups["yr"][-1]])
            dve.wait_ge(sem("xr_padded"), 1)

            def gated(t):
                dve.wait_ge(sem("rnn_i"), t + 1)
                dve.tensor_tensor(work[:, t], work[:, t], xc[:, t % 2], ALU.mult).then_inc(sem("rnn_ix"), 1)

            for t in range(DC):
                x = xrp[:, t]
                if t >= 2:
                    gated(t - 2)
                    dve.wait_ge(sem("rnn_ix"), t - 1)
                link(dve.tensor_scalar(xc[:, t % 2], x[:, 0:T], col("rnn_conv_w", t), col("rnn_conv_b", t), ALU.mult, ALU.add))
                for k in (1, 2, 3):
                    ins = dve.scalar_tensor_tensor(xc[:, t % 2], x[:, k:k + T], col("rnn_conv_w", DC * k + t), xc[:, t % 2],
                                                   ALU.mult, ALU.add)
                    if k < 3:
                        link(ins)
                ins.then_inc(sem("rnn_xc"), 1)
            gated(DC - 2)
            gated(DC - 1)
            for half in range(2):
                q = slice(4 * half, 4 * half + 4)
                a = xrp[:, q, 3:3 + T]
                for g in stage_groups["mod2"][4 * half:4 * half + 4]:
                    pass
                for t in range(4):
                    u = 4 * half + t
                    dve.wait_ge(sem("rnn_a"), u + 1)
                    link(dve.tensor_tensor(tmp2[:, t % 2], xrp[:, u, 3:3 + T], xrp[:, u, 3:3 + T], ALU.mult))
                    dve.scalar_tensor_tensor(wmul[:, t], tmp2[:, t % 2], 1.0, wmul[:, t], ALU.add, ALU.mult)\
                        .then_inc(sem("rnn_w"), 1)
                dve.wait_ge(sem("rnn_mult"), half + 1)
                link(dve.memset(wmul[:, :, 0:1], 1.0))
                link(dve.tensor_tensor(work[:, q, :], work[:, q, :], wmul, ALU.mult))
                for t in range(4):
                    u = 4 * half + t
                    ins = dve.tensor_tensor_scan(wmul[:, t], xrp[:, u, 3:3 + T], work[:, u], 0.0, ALU.mult, ALU.add)
                link(ins)
                dve.tensor_tensor(work[:, q, :], wmul, yg[:, q, :], ALU.mult).then_inc(sem("rnn_ob"), 1)
                dve.wait_ge(sem("rnn_ob_hi"), half + 1)
                low(opl[:, 4 + 4 * half:8 + 4 * half, :], work[:, q, :], oph[:, 4 + 4 * half:8 + 4 * half, :], "rnn_ob_lo")
            modulation(stage_groups["mod2"], 8)
            gi = iter(stage_groups["g"])
            for j in range(4):
                for b in range(3):
                    ahead(first_slot[next(gi)] + 2)
                g = stage_groups["branch_ac"][j]
                last = first_slot[g]
                ahead(last + 2)
                dve.wait_ge(sem("slot_used"), last + 1)
                dve.wait_ge(sem("act_read"), reads_at[stage_groups["g"][3 * j + 2]])
                ps = pair[:, pair_seq[g] % PAIRS]
                if j >= 2:
                    dve.wait_ge(sem("merged_hi"), j - 1)
                dve.tensor_tensor(mrg[:, j % 2], ps[:, :, 0:T], g_sig[:, j % 2, 0:2, :], ALU.mult).then_inc(sem("dve_chain"), 1)
                st["chain"] += 1
                dve.tensor_tensor(mrg2[:, j % 2], ps[:, :, T:2 * T], g_sig[:, j % 2, 4:6, :], ALU.mult).then_inc(sem("dve_read"), 1)
                dve.wait_ge(sem("dve_chain"), st["chain"])
                dve.wait_ge(sem("dve_read"), reads_at[g])
                link(dve.tensor_tensor(mrg[:, j % 2], mrg[:, j % 2], mrg2[:, j % 2], ALU.add))
                g = stage_groups["branch_b"][j]
                ps = group(g)
                dve.tensor_tensor(mrg2[:, j % 2], ps, g_sig[:, j % 2, 2:4, :], ALU.mult).then_inc(sem("dve_read"), 1)
                dve.wait_ge(sem("dve_read"), reads_at[g])
                dve.tensor_tensor(mrg[:, j % 2], mrg[:, j % 2], mrg2[:, j % 2], ALU.add).then_inc(sem("merged_f"), 1)
                dve.wait_ge(sem("merged_hi"), j + 1)
                low(opl[:, 16 + 2 * j:18 + 2 * j, :], mrg[:, j % 2], oph[:, 16 + 2 * j:18 + 2 * j, :], "merged_lo")
            for j, g in enumerate(stage_groups["w_out"]):
                add_modulated(g, j, 16)
            nf = VROW["norm_ffn"]
            link(dve.scalar_tensor_tensor(gain[:], mod[:, 32:40], 1.0, vec[:, nf:nf + DC], ALU.add, ALU.mult))
            norm("ffn", xT, lambda c: gain[:, c:c + 1], shift=24)
            ups = stage_groups["up"]
            for j in range(FC + 2):
                if j < FC:
                    ps = group(ups[j])
                    dve.wait_ge(sem("up_tap2"), 2 * (j + 1))
                    for k, back in ((1, 1), (0, 2)):
                        for m in range(2):
                            a = acc[:, j % 3, m]
                            last = k == 0 and m == 1
                            ins = dve.scalar_tensor_tensor(a[:, back:], ps[:, m, 0:T - back],
                                                           col("ffn_conv_w", 44 * k + 22 * m + j), a[:, back:], ALU.mult, ALU.add)
                            ins.then_inc(sem("dve_read" if last else "up_taps"), 1)
                            if k == 1 and m == 1:
                                dve.wait_ge(sem("up_taps"), 3 * j + 2)
                    dve.wait_ge(sem("dve_read"), reads_at[ups[j]])
                if 1 <= j <= FC:
                    i = j - 1
                    dve.wait_ge(sem("up_silu"), i + 1)
                    if i >= 3:
                        dve.wait_ge(sem("u_hi"), i - 2)
                    dve.tensor_tensor(uf[:, i % 3], sg[:, i % 3], acc[:, i % 3, 1], ALU.mult).then_inc(sem("u_ready"), 1)
                if j >= 2:
                    dve.wait_ge(sem("u_hi"), j - 1)
                    low(opl[:, j - 2], uf[:, (j - 2) % 3], oph[:, j - 2], "u_lo")
            for j, g in enumerate(stage_groups["down"]):
                add_modulated(g, j, 40)

            def add_plain(g, j):
                ps = group(g)
                dve.tensor_tensor(xT[:, 2 * j:2 * j + 2, :], ps, xT[:, 2 * j:2 * j + 2, :], ALU.add).then_inc(sem("dve_read"), 1)

            for l in range(2):
                norm(f"mix{l}", xT, lambda c: col("norm_mix_g_2", DC * l + c))
                dve.wait_ge(sem("mix_padded"), l + 1)
                for t, g in enumerate(stage_groups[f"mixa{l}"]):
                    ps = group(g)
                    dve.wait_ge(sem("ya_sig"), 3 * l + t + 1)
                    dve.tensor_tensor(yap[:, t, 30:30 + T], ps[:, 0], sgm[:, t % 2], ALU.mult).then_inc(sem("dve_read"), 1)
                dve.wait_ge(sem("dve_read"), reads_at[g])
                aw, ab = VROW["conv_a_w_2"] + 93 * l, VROW["conv_a_b_2"] + 3 * l
                taps = [(k, t) for k in range(TAPS_A) for t in range(3)]
                done = {"k": 0}

                def conv_a(n):
                    for k, t in taps[done["k"]:done["k"] + n]:
                        if k == 0:
                            ins = dve.tensor_scalar(y8[:, t], yap[:, t, 0:T], vec[:, aw + t:aw + t + 1], vec[:, ab + t:ab + t + 1],
                                                    ALU.mult, ALU.add)
                        else:
                            dve.wait_ge(sem("conv_taps"), 93 * l + 3 * k + t - 2)
                            ins = dve.scalar_tensor_tensor(y8[:, t], yap[:, t, k:k + T], vec[:, aw + 3 * k + t:aw + 3 * k + t + 1],
                                                           y8[:, t], ALU.mult, ALU.add)
                        ins.then_inc(sem("conv_taps"), 1)
                    done["k"] += n

                for stage in ("mix_bg", "mix_bgcg", "mix_cg"):
                    ahead(first_slot[stage_groups[f"{stage}{l}"][0]] + 2)
                    conv_a(9)
                g = stage_groups[f"mix_bin{l}"][0]
                ps = group(g)
                dve.wait_ge(sem("act_read"), reads_at[stage_groups[f"mix_cg{l}"][0]])
                dve.tensor_tensor(prod[:, 0:2, 2:2 + T], ps, cg[:, 0:2, :], ALU.mult).then_inc(sem("dve_read"), 1)
                conv_a(9)
                g = stage_groups[f"mix_binuv{l}"][0]
                ps = group(g)
                dve.wait_ge(sem("mix_v2"), l + 1)
                dve.tensor_tensor(prod[0:64, 2, 2:2 + T], ps[0:64, 0], cg[0:64, 2, :], ALU.mult).then_inc(sem("dve_read"), 1)
                for stage in ("mix_u", "mix_v"):
                    ahead(first_slot[stage_groups[f"{stage}{l}"][0]] + 2)
                    conv_a(9)
                ahead(first_slot[stage_groups[f"mixout{l}"][0]] + 2)
                dve.wait_ge(sem("means_summed"), 2 * l + 1)
                for t in range(3):
                    dve.scalar_tensor_tensor(vb[:, t], misc[:, 0, 0:T], -1.0 / 320, vb[:, t], ALU.mult, ALU.add)\
                        .then_inc(sem("centred"), 1)
                conv_a(12)
                dve.wait_ge(sem("root_ready"), ROOTS.index(f"v{l}") + 1)
                link(dve.reciprocal(rt[:], rt[:]))
                for t in range(3):
                    ins = dve.scalar_tensor_tensor(vb[:, t], vb[:, t], col("ln_c_g_2", 2 * t + l), rt[:], ALU.mult, ALU.mult)
                link(ins)
                for t in range(3):
                    dve.tensor_scalar(vb[:, t], vb[:, t], col("ln_c_b_2", 2 * t + l), None, ALU.add).then_inc(sem("mix_v_normed"), 1)
                conv_a(93 - done["k"])
                dve.wait_ge(sem("conv_taps"), 93 * (l + 1))
                bw = lambda k, t: col("conv_b_w_2", 6 * t + 3 * l + k)
                dve.wait_ge(sem("dve_read"), reads_at[stage_groups[f"mix_binuv{l}"][0]])
                dve.wait_ge(sem("mix_bg2"), l + 1)
                for t in range(3):
                    p = slice(0, 128) if t < 2 else slice(0, 64)
                    link(dve.tensor_scalar(vcb[p, t], prod[p, t, 0:T], bw(0, t)[p], None, ALU.mult))
                    for k in (1, 2):
                        link(dve.scalar_tensor_tensor(vcb[p, t], prod[p, t, k:k + T], bw(k, t)[p], vcb[p, t], ALU.mult, ALU.add))
                    dve.tensor_tensor(y8[p, 3 + t], y8[p, 3 + t], vcb[p, t], ALU.mult).then_inc(sem("b_done"), 1)
                dve.wait_ge(sem("c_mixed"), l + 1)
                dve.wait_ge(sem("gb_landed"), 80 * (l + 1))
                for t in range(3):
                    p = slice(0, 128) if t else slice(64, 128)
                    ps = misc[p, 2 + t // 2, (t % 2) * T:(t % 2 + 1) * T].rearrange("p (i s) -> p i s", i=TB)
                    tmp = vb[p, t].rearrange("p (i s) -> p i s", i=TB)
                    link(dve.tensor_tensor(tmp, ps, gb[p, t, :].unsqueeze(1).to_broadcast([p.stop - p.start, TB, P]), ALU.add))
                    dve.tensor_tensor(y8[p, 5 + t], y8[p, 5 + t], vb[p, t], ALU.mult).then_inc(sem("c_done"), 1)
                dve.wait_ge(sem("means_summed"), 2 * l + 2)
                for t in range(3):
                    dve.scalar_tensor_tensor(y8[:, t], misc[:, 0, 0:T], -1.0 / 384, y8[:, t], ALU.mult, ALU.add)\
                        .then_inc(sem("centred"), 1)
                dve.wait_ge(sem("root_ready"), ROOTS.index(f"a{l}") + 1)
                link(dve.reciprocal(rt[:], rt[:]))
                for t in range(3):
                    dve.scalar_tensor_tensor(y8[:, t], y8[:, t], col("ln_a_g_2", 3 * l + t), rt[:], ALU.mult, ALU.mult)\
                        .then_inc(sem("a_scaled"), 1)
                dve.wait_ge(sem("root_ready"), ROOTS.index(f"y{l}") + 1)
                dve.reciprocal(rt[:], rt[:]).then_inc(sem("y_rs"), 1)
                for c in range(DC):
                    dve.wait_ge(sem("y_spread"), 4 * l + c // 2 + 1)
                    dve.scalar_tensor_tensor(work[:, c], y8[:, c], col("mix_out_g_2", DC * l + c),
                                             misc[:, c // 2, (c % 2) * T:(c % 2 + 1) * T], ALU.mult, ALU.mult).then_inc(sem("y_scaled"), 1)
                for c in range(DC):
                    dve.wait_ge(sem("y_hi"), DC * l + c + 1)
                    low(hl[:, c], work[:, c], hh[:, c], "y_lo")
                for j, g in enumerate(stage_groups[f"mixout{l}"]):
                    add_plain(g, j)
                dve.wait_ge(sem("mem_rt"), l + 1)
                link(dve.reciprocal(tiny[:, 2, 0:2], tiny[:, 1, 0:2]))
                for i in range(TB):
                    dve.tensor_scalar(m_tok[:, i], m_tok[:, i], tiny[:, 2, i:i + 1], None, ALU.mult).then_inc(sem("mem_scaled"), 1)
                mg = VROW["norm_mem_g_2"] + DC * l
                for c in range(DC):
                    dve.wait_ge(sem("mem_hi"), DC * l + c // 2 * 2 + 2)
                    dve.scalar_tensor_tensor(opl[:, c], misc[:, c // 2, (c % 2) * T:(c % 2 + 1) * T], vec[:, mg + c:mg + c + 1],
                                             oph[:, c].bitcast(F32), ALU.mult, ALU.subtract).then_inc(sem("mem_lo"), 1)
                for stage in ("xk", "xv"):
                    for g in stage_groups[f"{stage}{l}"]:
                        ahead(first_slot[g] + 2)
                norm(f"x{l}", xT, lambda c: col("norm_x_g_2", DC * l + c))
                for g in stage_groups[f"xq{l}"]:
                    ahead(first_slot[g] + 2)
                ahead(first_slot[stage_groups[f"xo{l}"][0]] + 2)

                def x_max(h):
                    b = h % 2
                    dve.wait_ge(sem("x_scores"), 4 * l + h + 1)
                    link(dve.tensor_reduce(small[:, b, 0:2], misc[:, b, :].rearrange("p (i m) -> p i m", i=TB), AX_X, ALU.max))
                    dve.tensor_scalar(small[:, b, 2:4], small[:, b, 0:2], -1.0 / 16, None, ALU.mult).then_inc(sem("x_negmax"), 1)

                x_max(0)
                for h in range(4):
                    if h + 1 < 4:
                        x_max(h + 1)
                    b = h % 2
                    dve.wait_ge(sem("x_exp"), 2 * (4 * l + h + 1))
                    link(dve.reciprocal(small[:, b, 6:8], small[:, b, 4:6]))
                    for i in range(TB):
                        dve.tensor_scalar(xp[:, b, i], xp[:, b, i], small[:, b, 6 + i:7 + i], None, ALU.mult).then_inc(sem("x_p"), 1)
                    dve.wait_ge(sem("xo_hi"), 4 * l + h + 1)
                    low(hl[:, 2 * h:2 * h + 2, :], misc[:, 3, :].rearrange("p (a b) -> p a b", a=2), hh[:, 2 * h:2 * h + 2, :], "xo_lo")
                for j, g in enumerate(stage_groups[f"xo{l}"]):
                    add_plain(g, j)
                norm(f"ffn{l}", xT, lambda c: col("norm_ffn_g_2", DC * l + c))
                if l == 0:
                    ups2 = stage_groups["up2"]
                    for j in range(FC + 1):
                        if j < FC:
                            ps = group(ups2[j])
                            dve.wait_ge(sem("up2_silu"), j + 1)
                            if j >= 3:
                                dve.wait_ge(sem("u2_lo"), j - 2)
                            dve.tensor_tensor(uf[:, j % 3], ps[:, 1], sg[:, j % 3], ALU.mult).then_inc(sem("dve_read"), 1)
                        if j >= 1:
                            dve.wait_ge(sem("u2_hi"), j)
                            low(opl[:, j - 1], uf[:, (j - 1) % 3], oph[:, j - 1], "u2_lo")
                    for j, g in enumerate(stage_groups["down2"]):
                        add_plain(g, j)

            ahead(n_dense - 1)
            dve.wait_ge(sem("moe_consts"), 3)
            link(dve.tensor_copy(logit[:], misc[:, 1, 0:TB * NE].rearrange("p (i e) -> p i e", i=TB)))
            for i in range(TB):
                link(dve.max(best[:, i], logit[:, i]))
                link(dve.max_index(besti[:, i], best[:, i], logit[:, i]))
            dve.tensor_tensor(topw[:, :, 0], best[:, :, 1], best[:, :, 0], ALU.subtract).then_inc(sem("top_gap"), 1)
            link(dve.tensor_copy(topw[:, :, 2:4], besti[:, :, 0:2]))
            for i in range(TB):
                for k in range(2):
                    ins = dve.tensor_scalar(pick[:, k, i], iota[:, 0:NE], topw[:, i, 2 + k:3 + k], None, ALU.is_equal)
            link(ins)
            dve.wait_ge(sem("top_exp"), 1)
            link(dve.tensor_scalar(topw[:, :, 2], topw[:, :, 1], 1.0, None, ALU.add))
            link(dve.reciprocal(topw[:, :, 3], topw[:, :, 2]))
            link(dve.tensor_tensor(topw[:, :, 2], topw[:, :, 1], topw[:, :, 3], ALU.mult))
            for i in range(TB):
                link(dve.tensor_scalar(comb[:, i], pick[:, 0, i], topw[:, i, 3:4], None, ALU.mult))
                link(dve.scalar_tensor_tensor(comb[:, i], pick[:, 1, i], topw[:, i, 2:3], comb[:, i], ALU.mult, ALU.add))
            dve.tensor_tensor(pick[:, 0], pick[:, 0], pick[:, 1], ALU.add).then_inc(sem("picked"), 1)
            dve.wait_ge(sem("picked"), 1)
            dve.wait_ge(sem("ranked"), 1)
            link(dve.memset(rankm[:], -1e4))
            link(dve.scalar_tensor_tensor(rankm[:, :, 0:NE], misc[:, 0, 0:TB * NE].rearrange("p (i e) -> p i e", i=TB), 1.0,
                                          pick[:, 0], ALU.add, ALU.mult))
            link(dve.tensor_scalar(rankm[:, :, 0:NE], rankm[:, :, 0:NE], -1.0, None, ALU.add))
            link(dve.tensor_reduce(small[:, 0, 0:1], misc[:, 0, 16:16 + NE], AX_X, ALU.max))
            link(dve.tensor_scalar(small[:, 0, 1:2], small[:, 0, 0:1], float(P), None, ALU.is_gt))
            dve.tensor_copy(flag[0:1, 0:1], small[0:1, 0, 1:2]).then_inc(sem("overflow_known"), 1)
            dve.memset(ye, 0.0).then_inc(sem("m_yc"), 1)
            dve.memset(small[:, 1, 0:1], 0.0).then_inc(sem("m_c"), 1)
            dve.memset(small[:, 1, 1:2], 0.0).then_inc(sem("m_mul"), 2)
            dve.memset(small[:, 1, 2:3], 0.0).then_inc(sem("m_added"), 4)

            def moe_lo(E, k):
                r, q = (n_dense + k) % RAW, (n_dense + k) % SPLIT
                dve.wait_ge(sem("hi_ready"), E * MOE_SLOTS + (n_dense + k + 1))
                dve.tensor_tensor(wlo[:, q, :], raw[:, r, :], whi[:, q, :].bitcast(F32), ALU.subtract).then_inc(sem("lo_ready"), 1)

            def placed(dst, e, weighted, name):
                for i in range(TB):
                    if weighted:
                        ins = dve.tensor_scalar(dst[:, i], iota, rankm[:, i, bass.ds(e, 1)], comb[:, i, bass.ds(e, 1)],
                                                ALU.is_equal, ALU.mult)
                    else:
                        ins = dve.tensor_scalar(dst[:, i], iota, rankm[:, i, bass.ds(e, 1)], None, ALU.is_equal)
                ins.then_inc(sem(name), 1)

            def added(S):
                for r in range(4):
                    dve.wait_ge(sem("m_s"), S * 4 + (r + 1))
                    dve.tensor_tensor(xT[:, 2 * r:2 * r + 2, :], banks[:, r, :].rearrange("p (a b) -> p a b", a=2),
                                      xT[:, 2 * r:2 * r + 2, :], ALU.add).then_inc(sem("m_added"), 1)

            def moe_expert(e, u, p):
                E, Q = e + NE * p, e + (NE + 1) * p
                st["k"] = 2

                def upto(k):
                    while st["k"] <= k:
                        moe_lo(E, st["k"])
                        st["k"] += 1

                def hidden_lo(j):
                    dve.wait_ge(sem("m_hhi"), E * JE + (j + 1))
                    low(h_lo[j % 2], misc[:, 1 if j == JE - 1 else 0, :], h_hi[j % 2], "m_hlo")

                for j in range(JE):
                    upto(gate_last(j) + 2)
                    if j >= 1:
                        hidden_lo(j - 1)
                    if j == 2:
                        placed(place_w, e, True, "m_gw")
                    if j == 5:
                        placed(place, e + 1, False, "m_gt")
                    upto(gate_last(j) + 4)
                    dve.wait_ge(sem("slot_used"), E * MOE_SLOTS + (n_dense + gate_last(j) + 3))
                    dve.wait_ge(sem("m_sil"), E * JE + (j + 1))
                    dve.tensor_tensor(sh[:, j % 2, :], pair[:, j % 2, 1, :], sil[:, j % 2], ALU.mult).then_inc(sem("m_mul"), 1)
                upto(MOE_SLOTS - 1)
                for half in range(2):
                    dve.wait_ge(sem("m_xhi"), Q * 2 + (3 + half))
                    low(xg_lo[1 - u][:, half * 512:(half + 1) * 512], misc[:, 1 - half, :],
                        xg_hi[1 - u][:, half * 512:(half + 1) * 512], "m_xlo")
                hidden_lo(JE - 1)
                added(Q)
                upto(MOE_SLOTS + 1)

            def moe_pass(p):
                if p:
                    dve.tensor_scalar(rankm[:, :, 0:NE], rankm[:, :, 0:NE], -float(P), None, ALU.add).then_inc(sem("ranks_lowered"), 1)
                    dve.wait_ge(sem("ranks_lowered"), 1)
                dve.memset(comb_t[:, 1], 0.0).then_inc(sem("weights_cleared"), 1)
                dve.wait_ge(sem("weights_cleared"), p + 1)
                placed(place, 0, False, "m_gt")
                for half in range(2):
                    dve.wait_ge(sem("m_xhi"), 2 * (NE + 1) * p + half + 1)
                    low(xg_lo[0][:, half * 512:(half + 1) * 512], misc[:, 1 - half, :], xg_hi[0][:, half * 512:(half + 1) * 512], "m_xlo")
                with dve.Fori(0, NE // 2) as i:
                    for u in range(2):
                        moe_expert(2 * i + u, u, p)
                added((NE + 1) * p + NE)

            moe_lo(0, 0)
            moe_lo(0, 1)
            moe_pass(0)
            over = dve.value_load(flag[0:1, 0:1], min_val=0, max_val=1)
            with dve.If(over > 0):
                moe_pass(1)
                dve.wait_ge(sem("m_added"), 8 * (NE + 1) + 4)
            dve.wait_ge(sem("m_added"), 4 * (NE + 1) + 4)
            dve.memset(small[:, 1, 3:4], 0.0).then_inc(sem("moe_added"), 1)
            dve.wait_ge(sem("fin_act"), 3)
            link(dve.reciprocal(rt[:], rt[:]))
            for c in range(DC):
                dve.scalar_tensor_tensor(work[:, c], xT[:, c], col("norm_final_g_2", c), rt[:], ALU.mult, ALU.mult)\
                    .then_inc(sem("fin_scaled"), 1)


_INS = ['x', 'c', 'w_mod', 'b_mod', 'norm_mix', 'norm_ffn', 'w_in', 'qnorm_a', 'knorm_a', 'sinks', 'rnn_conv_w',
        'rnn_conv_b', 'rnn_gate_a_w', 'rnn_gate_a_b', 'rnn_gate_x_w', 'rnn_gate_x_b', 'rnn_lambda', 'qnorm_c',
        'knorm_c', 'rel_bias', 'w_branch', 'w_out', 'w_up', 'ffn_conv_w', 'ffn_conv_b', 'w_down', 'mem_2',
        'norm_mix_g_2', 'w_in_2', 'conv_a_w_2', 'conv_a_b_2', 'ln_a_g_2', 'ln_a_b_2', 'conv_b_w_2', 'ln_c_g_2',
        'ln_c_b_2', 'gmlp_ws_2', 'gmlp_b_2', 'mix_out_g_2', 'w_mix_out_2', 'norm_x_g_2', 'norm_mem_g_2', 'w_xq_2',
        'w_xkv_2', 'w_xo_2', 'norm_ffn_g_2', 'ffn_w_gate_2', 'ffn_w_up_2', 'ffn_w_down_2', 'moe_router_2',
        'moe_w_gate_2', 'moe_w_up_2', 'moe_w_down_2', 'norm_final_g_2']


def lay_out(nc, inputs):
    arrays, w = {}, {}
    for name in _INS:
        a = np.ascontiguousarray(inputs[name])
        arrays[f"in_{name}_dram"] = a
        w[name] = nc.dram_tensor(f"in_{name}_dram", a.shape, mybir.dt.from_np(a.dtype), kind="ExternalInput").ap()
    arrays["bucket_onehot_dram"] = bucket_onehot()
    onehot = nc.dram_tensor("bucket_onehot_dram", (32, T), F32, kind="ExternalInput").ap()
    out = nc.dram_tensor("out_0_dram", (1, T, D), F32, kind="ExternalOutput").ap()
    bias_dram = nc.dram_tensor("bias_rows", (NHEAD, 512), F32).ap()
    build_program(nc, w, onehot, out, bias_dram)
    return arrays


def kernel(**inputs):
    import concourse.bacc as _bacc
    from concourse.bass_utils import run_bass_kernel_spmd as _run

    nc = _bacc.Bacc("TRN2", target_bir_lowering=False, num_devices=1)
    arrays = lay_out(nc, inputs)
    r = _run(nc, [arrays], core_ids=[0])
    return r.results[0]["out_0_dram"]
```

```python
from contextlib import ExitStack

import numpy as np
import concourse.bass as bass
from concourse import mybir

ALU = mybir.AluOpType
ACT = mybir.ActivationFunctionType
F32 = mybir.dt.float32
F32R = mybir.dt.float32r
U32 = mybir.dt.uint32
I32 = mybir.dt.int32
AX_X = mybir.AxisListType.X

P = 128
T = 256
TB = T // P
D = 1024
DC = D // P
HD = 64
NHEAD = 16
FF = 2816
FC = FF // P
EPS = 1e-6
NEG = -1e30
WIN = 128
NE = 8
DE = 3584
JE = DE // 512
TAPS_A = 31
SLOT = 2048
RAW = 6
SPLIT = 3
PAIRS = 2
MOE_SLOTS = 6 * JE

QA, KA, VA, XR, YR, QC, KC, VC, GL = 0, 512, 640, 768, 1792, 2816, 3328, 3840, 4352
A_VAL, A_GATE, B_GATE, C_GATE, B_IN, C_U, C_V = 0, 384, 768, 1088, 1408, 1728, 2048

VEC = [("b_mod", 48), ("norm_mix", 8), ("norm_ffn", 8), ("rnn_conv_w", 32), ("rnn_conv_b", 8),
       ("rnn_gate_a_b", 8), ("rnn_gate_x_b", 8), ("rnn_lambda", 8),
       ("ffn_conv_w", 132), ("ffn_conv_b", 44),
       ("norm_mix_g_2", 16), ("norm_x_g_2", 16), ("norm_mem_g_2", 16), ("norm_ffn_g_2", 16), ("norm_final_g_2", 8),
       ("conv_a_w_2", 186), ("conv_a_b_2", 6), ("ln_a_g_2", 6), ("ln_a_b_2", 6), ("mix_out_g_2", 16),
       ("conv_b_w_2", 18), ("ln_c_g_2", 6), ("ln_c_b_2", 6),
       ("qnorm_a", 1), ("knorm_a", 1), ("qnorm_c", 1), ("knorm_c", 1)]
PIECEWISE = ("conv_b_w_2", "ln_c_g_2", "ln_c_b_2")
DOUBLED = ("qnorm_a", "knorm_a", "qnorm_c", "knorm_c")
VROW = {}
_at = 0
for _n, _r in VEC:
    VROW[_n] = _at
    _at += _r
N_VEC = _at
NV = -(-_at // P)


def vec_dmas():
    n = 0
    for name, rows in VEC:
        r = VROW[name]
        n += 2 if name in DOUBLED else 3 if name in PIECEWISE else (r + rows - 1) // P - r // P + 1
    return n


N_VEC_DMAS = vec_dmas()

SUMS = ["mix", "ffn"] + [f"{k}{l}" for l in range(2) for k in ("mix", "v", "a", "y", "x", "ffn")]
ROOTS = SUMS[:1] + ["qk"] + SUMS[1:]
NORM = {"mix": 0, "ffn": 1, "mix0": 2, "x0": 3, "ffn0": 4, "mix1": 5, "x1": 6, "ffn1": 7}


def bucket_onehot():
    dist = np.arange(T)
    large = 16 + (np.log(np.maximum(dist, 1).astype(np.float32) / 16) / np.float32(np.log(2048 / 16)) * 16).astype(np.int32)
    bucket = np.where(dist < 16, dist, np.minimum(large, 31))
    out = np.zeros((32, T), np.float32)
    out[bucket, T - 1 - dist] = 1.0
    return out


def plan(w):
    groups = []

    def rows(src, k0, n):
        return src[k0 * P:(k0 + n) * P, :]

    def dense(stage, src, cols, reader, kchunks=DC, k0=0):
        slots = []
        for c0 in range(0, kchunks, 8):
            n = min(8, kchunks - c0)
            parts, at = [], 0
            for col, width in cols:
                parts.append((rows(src, k0 + c0, n), 0, n, col, width, at))
                at += width
            slots.append((parts, n))
        groups.append((stage, slots, reader))

    w_in = w["w_in"][0]
    for j in range(8):
        dense("mod1", w["w_mod"][0], [(j * 256, 256)], None)
    for j in range(2):
        dense("qa", w_in, [(QA + j * 256, 256)], "act")
    dense("ka", w_in, [(KA, 64), (KA, 64), (KA + 64, 64), (KA + 64, 64)], "act")
    for j in range(2):
        dense("qc", w_in, [(QC + j * 256, 256)], "act")
    for j in range(2):
        dense("kc", w_in, [(KC + j * 256, 256)], "act")
    dense("va", w_in, [(VA, 128)], "act")
    for j in range(2):
        dense("vc", w_in, [(VC + j * 256, 256)], "act")
    for j in range(8, 16):
        dense("mod2", w["w_mod"][0], [(j * 256, 256)], None)
    for j in range(4):
        dense("xr", w_in, [(XR + j * 256, 256)], "act")
    for j in range(4):
        dense("yr", w_in, [(YR + j * 256, 256)], "act")
    for j in range(16, 24):
        dense("mod3", w["w_mod"][0], [(j * 256, 256)], None)
    wb = w["w_branch"][0]
    for j in range(4):
        for b in range(3):
            dense("g", w_in, [(GL + b * D + j * 256, 256)], "act")
        parts = [(rows(wb, 0, 4), 0, 4, j * 256, 256, 0), (rows(wb, 12, 4), 4, 4, j * 256, 256, 0)]
        groups.append(("branch_ac", [(parts, 8)], "dve"))
        dense("branch_b", wb, [(j * 256, 256)], "dve", k0=4)
    for j in range(4):
        dense("w_out", w["w_out"][0], [(j * 256, 256)], "dve")
    for j in range(FC):
        dense("up", w["w_up"][0], [(j * P, P), (FF + j * P, P)], "dve")
    for j in range(4):
        dense("down", w["w_down"][0], [(j * 256, 256)], "dve", FC)
    for l in range(2):
        wi = w["w_in_2"][l]
        for t in range(3):
            dense(f"mixa{l}", wi, [(A_VAL + t * P, P), (A_GATE + t * P, P)], "dve")
        dense(f"mix_bg{l}", wi, [(B_GATE, 256)], "act")
        dense(f"mix_bgcg{l}", wi, [(B_GATE + 256, P), (C_GATE + 256, P)], "act")
        dense(f"mix_cg{l}", wi, [(C_GATE, 256)], "act")
        dense(f"mix_bin{l}", wi, [(B_IN, 256)], "dve")
        dense(f"mix_binuv{l}", wi, [(B_IN + 256, P), (C_V + 192, P)], "dve")
        dense(f"mix_u{l}", wi, [(C_U + 64, 256)], "act")
        dense(f"mix_v{l}", wi, [(C_V - 64, 256)], "act")
        for j in range(4):
            dense(f"xk{l}", w["w_xkv_2"][l], [(j * 256, 256)], "dve")
        for j in range(4):
            dense(f"xv{l}", w["w_xkv_2"][l], [(D + j * 256, 256)], "dve")
        for j in range(4):
            dense(f"mixout{l}", w["w_mix_out_2"][l], [(j * 256, 256)], "dve")
        for j in range(4):
            dense(f"xq{l}", w["w_xq_2"][l], [(j * 256, 256)], "dve")
        for j in range(4):
            dense(f"xo{l}", w["w_xo_2"][l], [(j * 256, 256)], "dve")
        if l == 0:
            for j in range(FC):
                slot = [(w["ffn_w_gate_2"][0], 0, 8, j * P, P, 0), (w["ffn_w_up_2"][0], 0, 8, j * P, P, P)]
                groups.append(("up2", [(slot, 8)], "dve"))
            for j in range(4):
                dense("down2", w["ffn_w_down_2"][0], [(j * 256, 256)], "dve", FC)
    return groups


def build_program(nc, w, onehot, out, bias_dram):
    groups = plan(w)
    first_slot, at = [], 0
    for _, slots, _ in groups:
        first_slot.append(at)
        at += len(slots)
    n_dense = at
    stage_groups = {}
    for g, (stage, _, _) in enumerate(groups):
        stage_groups.setdefault(stage, []).append(g)
    order, pair_seq, reads_at = [], {}, {}
    count = {"act": 0, "dve": 0}
    for g, (_, _, reader) in enumerate(groups):
        if reader:
            count[reader] += 1
            reads_at[g] = count[reader]
            pair_seq[g] = len(order)
            order.append(g)
    landed_at, total, size_of, plain_no, split_no = {}, [0] * RAW, {}, {}, {}
    n = 0
    for stage, slots, reader in groups:
        for parts, _ in slots:
            if reader is None:
                plain_no[n] = len(plain_no)
            else:
                split_no[n] = len(split_no)
            total[n % RAW] += 16 * len(parts)
            landed_at[n] = total[n % RAW]
            size_of[n] = 256 * max(p[1] + p[2] for p in parts)
            n += 1
    n_split = len(split_no)
    mod_slots = [first_slot[g] for m in ("mod1", "mod2", "mod3") for g in stage_groups[m]]

    ctx = ExitStack()
    with ctx:
        def sb(name, shape, dt=F32):
            return ctx.enter_context(nc.sbuf_tensor(name, shape, dt))

        sems = {}

        def sem(name):
            if name not in sems:
                sems[name] = ctx.enter_context(nc.semaphore(name))
            return sems[name]

        raw = sb("raw", [P, RAW, SLOT])
        whi = sb("whi", [P, SPLIT, SLOT], F32R)
        wlo = sb("wlo", [P, SPLIT, SLOT], F32R)
        xT = sb("xT", [P, DC, T])
        hh = sb("hh", [P, DC, T], F32R)
        hl = sb("hl", [P, DC, T], F32R)
        oph = sb("oph", [P, 24, T], F32R)
        opl = sb("opl", [P, 24, T], F32R)
        work = sb("work", [P, DC, T])
        arena = sb("arena", [P, 5888])
        vec = sb("vec", [P, N_VEC])
        mod = sb("mod", [P, 48])
        gain = sb("gain", [P, DC])
        coef = sb("coef", [P, DC])
        tiny = sb("tiny", [P, 8, DC])
        cact = sb("cact", [P, DC])
        rt = sb("rt", [P, T])
        ident = sb("ident", [P, P])
        ones = sb("ones", [P, P])
        hsel = sb("hsel", [P, 162])
        spread = sb("spread", [P, 512])
        sinks = sb("sinks", [P, 8])
        consts = sb("consts", [P, 4])
        small = sb("small", [P, 2, 8])
        pair = ctx.enter_context(nc.psum_tensor("pair", [P, PAIRS, 2, 512], F32))
        misc = ctx.enter_context(nc.psum_tensor("misc", [P, 4, 512], F32))
        banks = pair[:, :, :, :].rearrange("p a b c -> p (a b) c")

        flag = sb("flag", [1, 1], I32)
        rw = sb("rw", [P, DC, NE])
        logit = sb("logit", [P, TB, NE])
        best = sb("best", [P, TB, 8])
        besti = sb("besti", [P, TB, 8], U32)
        topw = sb("topw", [P, TB, 4])
        pick = sb("pick", [P, 2, TB, NE])
        comb = sb("comb", [P, TB, NE])
        rankm = sb("rankm", [P, TB, NE + 2])

        block = ctx.enter_context(nc.Block())

        def aview(at, *shape):
            size = int(np.prod(shape))
            v = arena[:, at:at + size]
            if len(shape) == 1:
                return v
            names = "abc"[:len(shape)]
            return v.rearrange(f"p ({' '.join(names)}) -> p {' '.join(names)}",
                               **{k: s for k, s in zip(names, shape)})

        stage_rows = aview(0, NV, P)
        start_sq = aview(3072, DC, T)
        oh = arena[0:32, 2048:2048 + T]
        relb = arena[0:32, 2400:2400 + NHEAD]
        brow = arena[0:NHEAD, 2560:2560 + 512]
        x_tok = work[:, :, :].rearrange("p a b -> p (a b)").rearrange("p (i d) -> p i d", i=TB)
        qa, ka, qc, kc = aview(0, 4, T), aview(1024, 2, T), aview(1536, 4, T), aview(2560, 4, T)
        va, vc = aview(3584, TB, 128), aview(3840, TB, 512)
        qk = aview(0, 14, T)
        qk_sq = aview(4864, 2, 2, T)
        s_buf = [work[:, 0:2, :].rearrange("p a b -> p (a b)")[:, 0:384],
                 work[:, 2:4, :].rearrange("p a b -> p (a b)")[:, 0:384]]
        pt_buf = [work[:, 4:6, :].rearrange("p a b -> p (a b)")[:, 0:384],
                  aview(4864, 384)]
        bias_buf = [work[:, 6, :].rearrange("p (a b) -> p a b", a=2), work[:, 7, :].rearrange("p (a b) -> p a b", a=2)]
        def mrow(j):
            return rt[0:1, :] if j >= 16 else arena[0:1, 5248 + T * (j % 2):5248 + T * (j % 2 + 1)]

        flip = work[:, 0:2, :].rearrange("p a b -> p (a b)")[:, 384:512]
        xrp, yg = aview(0, DC, T + 3), aview(2080, DC, T)
        gw = aview(4128, 2, DC, HD)
        xc = aview(5152, 2, T)
        wmul = [aview(4128, 4, T), banks[:, 0:2, :].rearrange("p a (c t) -> p (a c) t", t=T)]
        tmp2 = aview(5152, 2, T)
        g_sig = aview(0, 2, 6, T)
        mrg = aview(3072, 2, 2, T)
        mrg2 = aview(4096, 2, 2, T)
        acc = aview(0, 3, 2, T)
        sg = aview(1536, 3, T)
        uf = aview(2304, 3, T)
        y8 = aview(0, DC, T)
        yap = aview(2048, 3, T + 30)
        cg = aview(2048 + 858, 3, T)
        prod = aview(2048 + 858 + 768, 3, T + 2)
        vb = aview(2048 + 858 + 768 + 774, 3, T)
        sgm = aview(5216, 2, T)
        vcb = cg
        wflat = work[:, :, :].rearrange("p a b -> p (a b)")
        vtok = wflat[:, 0:768].rearrange("p (i f) -> p i f", i=TB)
        wst = wflat[:, 768:768 + 640].rearrange("p (g j) -> p g j", g=5)
        wsl = wflat[:, 1408:1408 + 640].rearrange("p (g j) -> p g j", g=5)
        gb = aview(5216, 3, P)
        sq3 = cg
        m_tok = work[:, :, :].rearrange("p a b -> p (a b)").rearrange("p (i d) -> p i d", i=TB)
        m_sq = oph[:, 0:8, :].rearrange("p a b -> p (a b)").rearrange("p (i d) -> p i d", i=TB)
        queries, keys_at = [b[:, 0:8, :] for b in (oph, opl)], [b[:, 8:16, :] for b in (oph, opl)]
        values_at = [b[:, 16:24, :].rearrange("p a b -> p (a b)").rearrange("p (i d) -> p i d", i=TB) for b in (oph, opl)]
        xp = aview(0, 2, 2, T)

        hn_tok = aview(0, TB, D)
        place = wflat[:, 128:384].rearrange("p (i s) -> p i s", i=TB)
        place_w = wflat[:, 384:640].rearrange("p (i s) -> p i s", i=TB)
        comb_t = wflat[:, 640:1152].rearrange("p (b t) -> p b t", b=2)
        ye = aview(2048, D)
        sil, sh = aview(3072, 2, 512), aview(4096, 2, 512)
        ohf, olf = oph[:, :, :].rearrange("p a b -> p (a b)"), opl[:, :, :].rearrange("p a b -> p (a b)")
        xg_hi, xg_lo = [ohf[:, b * D:(b + 1) * D] for b in range(2)], [olf[:, b * D:(b + 1) * D] for b in range(2)]
        h_hi = [ohf[:, 2 * D + b * 512:2 * D + (b + 1) * 512] for b in range(2)]
        h_lo = [olf[:, 2 * D + b * 512:2 * D + (b + 1) * 512] for b in range(2)]
        iota = aview(5120, P)
        tri = rt[:, 0:P]

        def x_bank(l, h):
            return pair[:, 1 - pair_seq[stage_groups[f"xo{l}"][0]] % PAIRS, h % 2, :]

        def exps(h):
            return 3 * (h + 1) if h < 8 else 24 + 2 * (h - 7)

        def gate_last(j):
            return 1 if j == 0 else 6 * j - 1

        @block.sync
        def _(sp):
            def vector_loads():
                sp.wait_ge(sem("rows_cleared"), 1)
                for name, rows in VEC:
                    r = VROW[name]
                    if name in DOUBLED:
                        for half in (0, 64):
                            sp.dma_start(stage_rows[r % P:r % P + 1, r // P, half:half + 64], w[name])\
                                .then_inc(sem("vec_landed"), 16)
                        continue
                    if name in PIECEWISE:
                        per = rows // 3
                        src = w[name] if len(w[name].shape) == 2 else w[name].rearrange("l k c -> (l k) c")
                        pieces = [(0, 128, 0), (128, 256, 0), (256, 320, 0)] if name == "conv_b_w_2" else \
                            [(0, 64, 64), (64, 192, 0), (192, 320, 0)]
                        for i, (a, b, o) in enumerate(pieces):
                            q = r + i * per
                            sp.dma_start(stage_rows[q % P:q % P + per, q // P, o:o + b - a], src[:, a:b])\
                                .then_inc(sem("vec_landed"), 16)
                        continue
                    flat = w[name]
                    dims = "abc"[:len(flat.shape) - 1]
                    if len(flat.shape) == 1:
                        flat = flat.rearrange("(r p) -> r p", p=P)
                    elif len(flat.shape) == 2:
                        flat = flat.rearrange("a (r p) -> (a r) p", p=P)
                    else:
                        flat = flat.rearrange("a b (r p) -> (a b r) p", p=P)
                    done = 0
                    while done < rows:
                        q = r + done
                        k = min(rows - done, P - q % P)
                        sp.dma_start(stage_rows[q % P:q % P + k, q // P, :], flat[done:done + k, :])\
                            .then_inc(sem("vec_landed"), 16)
                        done += k
                sp.dma_start(oh, onehot).then_inc(sem("table_landed"), 16)
                sp.dma_start(relb, w["rel_bias"]).then_inc(sem("table_landed"), 16)
                sp.dma_start(sinks[:], bass.AP(w["sinks"].tensor, 0, [[0, P], [1, 8]])).then_inc(sem("table_landed"), 16)

            sp.dma_start(x_tok, w["x"][0].rearrange("(i p) d -> p i d", p=P)).then_inc(sem("x_landed"), 16)
            sp.dma_start(cact[:], w["c"][0].rearrange("(k p) -> p k", p=P),
                         allow_slow_non_contiguous=True).then_inc(sem("c_landed"), 16)
            n = 0
            for _, slots, _ in groups:
                for parts, _ in slots:
                    if n == RAW:
                        vector_loads()
                    if n >= RAW and n - RAW in plain_no:
                        sp.wait_ge(sem("plain_used"), plain_no[n - RAW] + 1)
                    elif n >= RAW:
                        sp.wait_ge(sem("lo_ready"), split_no[n - RAW] + 1)
                    dst = raw[:, n % RAW, :].rearrange("p (c m) -> p c m", m=256)
                    for src, c0, nc_, col, width, at_ in parts:
                        sp.dma_start(dst[:, c0:c0 + nc_, at_:at_ + width],
                                     src.rearrange("(c p) m -> p c m", p=P)[:, :, col:col + width])\
                          .then_inc(sem(f"landed{n % RAW}"), 16)
                    n += 1
            wg, wu, wd = (w[x][0] for x in ("moe_w_gate_2", "moe_w_up_2", "moe_w_down_2"))

            def source(e, k):
                j, r = (0, k) if k < 4 else ((k - 4) // 6 + 1, (k - 4) % 6)
                if j < JE and r < 4:
                    src = (wg, wu)[r // 2][e, (r % 2) * 512:(r % 2 + 1) * 512, j * 512:(j + 1) * 512]
                    return src.rearrange("(c p) m -> p c m", p=P), 512
                half = r - 4 if j < JE else r
                row = (j - 1) * 512 + half * 256
                return wd[e, row:row + 256, :].rearrange("(c p) m -> p c m", p=P), D

            def load(E, e, k):
                r = (n_dense + k) % RAW
                sp.wait_ge(sem("lo_ready"), E * MOE_SLOTS + (n_split + k - RAW + 1))
                src, width = source(e, k % MOE_SLOTS)
                sp.dma_start(raw[:, r, :].rearrange("p (c m) -> p c m", m=width), src).then_inc(sem(f"landed{r}"), 16)

            def moe_pass(p):
                with sp.Fori(0, NE - 1) as e:
                    for k in range(2, MOE_SLOTS):
                        load(e + NE * p, e, k)
                    for k in (0, 1):
                        load(e + NE * p, e + 1, k + MOE_SLOTS)
                for k in range(2, MOE_SLOTS):
                    load(NE - 1 + NE * p, NE - 1, k)
                for k in (0, 1):
                    load(NE - 1 + NE * p, 0, k + MOE_SLOTS)

            load(0, 0, 0)
            load(0, 0, 1)
            moe_pass(0)
            sp.wait_ge(sem("overflow_known"), 1)
            over = sp.value_load(flag[0:1, 0:1], min_val=0, max_val=1)
            with sp.If(over > 0):
                moe_pass(1)
            sp.wait_ge(sem("out_written"), 16 * TB)

        @block.gpsimd
        def _(pool):
            st = {"chain": 0}

            def link(ins):
                st["chain"] += 1
                ins.then_inc(sem("pool_chain"), 1)
                pool.wait_ge(sem("pool_chain"), st["chain"])

            link(pool.memset(ident[:], 0.0))
            link(pool.affine_select(out=ident[:], in_=ident[:], compare_op=ALU.not_equal, fill=1.0, base=0,
                                    pattern=[[-1, P]], channel_multiplier=1))
            link(pool.memset(ones[:], 1.0))
            link(pool.memset(hsel[:], 0.0))
            link(pool.memset(hsel[0:64, 0:162:32], 1.0))
            link(pool.memset(hsel[64:128, 1:162:32], 1.0))
            link(pool.memset(consts[:, 1:2], 1e-30))
            link(pool.memset(spread[:], 1.0))
            for b in range(4):
                rows = spread[32 * b:32 * b + 32, :]
                link(pool.affine_select(out=rows, in_=rows, compare_op=ALU.is_ge, fill=0.0, base=512 * b,
                                        pattern=[[1, 512]], channel_multiplier=-64))
                link(pool.affine_select(out=rows, in_=rows, compare_op=ALU.is_ge, fill=0.0, base=63 - 512 * b,
                                        pattern=[[-1, 512]], channel_multiplier=64))
            pool.memset(consts[:, 0:1], EPS).then_inc(sem("consts_ready"), 1)
            pool.wait_ge(sem("brow_ready"), 2)
            pool.dma_start(bias_dram, brow).then_inc(sem("brow_stored"), 16)
            pool.wait_ge(sem("brow_stored"), 16)
            pool.wait_ge(sem("h_lo"), DC)
            link(pool.memset(flip, 0.0))
            pool.affine_select(out=flip, in_=flip, compare_op=ALU.not_equal, fill=1.0, base=1 - P, pattern=[[1, P]],
                               channel_multiplier=1).then_inc(sem("flip_ready"), 1)
            for h in range(NHEAD):
                if h >= 2:
                    pool.wait_ge(sem("att_scores"), h - 1)
                pool.dma_start(bias_buf[h % 2], bass.AP(bias_dram.tensor, h * 512, [[1, P], [P, 2], [1, P]]))\
                    .then_inc(sem(f"bias_landed{h % 2}"), 16)
            pool.wait_ge(sem("att_out_lo"), 8)
            pool.memset(xrp[:, :, 0:3], 0.0).then_inc(sem("xr_padded"), 1)
            for k, name in enumerate(("rnn_gate_a_w", "rnn_gate_x_w")):
                for half in range(2):
                    src = w[name][0].rearrange("(t h) c d -> h c t d", h=2)
                    pool.dma_start(gw[64 * half:64 * half + 64, k], src[half]).then_inc(sem("gate_w_landed"), 16)
            for l in range(2):
                pool.wait_ge(sem("dve_read"), reads_at[stage_groups[("down", "down2")[l]][-1]])
                link(pool.memset(yap[:, :, 0:30], 0.0))
                pool.memset(prod[:, :, 0:2], 0.0).then_inc(sem("mix_padded"), 1)
                pool.wait_ge(sem("h_lo"), DC * (NORM[f"mix{l}"] + 1))
                pool.dma_start(m_tok, w["mem_2"][0].rearrange("(i p) d -> p i d", p=P)).then_inc(sem("mem_landed"), 16)
                pool.wait_ge(sem("mem_turned"), 4 * (l + 1))
                pool.dma_start(wsl, w["gmlp_ws_2"][l].rearrange("g i j -> i g j")).then_inc(sem("ws_landed"), 16)
                pool.wait_ge(sem("ws_landed"), 16 * (l + 1))
                pool.wait_ge(sem("mix_padded"), l + 1)
                pool.memset(wsl[0:64, :, 64:128], 0.0).then_inc(sem("ws_masked"), 1)
                pool.wait_ge(sem("mix_v_normed"), 3 * (l + 1))
                for k in range(3):
                    for half in range(2):
                        g = 2 * k - 1 + half
                        if g < 0:
                            continue
                        pool.dma_start(gb[64 * half:64 * half + 64, k, :],
                                       bass.AP(w["gmlp_b_2"].tensor, (l * 5 + g) * P, [[0, 64], [1, P]]))\
                            .then_inc(sem("gb_landed"), 16)
            pool.dma_start(rw[:], w["moe_router_2"][0].rearrange("(c p) e -> p c e", p=P)).then_inc(sem("router_landed"), 16)
            pool.wait_ge(sem("h_scaled"), DC * (NORM["ffn1"] + 1))
            pool.wait_ge(sem("ws_masked"), 2)
            pool.memset(tri, 1.0).then_inc(sem("moe_consts"), 1)
            pool.wait_ge(sem("moe_consts"), 1)
            pool.affine_select(out=tri, in_=tri, compare_op=ALU.is_gt, fill=0.0, base=0, pattern=[[1, P]],
                               channel_multiplier=-1).then_inc(sem("moe_consts"), 1)
            pool.wait_ge(sem("moe_consts"), 2)
            pool.iota(iota, pattern=[[1, P]], base=0, channel_multiplier=0,
                      allow_small_or_imprecise_dtypes=True).then_inc(sem("moe_consts"), 1)

        @block.scalar
        def _(act):
            st = {"hi": 0}

            def ahead(n):
                while st["hi"] <= min(n, n_dense - 1):
                    s = st["hi"]
                    st["hi"] += 1
                    if s in plain_no:
                        continue
                    i = split_no[s]
                    act.wait_ge(sem(f"landed{s % RAW}"), landed_at[s])
                    if i >= SPLIT:
                        act.wait_ge(sem("slot_used"), i - SPLIT + 1)
                    size = size_of[s]
                    act.copy(whi[:, i % SPLIT, 0:size], raw[:, s % RAW, 0:size]).then_inc(sem("hi_ready"), 1)

            def group(g):
                last = first_slot[g] + len(groups[g][1]) - 1
                ahead(last + 2)
                act.wait_ge(sem("slot_used"), split_no[last] + 1)
                return pair[:, pair_seq[g] % PAIRS, :, 0:T]

            def norm(name, src, after, shift=None):
                k = NORM[name]
                for j in range(4):
                    g = stage_groups[after][j]
                    ahead(first_slot[g] + len(groups[g][1]) + 1)
                    act.wait_ge(sem("dve_read"), reads_at[g])
                    act.activation(work[:, 2 * j:2 * j + 2, :], src[:, 2 * j:2 * j + 2, :], ACT.Square).then_inc(sem("sq_ready"), 1)
                act.wait_ge(sem("squares_summed"), SUMS.index(name) + 1)
                act.activation(rt[:], misc[:, 0, 0:T], ACT.Sqrt, bias=consts[:, 0:1], scale=1.0 / D)\
                    .then_inc(sem("root_ready"), 1)
                if name != "ffn1":
                    high(name, shift)

            def high(name, shift=None):
                k = NORM[name]
                for c in range(DC):
                    act.wait_ge(sem("h_scaled"), DC * k + c + 1)
                    if shift is None:
                        act.copy(hh[:, c], work[:, c]).then_inc(sem("h_hi"), 1)
                    else:
                        act.activation(hh[:, c], work[:, c], ACT.Identity, bias=mod[:, shift + c:shift + c + 1])\
                            .then_inc(sem("h_hi"), 1)

            def mod_row(j):
                act.wait_ge(sem("plain_used"), j + 1)
                act.copy(mrow(j), banks[0:1, 2 + j % 2, 0:T]).then_inc(sem("mod_row"), 1)

            act.wait_ge(sem("c_landed"), 16)
            act.activation(cact[:], cact[:], ACT.Silu).then_inc(sem("c_ready"), 1)
            for j in range(8):
                mod_row(j)
                if j < 4:
                    act.wait_ge(sem("x_turned"), j + 1)
                    act.copy(xT[:, 2 * j:2 * j + 2, :], banks[:, j % 2, :].rearrange("p (c t) -> p c t", c=2))\
                        .then_inc(sem("x_copied"), 1)
                    act.wait_ge(sem("x_copied"), j + 1)
                    act.activation(start_sq[:, 2 * j:2 * j + 2, :], xT[:, 2 * j:2 * j + 2, :], ACT.Square).then_inc(sem("sq_ready"), 1)
                if j == 5:
                    act.wait_ge(sem("squares_summed"), 1)
                    act.activation(rt[:], misc[:, 0, 0:T], ACT.Sqrt, bias=consts[:, 0:1], scale=1.0 / D)\
                        .then_inc(sem("root_ready"), 1)
                    ahead(first_slot[stage_groups["qa"][0]] + 1)
            act.wait_ge(sem("vec_ready"), NV)
            high("mix", shift=0)
            act.wait_ge(sem("vec_ready"), NV)
            act.activation(tiny[:, 0], vec[:, VROW["rnn_lambda"]:VROW["rnn_lambda"] + DC], ACT.Abs)\
                .then_inc(sem("act_start"), 1)
            act.wait_ge(sem("act_start"), 1)
            act.activation(tiny[:, 1], tiny[:, 0], ACT.Exp, scale=-1.0).then_inc(sem("act_start"), 1)

            tiles = [("qa", qa), ("ka", ka), ("qc", qc), ("kc", kc)]
            act.wait_ge(sem("brow_stored"), 16)
            i = 0
            for stage, dst in tiles:
                for j, g in enumerate(stage_groups[stage]):
                    ps = group(g)
                    if i >= 2:
                        act.wait_ge(sem("qk_ss"), i - 1)
                    act.activation(qk_sq[:, i % 2], ps, ACT.Square).then_inc(sem("qk_sq"), 1)
                    act.copy(dst[:, 2 * j:2 * j + 2, :], ps).then_inc(sem("act_read"), 1)
                    i += 1
            for j, g in enumerate(stage_groups["va"]):
                ps = group(g)
                act.copy(va, ps[:, :, 0:P]).then_inc(sem("act_read"), 1)
            act.wait_ge(sem("qk_ss"), 7)
            act.activation(rt[:], misc[:, 0, 0:T], ACT.Sqrt, bias=consts[:, 0:1], scale=1.0 / HD)\
                .then_inc(sem("root_ready"), 1)
            for j, g in enumerate(stage_groups["vc"]):
                ps = group(g)
                act.copy(vc[:, :, j * 256:(j + 1) * 256], ps).then_inc(sem("act_read"), 1)


            def expo(h):
                b, s = h % 2, small[:, h % 2]
                act.wait_ge(sem("att_negmax"), h + 1)
                if h >= 2:
                    act.wait_ge(sem("att_pt"), h - 1)
                act.activation(s_buf[b][:, 0:P], misc[:, b, 0:P], ACT.Exp, bias=s[:, 2:3], accum_out=s[:, 4:5])\
                    .then_inc(sem("att_exp"), 1)
                act.activation(s_buf[b][:, P:384], misc[:, b, P:384], ACT.Exp, bias=s[:, 3:4], accum_out=s[:, 5:6])\
                    .then_inc(sem("att_exp"), 1)
                if h < 8:
                    act.activation(s[:, 6:8], s[:, 2:4], ACT.Exp, bias=sinks[:, h:h + 1]).then_inc(sem("att_exp"), 1)

            def turned(h):
                act.wait_ge(sem("att_pt"), h + 1)
                if h >= 2:
                    act.wait_ge(sem("att_o"), h - 1)
                act.copy(pt_buf[h % 2], misc[:, 2, 0:384]).then_inc(sem("att_pt_sb"), 1)

            def out_high(i):
                act.wait_ge(sem("att_o"), 2 * i + 2)
                chunk = i if i < 4 else 8 + i
                act.copy(oph[:, chunk], banks[:, i % 2, 0:T]).then_inc(sem("att_out_hi"), 1)

            expo(0)
            for h in range(NHEAD):
                if h + 1 < NHEAD:
                    expo(h + 1)
                turned(h)
                if h % 2 == 0 and h >= 2:
                    out_high(h // 2 - 1)
                    mod_row(7 + h // 2)
                if h == 13:
                    ahead(first_slot[stage_groups["xr"][0]] + 1)
            out_high(7)
            mod_row(15)

            act.wait_ge(sem("att_out_lo"), 8)
            for j, g in enumerate(stage_groups["xr"]):
                ps = group(g)
                act.copy(xrp[:, 2 * j:2 * j + 2, 3:3 + T], ps).then_inc(sem("act_read"), 1)
            def gates(t):
                act.wait_ge(sem("rnn_gates"), t + 1)
                act.activation(xrp[:, t, 3:3 + T], misc[:, t % 2, 0:T], ACT.Sigmoid,
                               bias=vec[:, VROW["rnn_gate_a_b"] + t:VROW["rnn_gate_a_b"] + t + 1]).then_inc(sem("rnn_r"), 1)
                act.activation(work[:, t], misc[:, t % 2, T:2 * T], ACT.Sigmoid,
                               bias=vec[:, VROW["rnn_gate_x_b"] + t:VROW["rnn_gate_x_b"] + t + 1]).then_inc(sem("rnn_i"), 1)

            for j, g in enumerate(stage_groups["yr"]):
                ps = group(g)
                act.activation(yg[:, 2 * j:2 * j + 2, :], ps, ACT.Gelu_apprx_tanh).then_inc(sem("act_read"), 1)
                if j >= 1:
                    gates(2 * j - 2)
                    gates(2 * j - 1)
            gates(DC - 2)
            gates(DC - 1)
            act.wait_ge(sem("rnn_r"), DC)
            act.wait_ge(sem("rnn_ix"), DC)
            for u in range(DC):
                act.activation(wmul[u // 4][:, u % 4], xrp[:, u, 3:3 + T], ACT.Tanh, scale=coef[:, u:u + 1]).then_inc(sem("rnn_tanh"), 1)
            mod_row(16)
            for u in range(DC):
                act.wait_ge(sem("rnn_tanh"), u + 1)
                act.activation(xrp[:, u, 3:3 + T], xrp[:, u, 3:3 + T], ACT.Exp, scale=coef[:, u:u + 1])\
                    .then_inc(sem("rnn_a"), 1)
            for half in range(2):
                mod_row(17 + half)
                act.wait_ge(sem("rnn_w"), 4 * (half + 1))
                act.activation(wmul[half], wmul[half], ACT.Sqrt, scale=-1.0, bias=consts[:, 1:2]).then_inc(sem("rnn_mult"), 1)
            for half in range(2):
                mod_row(19 + half)
                act.wait_ge(sem("rnn_ob"), half + 1)
                act.copy(oph[:, 4 + 4 * half:8 + 4 * half, :], work[:, 4 * half:4 * half + 4, :]).then_inc(sem("rnn_ob_hi"), 1)
            mod_row(21)
            ahead(first_slot[stage_groups["g"][0]] + 1)
            mod_row(22)
            mod_row(23)
            ahead(first_slot[stage_groups["g"][0]] + 2)
            act.wait_ge(sem("rnn_ob_lo"), 2)
            gi = iter(stage_groups["g"])
            for j in range(4):
                for b in range(3):
                    ps = group(next(gi))
                    if j >= 2:
                        act.wait_ge(sem("merged_f"), j - 1)
                    act.activation(g_sig[:, j % 2, 2 * b:2 * b + 2, :], ps, ACT.Sigmoid).then_inc(sem("act_read"), 1)
                gb_ = stage_groups["branch_b"][j]
                ahead(first_slot[gb_] + 2)
                act.wait_ge(sem("merged_f"), j + 1)
                act.copy(oph[:, 16 + 2 * j:18 + 2 * j, :], mrg[:, j % 2]).then_inc(sem("merged_hi"), 1)
            norm("ffn", xT, "w_out", shift=24)
            ups = stage_groups["up"]
            fw, fb = VROW["ffn_conv_w"], VROW["ffn_conv_b"]
            for j in range(FC + 2):
                if j < FC:
                    ps = group(ups[j])
                    if j >= 3:
                        act.wait_ge(sem("u_ready"), j - 2)
                    for m in range(2):
                        act.activation(acc[:, j % 3, m], ps[:, m], ACT.Identity,
                                       scale=vec[:, fw + 88 + 22 * m + j:fw + 89 + 22 * m + j],
                                       bias=vec[:, fb + 22 * m + j:fb + 22 * m + j + 1]).then_inc(sem("up_tap2"), 1)
                if 1 <= j <= FC:
                    act.wait_ge(sem("dve_read"), reads_at[ups[j - 1]])
                    act.activation(sg[:, (j - 1) % 3], acc[:, (j - 1) % 3, 0], ACT.Silu).then_inc(sem("up_silu"), 1)
                if j >= 2:
                    act.wait_ge(sem("u_ready"), j - 1)
                    act.copy(oph[:, j - 2], uf[:, (j - 2) % 3]).then_inc(sem("u_hi"), 1)
            for l in range(2):
                norm(f"mix{l}", xT, ("down", "down2")[l])
                for t, g in enumerate(stage_groups[f"mixa{l}"]):
                    ps = group(g)
                    if t == 2:
                        act.wait_ge(sem("dve_read"), reads_at[stage_groups[f"mixa{l}"][0]])
                    act.activation(sgm[:, t % 2], ps[:, 1], ACT.Sigmoid).then_inc(sem("ya_sig"), 1)
                act.wait_ge(sem("mem_landed"), 16 * (l + 1))
                for i in range(TB):
                    act.activation(m_sq[:, i], m_tok[:, i], ACT.Square, accum_out=tiny[:, 0, i:i + 1]).then_inc(sem("mem_sq"), 1)
                act.wait_ge(sem("mem_sq"), 2 * (l + 1))
                act.activation(tiny[:, 1, 0:2], tiny[:, 0, 0:2], ACT.Sqrt, bias=consts[:, 0:1], scale=1.0 / D)\
                    .then_inc(sem("mem_rt"), 1)
                ps = group(stage_groups[f"mix_bg{l}"][0])
                act.copy(y8[:, 3:5, :], ps).then_inc(sem("act_read"), 1)
                ps = group(stage_groups[f"mix_bgcg{l}"][0])
                act.copy(y8[0:64, 5, :], ps[0:64, 0]).then_inc(sem("mix_bg2"), 1)
                act.copy(cg[:, 2, :], ps[:, 1]).then_inc(sem("act_read"), 1)
                ps = group(stage_groups[f"mix_cg{l}"][0])
                act.copy(cg[:, 0:2, :], ps).then_inc(sem("act_read"), 1)
                mg = VROW["norm_mem_g_2"] + DC * l
                for c in range(DC):
                    act.wait_ge(sem("mem_turned"), 4 * l + c // 2 + 1)
                    act.activation(oph[:, c], misc[:, c // 2, (c % 2) * T:(c % 2 + 1) * T], ACT.Copy,
                                   scale=vec[:, mg + c:mg + c + 1]).then_inc(sem("mem_hi"), 1)
                ahead(first_slot[stage_groups[f"mix_bin{l}"][0]] + 2)
                ps = group(stage_groups[f"mix_binuv{l}"][0])
                act.activation(y8[64:128, 5, :], ps[64:128, 0], ACT.Gelu_apprx_tanh)
                act.activation(vb[:, 2], ps[:, 1], ACT.Gelu_apprx_tanh).then_inc(sem("mix_v2"), 1)
                ps = group(stage_groups[f"mix_u{l}"][0])
                act.activation(y8[:, 6:8, :], ps, ACT.Gelu_apprx_tanh).then_inc(sem("act_read"), 1)
                ps = group(stage_groups[f"mix_v{l}"][0])
                act.activation(vb[:, 0:2], ps, ACT.Gelu_apprx_tanh).then_inc(sem("act_read"), 1)

                def keys(j):
                    ps = group(stage_groups[f"xk{l}"][j])
                    act.copy(keys_at[0][:, 2 * j:2 * j + 2, :], ps).then_inc(sem("kvq_hi"), 1)

                def values(j):
                    ps = group(stage_groups[f"xv{l}"][j])
                    act.copy(values_at[0][:, :, j * 256:(j + 1) * 256], ps).then_inc(sem("kvq_hi"), 1)

                act.wait_ge(sem("centred"), 6 * l + 3)
                act.activation(sq3, vb, ACT.Square).then_inc(sem("mix_sq"), 1)
                keys(0)
                act.wait_ge(sem("squares_summed"), SUMS.index(f"v{l}") + 1)
                act.activation(rt[:], misc[:, 1, 0:T], ACT.Sqrt, bias=consts[:, 0:1], scale=1.0 / 320).then_inc(sem("root_ready"), 1)
                keys(1)
                for i in range(TB):
                    act.wait_ge(sem("v_turned"), 2 * l + i + 1)
                    act.copy(vtok[:, i, :], misc[:, 2 + i, 0:384]).then_inc(sem("spatial_ready"), 1)
                keys(2)
                act.wait_ge(sem("ws_turned"), l + 1)
                act.copy(wst[:, 0:4, :], misc[:, 0, :].rearrange("p (g j) -> p g j", g=4)).then_inc(sem("spatial_ready"), 1)
                act.copy(wst[:, 4, :], misc[:, 1, 0:P]).then_inc(sem("spatial_ready"), 1)
                keys(3)
                act.wait_ge(sem("centred"), 6 * l + 6)
                act.activation(sq3, y8[:, 0:3, :], ACT.Square).then_inc(sem("mix_sq"), 1)
                values(0)
                act.wait_ge(sem("squares_summed"), SUMS.index(f"a{l}") + 1)
                act.activation(rt[:], misc[:, 1, 0:T], ACT.Sqrt, bias=consts[:, 0:1], scale=1.0 / 384).then_inc(sem("root_ready"), 1)
                la = VROW["ln_a_b_2"] + 3 * l
                for t in range(3):
                    act.wait_ge(sem("a_scaled"), 3 * l + t + 1)
                    act.activation(y8[:, t], y8[:, t], ACT.Silu, bias=vec[:, la + t:la + t + 1]).then_inc(sem("a_done"), 1)
                act.wait_ge(sem("a_done"), 3 * (l + 1))
                act.wait_ge(sem("c_done"), 3 * (l + 1))
                act.wait_ge(sem("b_done"), 3 * (l + 1))
                act.activation(work[:], y8, ACT.Square).then_inc(sem("mix_sq"), 1)
                values(1)
                act.wait_ge(sem("squares_summed"), SUMS.index(f"y{l}") + 1)
                act.activation(rt[:], misc[:, 0, 0:T], ACT.Sqrt, bias=consts[:, 0:1], scale=1.0 / 64)\
                    .then_inc(sem("root_ready"), 1)
                values(2)
                for c in range(DC):
                    act.wait_ge(sem("y_scaled"), DC * l + c + 1)
                    act.copy(hh[:, c], work[:, c]).then_inc(sem("y_hi"), 1)
                values(3)
                norm(f"x{l}", xT, f"mixout{l}")
                for j, g in enumerate(stage_groups[f"xq{l}"]):
                    ps = group(g)
                    act.copy(queries[0][:, 2 * j:2 * j + 2, :], ps).then_inc(sem("kvq_hi"), 1)
                ahead(first_slot[stage_groups[f"xo{l}"][0]] + 2)
                def xexp(h):
                    b = h % 2
                    act.wait_ge(sem("x_negmax"), 4 * l + h + 1)
                    if h >= 2:
                        act.wait_ge(sem("x_pt"), 4 * l + h - 1)
                    for i in range(TB):
                        act.activation(xp[:, b, i], misc[:, b, i * T:(i + 1) * T], ACT.Exp, bias=small[:, b, 2 + i:3 + i],
                                       scale=1.0 / 16, accum_out=small[:, b, 4 + i:5 + i]).then_inc(sem("x_exp"), 1)

                def x_out(h):
                    act.wait_ge(sem("x_o"), 4 * l + h + 1)
                    act.copy(hh[:, 2 * h:2 * h + 2, :], x_bank(l, h).rearrange("p (a b) -> p a b", a=2)).then_inc(sem("xo_hi"), 1)

                xexp(0)
                for h in range(4):
                    if h + 1 < 4:
                        xexp(h + 1)
                    b = h % 2
                    act.wait_ge(sem("x_pt"), 4 * l + h + 1)
                    act.copy(queries[0][:, 2 * h:2 * h + 2, :], misc[:, 2 + h % 2, :].rearrange("p (a b) -> p a b", a=2))\
                        .then_inc(sem("x_pt_sb"), 1)
                    if h >= 1:
                        x_out(h - 1)
                x_out(3)
                norm(f"ffn{l}", xT, f"xo{l}")
                if l == 0:
                    ups2 = stage_groups["up2"]
                    for j in range(FC + 1):
                        if j < FC:
                            ps = group(ups2[j])
                            if j >= 3:
                                act.wait_ge(sem("dve_read"), reads_at[ups2[j - 3]])
                            act.activation(sg[:, j % 3], ps[:, 0], ACT.Silu).then_inc(sem("up2_silu"), 1)
                        if j >= 1:
                            act.wait_ge(sem("dve_read"), reads_at[ups2[j - 1]])
                            act.copy(oph[:, j - 1], uf[:, (j - 1) % 3]).then_inc(sem("u2_hi"), 1)
            ahead(n_dense - 1)
            for q in range(4):
                if q == 2:
                    act.wait_ge(sem("top_gap"), 1)
                    act.activation(topw[:, :, 1], topw[:, :, 0], ACT.Exp).then_inc(sem("top_exp"), 1)
                act.wait_ge(sem("hn_turned"), q + 1)
                act.copy(hn_tok[:, q // 2, (q % 2) * 512:(q % 2 + 1) * 512], banks[:, q, :]).then_inc(sem("hn_tok"), 1)

            def moe_hi(E, k):
                r, q = (n_dense + k) % RAW, (n_split + k) % SPLIT
                act.wait_ge(sem(f"landed{r}"), E * (16 * JE) + (total[r] + 16 * (k // RAW + 1)))
                act.wait_ge(sem("slot_used"), E * MOE_SLOTS + (n_split + k - SPLIT + 1))
                act.copy(whi[:, q, :], raw[:, r, :]).then_inc(sem("hi_ready"), 1)

            def moe_expert(e, u, p):
                E, Q = e + NE * p, e + (NE + 1) * p
                st["k"] = 2

                def upto(k):
                    while st["k"] <= k:
                        moe_hi(E, st["k"])
                        st["k"] += 1

                def hidden_hi(j):
                    act.wait_ge(sem("m_hT"), E * JE + (j + 1))
                    act.copy(h_hi[j % 2], misc[:, 1 if j == JE - 1 else 0, :]).then_inc(sem("m_hhi"), 1)

                for j in range(JE):
                    upto(gate_last(j) + 2)
                    act.wait_ge(sem("slot_used"), E * MOE_SLOTS + (n_split + gate_last(j) + 1))
                    act.activation(sil[:, j % 2], pair[:, j % 2, 0, :], ACT.Silu).then_inc(sem("m_sil"), 1)
                    if j >= 1:
                        hidden_hi(j - 1)
                    if j == 4:
                        act.wait_ge(sem("m_ct"), E + 1)
                        act.copy(comb_t[:, u], misc[:, 1, 0:T]).then_inc(sem("m_c"), 1)
                upto(MOE_SLOTS - 1)
                for half in range(2):
                    act.wait_ge(sem("m_x"), Q * 2 + (3 + half))
                    act.copy(xg_hi[1 - u][:, half * 512:(half + 1) * 512], misc[:, 1 - half, :]).then_inc(sem("m_xhi"), 1)
                hidden_hi(JE - 1)
                upto(MOE_SLOTS + 1)
                act.wait_ge(sem("slot_used"), E * MOE_SLOTS + (n_split + MOE_SLOTS))
                act.copy(ye, misc[:, 2:4, :].rearrange("p a b -> p (a b)")).then_inc(sem("m_yc"), 1)

            def moe_pass(p):
                for half in range(2):
                    act.wait_ge(sem("m_x"), 2 * (NE + 1) * p + half + 1)
                    act.copy(xg_hi[0][:, half * 512:(half + 1) * 512], misc[:, 1 - half, :]).then_inc(sem("m_xhi"), 1)
                with act.Fori(0, NE // 2) as i:
                    for u in range(2):
                        moe_expert(2 * i + u, u, p)

            moe_hi(0, 0)
            moe_hi(0, 1)
            moe_pass(0)
            act.wait_ge(sem("overflow_known"), 1)
            over = act.value_load(flag[0:1, 0:1], min_val=0, max_val=1)
            with act.If(over > 0):
                moe_pass(1)
            act.wait_ge(sem("moe_added"), 1)
            for c in range(0, DC, 4):
                act.activation(work[:, c:c + 4, :], xT[:, c:c + 4, :], ACT.Square).then_inc(sem("fin_act"), 1)
            act.wait_ge(sem("fin_pe"), 1)
            act.activation(rt[:], misc[:, 0, 0:T], ACT.Sqrt, bias=consts[:, 0:1], scale=1.0 / D).then_inc(sem("fin_act"), 1)
            for i in range(TB):
                for b in range(2):
                    act.wait_ge(sem("fin_pe"), 1 + 2 * i + b + 1)
                    act.copy(hn_tok[:, i, b * 512:(b + 1) * 512], banks[:, 2 * i + b, :]).then_inc(sem("fin_act"), 1)
                act.wait_ge(sem("fin_act"), 3 + 2 * i + 2)
                act.dma_start(out[0].rearrange("(i p) d -> p i d", p=P)[:, i, :], hn_tok[:, i, :])\
                    .then_inc(sem("out_written"), 16)

        @block.tensor
        def _(pe):
            def three(out_, w_hi, w_lo, x_hi, x_lo, start, stop, weights_move=False):
                for i, (a, b) in enumerate(((w_hi, x_hi), (w_hi, x_lo), (w_lo, x_hi))):
                    lhs, rhs = (b, a) if weights_move else (a, b)
                    ins = pe.matmul(out_, lhs, rhs, start=start and i == 0, stop=stop and i == 2)
                return ins

            def free_pair(g):
                q = pair_seq[g]
                if q >= PAIRS:
                    before = order[q - PAIRS]
                    pe.wait_ge(sem(f"{groups[before][2]}_read"), reads_at[before])

            def dense_group(g, xh, xl, weights_move=False, width=256, chunk0=0, each_chunk=None):
                free_pair(g)
                q = pair_seq[g] % PAIRS
                slots = groups[g][1]
                done = 0
                for k, (_, nch) in enumerate(slots):
                    n = first_slot[g] + k
                    i = split_no[n]
                    pe.wait_ge(sem("lo_ready"), i + 1)
                    for m in range(2):
                        for c in range(nch):
                            x = chunk0 + done + c
                            if each_chunk is not None and m == 0:
                                pe.wait_ge(*each_chunk(x))
                            wh, wl = whi[:, i % SPLIT, c * 256:(c + 1) * 256], wlo[:, i % SPLIT, c * 256:(c + 1) * 256]
                            start, stop = done + c == 0, k == len(slots) - 1 and c == nch - 1
                            if weights_move:
                                tok = slice(m * P, (m + 1) * P)
                                ins = three(pair[:, q, m, 0:width], wh[:, 0:width], wl[:, 0:width], xh[:, x, tok],
                                            xl[:, x, tok], start, stop, True)
                            else:
                                col = slice(m * P, (m + 1) * P)
                                ins = three(pair[:, q, m, 0:T], wh[:, col], wl[:, col], xh[:, x], xl[:, x], start, stop)
                    ins.then_inc(sem("slot_used"), 1)
                    done += nch

            def mod_columns(j):
                pe.wait_ge(sem("mod_row"), j + 1)
                for m in range(2):
                    ins = pe.matmul(misc[:, 3, 2 * j + m:2 * j + m + 1], mrow(j)[:, m * P:(m + 1) * P], ones[0:1, 0:1],
                                    start=True, stop=True)
                ins.then_inc(sem("mod_columns"), 1)

            def mod_slot(j, lag):
                mod_half(j, 0, lag)
                mod_half(j, 1, lag)

            def mod_half(j, half, lag):
                n = mod_slots[j]
                if half == 0:
                    pe.wait_ge(sem(f"landed{n % RAW}"), landed_at[n])
                    if lag:
                        mod_columns(j - lag)
                for c in range(4 * half, 4 * half + 4):
                    ins = pe.matmul(banks[0:1, 2 + j % 2, 0:T], cact[:, c:c + 1], raw[:, n % RAW, c * 256:(c + 1) * 256],
                                    start=(c == 0), stop=(c == DC - 1))
                if half:
                    ins.then_inc(sem("plain_used"), 1)

            def sums(k, j, squares=work):
                pe.wait_ge(sem("sq_ready"), 4 * k + j + 1)
                for c in (2 * j, 2 * j + 1):
                    ins = pe.matmul(misc[:, 0, 0:T], ones[:], squares[:, c], start=(c == 0), stop=(c == DC - 1))
                if j == 3:
                    ins.then_inc(sem("squares_summed"), 1)

            def into_norm(stage, name, xh, xl, **how):
                each = how.pop("each_chunk", None)
                for j, g in enumerate(stage_groups[stage]):
                    dense_group(g, xh, xl, each_chunk=each if j == 0 else None, **how)
                    if j >= 1:
                        sums(NORM[name], j - 1)
                sums(NORM[name], 3)

            def h_chunk(k):
                return lambda c: (sem("h_lo"), DC * k + c + 1)

            pe.wait_ge(sem("consts_ready"), 1)
            pe.wait_ge(sem("c_ready"), 1)
            pe.wait_ge(sem("x_landed"), 16)
            for j in range(8):
                mod_slot(j, 2 if j >= 2 else 0)
                if j < 4:
                    if j >= 2:
                        pe.wait_ge(sem("x_copied"), j - 1)
                    for c in (2 * j, 2 * j + 1):
                        for i in range(TB):
                            ins = pe.transpose(banks[:, j % 2, (c % 2) * T + i * P:(c % 2) * T + (i + 1) * P],
                                               x_tok[:, i, c * P:(c + 1) * P], ident[:])
                    ins.then_inc(sem("x_turned"), 1)
                if 1 <= j <= 4:
                    sums(0, j - 1, start_sq)
                if j == 6:
                    pe.wait_ge(sem("vec_landed"), 16 * N_VEC_DMAS)
                    pe.wait_ge(sem("root_ready"), 1)
                    for v in range(NV):
                        pe.transpose(misc[:, v // 4, (v % 4) * P:(v % 4 + 1) * P], stage_rows[:, v, :], ident[:])\
                            .then_inc(sem("pe_start"), 1)
                    pe.wait_ge(sem("table_landed"), 48)
                    pe.matmul(misc[0:NHEAD, 2, 0:T], relb, oh, start=True, stop=True).then_inc(sem("pe_start"), 1)
            mod_columns(6)
            mod_columns(7)
            qk_groups = stage_groups["qa"] + stage_groups["ka"] + stage_groups["qc"] + stage_groups["kc"]

            def qk_squares(i):
                pe.wait_ge(sem("qk_sq"), i + 1)
                for m in range(2):
                    t = 2 * i + m
                    ins = pe.matmul(misc[:, 0, 0:T], hsel[:, 32 - 2 * t:160 - 2 * t], qk_sq[:, i % 2, m],
                                    start=(t == 0), stop=(t == 13))
                ins.then_inc(sem("qk_ss"), 1)

            for i, g in enumerate(qk_groups):
                dense_group(g, hh, hl, each_chunk=h_chunk(0) if i == 0 else None)
                if i >= 1:
                    qk_squares(i - 1)
            dense_group(stage_groups["va"][0], hh, hl, weights_move=True, width=P)
            qk_squares(6)
            def spread_roots(tiles):
                for t in tiles:
                    if t % 2 == 0 and t >= 8:
                        pe.wait_ge(sem("qk_normed"), t - 6)
                    rows = slice(32 * (t // 4), 32 * (t // 4) + 32)
                    ins = pe.matmul(misc[:, (t // 2) % 4, (t % 2) * T:(t % 2 + 1) * T], spread[rows, (t % 4) * P:(t % 4 + 1) * P],
                                    rt[rows, :], start=True, stop=True)
                    if t % 2:
                        ins.then_inc(sem("qk_spread"), 1)

            dense_group(stage_groups["vc"][0], hh, hl, weights_move=True)
            pe.wait_ge(sem("qk_rs"), 1)
            spread_roots(range(8))
            dense_group(stage_groups["vc"][1], hh, hl, weights_move=True)
            spread_roots(range(8, 14))

            def operands(h):
                half = slice(64 * (h % 2), 64 * (h % 2) + 64)
                if h < 8:
                    return qa[half, h // 2], ka[half, h // 4], va[:, :, 64 * (h // 4):64 * (h // 4) + 64]
                h -= 8
                return qc[half, h // 2], kc[half, h // 2], vc[:, :, 64 * h:64 * h + 64]

            def scores(h):
                q, k, _ = operands(h)
                if h >= 2:
                    pe.wait_ge(sem("att_exp"), exps(h - 2))
                pe.wait_ge(sem(f"bias_landed{h % 2}"), 16 * (h // 2 + 1))
                for i, (qb, kb) in enumerate(((0, 0), (1, 0), (1, 1))):
                    s = misc[:, h % 2, i * P:(i + 1) * P]
                    pe.matmul(s, q[:, qb * P:(qb + 1) * P], k[:, kb * P:(kb + 1) * P], start=True, stop=False)
                    ins = pe.matmul(s, flip, bias_buf[h % 2][:, 1 - (qb - kb), :], start=False, stop=True)
                ins.then_inc(sem("att_scores"), 1)

            pe.wait_ge(sem("qk_normed"), 14)
            pe.wait_ge(sem("flip_ready"), 1)
            pe.wait_ge(sem("act_read"), reads_at[stage_groups["vc"][1]])
            scores(0)
            scores(1)
            for h in range(NHEAD):
                pe.wait_ge(sem("att_p"), 2 * (h + 1))
                if h >= 1:
                    pe.wait_ge(sem("att_pt_sb"), h)
                for i in range(3):
                    ins = pe.transpose(misc[:, 2, i * P:(i + 1) * P], s_buf[h % 2][:, i * P:(i + 1) * P], ident[:])
                ins.then_inc(sem("att_pt"), 1)
                if h + 2 < NHEAD:
                    scores(h + 2)
                mod_half(8 + h // 2, h % 2, 2 if h >= 4 else 0)
                pe.wait_ge(sem("att_pt_sb"), h + 1)
                i = h // 2
                if h % 2 == 0 and i >= 2:
                    pe.wait_ge(sem("att_out_lo"), i - 1)
                _, _, v = operands(h)
                half = slice(64 * (h % 2), 64 * (h % 2) + 64)
                pe.matmul(banks[half, i % 2, 0:T], v[:, 0], pt_buf[h % 2][:, 0:T], start=True, stop=False)
                pe.matmul(banks[half, i % 2, P:T], v[:, 1], pt_buf[h % 2][:, T:384], start=False, stop=True)\
                    .then_inc(sem("att_o"), 1)

            mod_columns(14)
            mod_columns(15)
            pe.wait_ge(sem("att_out_lo"), 8)
            def gates(t):
                pe.wait_ge(sem("rnn_xc"), t + 1)
                if t >= 2:
                    pe.wait_ge(sem("rnn_i"), t - 1)
                for k in range(2):
                    for half in range(2):
                        p = slice(64 * half, 64 * half + 64)
                        ins = pe.matmul(misc[p, t % 2, k * T:(k + 1) * T], gw[p, k, t, :], xc[p, t % 2], start=True, stop=True)
                ins.then_inc(sem("rnn_gates"), 1)

            for g in stage_groups["xr"]:
                dense_group(g, hh, hl)
            pe.wait_ge(sem("gate_w_landed"), 64)
            for j, g in enumerate(stage_groups["yr"]):
                dense_group(g, hh, hl)
                if j >= 1:
                    gates(2 * j - 2)
                    gates(2 * j - 1)
            gates(DC - 2)
            gates(DC - 1)
            pe.wait_ge(sem("act_read"), reads_at[stage_groups["yr"][-1]])
            for j in range(16, 24):
                mod_slot(j, 1 if j > 16 else 0)
            mod_columns(23)
            pe.wait_ge(sem("rnn_ob_lo"), 2)
            gi = iter(stage_groups["g"])
            for j in range(4):
                for b in range(3):
                    dense_group(next(gi), hh, hl)
                g = stage_groups["branch_ac"][j]
                free_pair(g)
                n, q = split_no[first_slot[g]], pair_seq[g] % PAIRS
                pe.wait_ge(sem("lo_ready"), n + 1)
                for m in range(2):
                    for c in range(DC):
                        x, at = (c, 0) if c < 4 else (8 + c, T)
                        col = slice(c * 256 + m * P, c * 256 + (m + 1) * P)
                        ins = three(pair[:, q, m, at:at + T], whi[:, n % SPLIT, col], wlo[:, n % SPLIT, col],
                                    oph[:, x], opl[:, x], c % 4 == 0, c % 4 == 3)
                ins.then_inc(sem("slot_used"), 1)
                dense_group(stage_groups["branch_b"][j], oph, opl, chunk0=4)
            pe.wait_ge(sem("merged_lo"), 4)
            into_norm("w_out", "ffn", oph, opl, chunk0=16)
            for i, g in enumerate(stage_groups["up"]):
                dense_group(g, hh, hl, each_chunk=h_chunk(1) if i == 0 else None)
            into_norm("down", "mix0", oph, opl, each_chunk=lambda c: (sem("u_lo"), c + 1))

            for l in range(2):
                k0 = NORM[f"mix{l}"]
                first = True
                for stage in ("mixa", "mix_bg", "mix_bgcg", "mix_cg", "mix_bin", "mix_binuv", "mix_u", "mix_v"):
                    for g in stage_groups[f"{stage}{l}"]:
                        dense_group(g, hh, hl, each_chunk=h_chunk(k0) if first else None)
                        first = False
                    if stage == "mix_bgcg":
                        pe.wait_ge(sem("mem_scaled"), 2 * (l + 1))
                        for c in range(DC):
                            for i in range(TB):
                                ins = pe.transpose(misc[:, c // 2, (c % 2) * T + i * P:(c % 2) * T + (i + 1) * P],
                                                   m_tok[:, i, c * P:(c + 1) * P], ident[:])
                            if c % 2:
                                ins.then_inc(sem("mem_turned"), 1)

                def keys(j):
                    dense_group(stage_groups[f"xk{l}"][j], oph, opl)

                def values(j):
                    dense_group(stage_groups[f"xv{l}"][j], oph, opl, weights_move=True)

                pe.wait_ge(sem("mem_lo"), DC * (l + 1))
                pe.wait_ge(sem("act_read"), reads_at[stage_groups[f"mix_v{l}"][0]])

                def over_v(src, bank, name):
                    pe.matmul(misc[:, bank, 0:T], ones[64:128, :], src[64:128, 0], start=True, stop=False)
                    pe.matmul(misc[:, bank, 0:T], ones[:], src[:, 1], start=False, stop=False)
                    pe.matmul(misc[:, bank, 0:T], ones[:], src[:, 2], start=False, stop=True).then_inc(sem(name), 1)

                over_v(vb, 0, "means_summed")
                keys(0)
                pe.wait_ge(sem("mix_sq"), 3 * l + 1)
                over_v(sq3, 1, "squares_summed")
                keys(1)
                pe.wait_ge(sem("mix_v_normed"), 3 * (l + 1))
                for i in range(TB):
                    for t in range(3):
                        ins = pe.transpose(misc[:, 2 + i, t * P:(t + 1) * P], vb[:, t, i * P:(i + 1) * P], ident[:])
                    ins.then_inc(sem("v_turned"), 1)
                keys(2)
                pe.wait_ge(sem("ws_masked"), l + 1)
                for g in range(5):
                    dst = misc[:, 0, g * P:(g + 1) * P] if g < 4 else misc[:, 1, 0:P]
                    ins = pe.transpose(dst, wsl[:, g, :], ident[:])
                ins.then_inc(sem("ws_turned"), 1)
                pe.wait_ge(sem("spatial_ready"), 4 * (l + 1))
                for g in range(5):
                    k, p = (g + 1) // 2, 64 * ((g + 1) % 2)
                    for i in range(TB):
                        at = (k % 2) * T + i * P
                        ins = pe.matmul(misc[p:p + 64, 2 + k // 2, at:at + P], vtok[:, i, 64 + 64 * g:128 + 64 * g],
                                        wst[:, g, :], start=True, stop=True)
                ins.then_inc(sem("c_mixed"), 1)
                keys(3)
                pe.wait_ge(sem("conv_taps"), 93 * (l + 1))
                for t in range(3):
                    ins = pe.matmul(misc[:, 0, 0:T], ones[:], y8[:, t], start=(t == 0), stop=(t == 2))
                ins.then_inc(sem("means_summed"), 1)
                values(0)
                pe.wait_ge(sem("mix_sq"), 3 * l + 2)
                for t in range(3):
                    ins = pe.matmul(misc[:, 1, 0:T], ones[:], sq3[:, t], start=(t == 0), stop=(t == 2))
                ins.then_inc(sem("squares_summed"), 1)
                values(1)
                pe.wait_ge(sem("mix_sq"), 3 * l + 3)
                for c in range(DC):
                    ins = pe.matmul(misc[:, 0, 0:T], hsel[:, 32 - 2 * c:160 - 2 * c], work[:, c],
                                    start=(c == 0), stop=(c == DC - 1))
                ins.then_inc(sem("squares_summed"), 1)
                values(2)
                pe.wait_ge(sem("y_rs"), l + 1)
                for c in range(DC):
                    rows = slice(32 * (c // 4), 32 * (c // 4) + 32)
                    ins = pe.matmul(misc[:, c // 2, (c % 2) * T:(c % 2 + 1) * T], spread[rows, (c % 4) * P:(c % 4 + 1) * P],
                                    rt[rows, :], start=True, stop=True)
                    if c % 2:
                        ins.then_inc(sem("y_spread"), 1)
                values(3)
                into_norm(f"mixout{l}", f"x{l}", hh, hl, each_chunk=lambda c: (sem("y_lo"), DC * l + c + 1))
                k1 = NORM[f"x{l}"]
                for i, g in enumerate(stage_groups[f"xq{l}"]):
                    dense_group(g, hh, hl, each_chunk=h_chunk(k1) if i == 0 else None)

                def x_scores(h):
                    if h >= 2:
                        pe.wait_ge(sem("x_exp"), 2 * (4 * l + h - 1))
                    for i in range(TB):
                        for c in range(2):
                            q_hi, q_lo = [q[:, 2 * h + c, i * P:(i + 1) * P] for q in queries]
                            k_hi, k_lo = [k[:, 2 * h + c, :] for k in keys_at]
                            ins = three(misc[:, h % 2, i * T:(i + 1) * T], q_hi, q_lo, k_hi, k_lo, c == 0, c == 1)
                    ins.then_inc(sem("x_scores"), 1)

                pe.wait_ge(sem("dve_read"), reads_at[stage_groups[f"xq{l}"][-1]])
                x_scores(0)
                x_scores(1)
                for h in range(4):
                    b = h % 2
                    pe.wait_ge(sem("x_p"), 2 * (4 * l + h + 1))
                    if h >= 2:
                        pe.wait_ge(sem("x_pt_lo"), 4 * l + h - 1)
                    for mc in range(2):
                        for i in range(TB):
                            at = mc * T + i * P
                            ins = pe.transpose(misc[:, 2 + h % 2, at:at + P], xp[:, b, i, mc * P:(mc + 1) * P], ident[:])
                    ins.then_inc(sem("x_pt"), 1)
                    if h + 2 < 4:
                        x_scores(h + 2)
                    pe.wait_ge(sem("x_pt_lo"), 4 * l + h + 1)
                    if h >= 2:
                        pe.wait_ge(sem("xo_lo"), 4 * l + h - 1)
                    for dt in range(2):
                        for mc in range(2):
                            v_hi, v_lo = [v[:, mc, h * T + dt * P:h * T + (dt + 1) * P] for v in values_at]
                            p_hi, p_lo = [p[:, 2 * h + mc, :] for p in queries]
                            ins = three(x_bank(l, h)[:, dt * T:(dt + 1) * T], v_hi, v_lo, p_hi, p_lo, mc == 0, mc == 1)
                    ins.then_inc(sem("x_o"), 1)
                into_norm(f"xo{l}", f"ffn{l}", hh, hl, each_chunk=lambda c: (sem("xo_lo"), 4 * l + c // 2 + 1))
                if l == 0:
                    for i, g in enumerate(stage_groups["up2"]):
                        dense_group(g, hh, hl, each_chunk=h_chunk(NORM["ffn0"]) if i == 0 else None)
                    into_norm("down2", "mix1", oph, opl, each_chunk=lambda c: (sem("u2_lo"), c + 1))

            pe.wait_ge(sem("router_landed"), 16)
            pe.wait_ge(sem("h_scaled"), DC * (NORM["ffn1"] + 1))
            for i in range(TB):
                for c in range(DC):
                    ins = pe.matmul(misc[:, 1, i * NE:(i + 1) * NE], work[:, c, i * P:(i + 1) * P], rw[:, c, :],
                                    start=(c == 0), stop=(c == DC - 1))
            ins.then_inc(sem("logits_done"), 1)
            for i in range(TB):
                for c in range(DC):
                    ins = pe.transpose(banks[:, 2 * i + c // 4, (c % 4) * P:(c % 4 + 1) * P], work[:, c, i * P:(i + 1) * P], ident[:])
                    if c % 4 == 3:
                        ins.then_inc(sem("hn_turned"), 1)
            pe.wait_ge(sem("picked"), 1)
            pe.wait_ge(sem("moe_consts"), 2)
            sel = pick[:, 0]
            pe.matmul(misc[:, 0, 0:NE], tri, sel[:, 0], start=True, stop=True)
            pe.matmul(misc[:, 0, NE:2 * NE], tri, sel[:, 1], start=True, stop=False)
            pe.matmul(misc[:, 0, NE:2 * NE], ones[:], sel[:, 0], start=False, stop=True)
            pe.matmul(misc[:, 0, 16:16 + NE], ones[:], sel[:, 0], start=True, stop=False)
            pe.matmul(misc[:, 0, 16:16 + NE], ones[:], sel[:, 1], start=False, stop=True).then_inc(sem("ranked"), 1)
            pe.wait_ge(sem("hn_tok"), 4)

            def gather(Q):
                pe.wait_ge(sem("m_gt"), Q + 1)
                for half in range(2):
                    for c in range(4):
                        f = (4 * half + c) * P
                        for i in range(TB):
                            ins = pe.matmul(misc[:, 1 - half, c * P:(c + 1) * P], hn_tok[:, i, f:f + P], place[:, i, :],
                                            start=(i == 0), stop=(i == 1))
                    ins.then_inc(sem("m_x"), 1)

            def scatter(S, cb, E):
                pe.wait_ge(sem("m_yc"), E)
                pe.wait_ge(sem("m_c"), E)
                for r in range(4):
                    for m in range(2):
                        f = (2 * r + m) * P
                        ins = pe.matmul(banks[:, r, m * T:(m + 1) * T], ye[:, f:f + P], comb_t[:, cb], start=True, stop=True)
                    ins.then_inc(sem("m_s"), 1)

            def moe_expert(e, u, p):
                E, Q = e + NE * p, e + (NE + 1) * p

                def gate_or_up(j, kind):
                    for half in range(2):
                        k = (0 if j == 0 else 6 * j - 2) + 2 * kind + half
                        q = (n_split + k) % SPLIT
                        pe.wait_ge(sem("lo_ready"), E * MOE_SLOTS + (n_split + k + 1))
                        for c in range(4):
                            x = slice((4 * half + c) * P, (4 * half + c + 1) * P)
                            col = slice(c * 512, (c + 1) * 512)
                            ins = three(pair[:, j % 2, kind, :], whi[:, q, col], wlo[:, q, col], xg_hi[u][:, x], xg_lo[u][:, x],
                                        half == 0 and c == 0, half == 1 and c == 3, True)
                        ins.then_inc(sem("slot_used"), 1)

                def turn(j):
                    pe.wait_ge(sem("m_mul"), E * JE + (j + 3))
                    bank = 1 if j == JE - 1 else 0
                    if j == JE - 1:
                        pe.wait_ge(sem("m_xlo"), Q * 2 + 3)
                    for c in range(4):
                        ins = pe.transpose(misc[:, bank, c * P:(c + 1) * P], sh[:, j % 2, c * P:(c + 1) * P], ident[:])
                    ins.then_inc(sem("m_hT"), 1)

                def down(j):
                    pe.wait_ge(sem("m_hlo"), E * JE + (j + 1))
                    if j == 0:
                        pe.wait_ge(sem("m_yc"), E + 1)
                    for half in range(2):
                        k = (6 * j + 8 if j < JE - 1 else 6 * j + 4) + half
                        q = (n_split + k) % SPLIT
                        pe.wait_ge(sem("lo_ready"), E * MOE_SLOTS + (n_split + k + 1))
                        for c in range(2):
                            x = slice((2 * half + c) * P, (2 * half + c + 1) * P)
                            for m in range(2):
                                col = slice(c * D + m * 512, c * D + (m + 1) * 512)
                                ins = three(misc[:, 2 + m, :], whi[:, q, col], wlo[:, q, col], h_hi[j % 2][:, x], h_lo[j % 2][:, x],
                                            j == 0 and half == 0 and c == 0, j == JE - 1 and half == 1 and c == 1, True)
                        ins.then_inc(sem("slot_used"), 1)

                for j in range(JE):
                    if j == 0:
                        pe.wait_ge(sem("m_xlo"), Q * 2 + 2)
                        pe.wait_ge(sem("m_added"), Q * 4 + 4)
                        pe.wait_ge(sem("m_mul"), E * JE + 2)
                    elif j == 1:
                        pe.wait_ge(sem("m_mul"), E * JE + 1)
                    else:
                        pe.wait_ge(sem("m_mul"), E * JE + (j + 1))
                    gate_or_up(j, 0)
                    if j >= 1:
                        turn(j - 1)
                    gate_or_up(j, 1)
                    if j >= 1:
                        down(j - 1)
                    if j == 3:
                        pe.wait_ge(sem("m_gw"), E + 1)
                        for i in range(TB):
                            ins = pe.transpose(misc[:, 1, i * P:(i + 1) * P], place_w[:, i, :], ident[:])
                        ins.then_inc(sem("m_ct"), 1)
                pe.wait_ge(sem("m_c"), E + 2)
                pe.wait_ge(sem("m_hlo"), E * JE + (JE - 1))
                gather(Q + 1)
                turn(JE - 1)
                scatter(Q, 1 - u, E + 1)
                down(JE - 1)

            def moe_pass(p):
                gather((NE + 1) * p)
                with pe.Fori(0, NE // 2) as i:
                    for u in range(2):
                        moe_expert(2 * i + u, u, p)
                pe.wait_ge(sem("m_mul"), NE * (p + 1) * JE + 2)
                pe.wait_ge(sem("m_added"), 4 * ((NE + 1) * p + NE) + 4)
                scatter(0, 1, NE * (p + 1) + 1)

            moe_pass(0)
            pe.wait_ge(sem("overflow_known"), 1)
            over = pe.value_load(flag[0:1, 0:1], min_val=0, max_val=1)
            with pe.If(over > 0):
                pe.wait_ge(sem("m_added"), 4 * (NE + 1) + 4)
                moe_pass(1)
            for c in range(DC):
                if c % 4 == 0:
                    pe.wait_ge(sem("fin_act"), c // 4 + 1)
                ins = pe.matmul(misc[:, 0, 0:T], ones[:], work[:, c], start=(c == 0), stop=(c == DC - 1))
            ins.then_inc(sem("fin_pe"), 1)
            for i in range(TB):
                for c in range(DC):
                    pe.wait_ge(sem("fin_scaled"), c + 1)
                    ins = pe.transpose(banks[:, 2 * i + c // 4, (c % 4) * P:(c % 4 + 1) * P], work[:, c, i * P:(i + 1) * P], ident[:])
                    if c % 4 == 3:
                        ins.then_inc(sem("fin_pe"), 1)

        @block.vector
        def _(dve):
            st = {"lo": 0, "chain": 0}

            def link(ins):
                st["chain"] += 1
                ins.then_inc(sem("dve_chain"), 1)
                dve.wait_ge(sem("dve_chain"), st["chain"])

            def ahead(n):
                while st["lo"] <= min(n, n_dense - 1):
                    s = st["lo"]
                    st["lo"] += 1
                    if s in plain_no:
                        continue
                    i = split_no[s]
                    dve.wait_ge(sem("hi_ready"), i + 1)
                    size = size_of[s]
                    dve.tensor_tensor(wlo[:, i % SPLIT, 0:size], raw[:, s % RAW, 0:size],
                                      whi[:, i % SPLIT, 0:size].bitcast(F32), ALU.subtract).then_inc(sem("lo_ready"), 1)

            def group(g):
                last = first_slot[g] + len(groups[g][1]) - 1
                ahead(last + 2)
                dve.wait_ge(sem("slot_used"), split_no[last] + 1)
                return pair[:, pair_seq[g] % PAIRS, :, 0:T]

            def col(name, i):
                return vec[:, VROW[name] + i:VROW[name] + i + 1]

            def low(dst, src, hi, name):
                dve.tensor_tensor(dst, src, hi.bitcast(F32), ALU.subtract).then_inc(sem(name), 1)

            def norm(name, src, gains, shift=None):
                k = NORM[name]
                if name != "mix":
                    dve.wait_ge(sem("root_ready"), ROOTS.index(name) + 1)
                    link(dve.reciprocal(rt[:], rt[:]))
                for c in range(DC):
                    dve.scalar_tensor_tensor(work[:, c], src[:, c], gains(c), rt[:], ALU.mult, ALU.mult)\
                        .then_inc(sem("h_scaled"), 1)
                if name == "ffn1":
                    return
                for c in range(DC):
                    dve.wait_ge(sem("h_hi"), DC * k + c + 1)
                    if shift is None:
                        low(hl[:, c], work[:, c], hh[:, c], "h_lo")
                    else:
                        dve.scalar_tensor_tensor(hl[:, c], work[:, c], mod[:, shift + c:shift + c + 1],
                                                 hh[:, c].bitcast(F32), ALU.add, ALU.subtract).then_inc(sem("h_lo"), 1)

            def add_modulated(g, j, gate):
                ps = group(g)
                for m in range(2):
                    t = 2 * j + m
                    ins = dve.scalar_tensor_tensor(xT[:, t], ps[:, m], mod[:, gate + t:gate + t + 1], xT[:, t], ALU.mult, ALU.add)
                ins.then_inc(sem("dve_read"), 1)

            dve.memset(stage_rows, 0.0).then_inc(sem("rows_cleared"), 1)
            link(dve.memset(brow, NEG))
            dve.wait_ge(sem("root_ready"), 1)
            link(dve.reciprocal(rt[:], rt[:]))
            ahead(first_slot[stage_groups["qa"][0]] + 1)
            for v in range(NV):
                dve.wait_ge(sem("pe_start"), NV)
                k = min(P, N_VEC - v * P)
                dve.tensor_copy(vec[:, v * P:v * P + k], misc[:, v // 4, (v % 4) * P:(v % 4) * P + k])\
                    .then_inc(sem("vec_ready"), 1)
            dve.wait_ge(sem("vec_ready"), NV)
            for name in ("qnorm_a", "qnorm_c"):
                link(dve.tensor_scalar(col(name, 0), col(name, 0), HD ** -0.5, None, ALU.mult))
            dve.wait_ge(sem("pe_start"), NV + 1)
            dve.wait_ge(sem("consts_ready"), 1)
            link(dve.tensor_copy(brow[:, 0:T], misc[0:NHEAD, 2, 0:T]))
            dve.memset(brow[0:8, 0:WIN], NEG).then_inc(sem("brow_ready"), 2)
            bm = VROW["b_mod"]

            def modulation(j0, j1):
                dve.wait_ge(sem("mod_columns"), j1)
                a, b = 2 * j0, 2 * j1
                link(dve.tensor_tensor(mod[:, a:b], vec[:, bm + a:bm + b], misc[:, 3, a:b], ALU.add))

            modulation(0, 8)
            nm = VROW["norm_mix"]
            link(dve.scalar_tensor_tensor(gain[:], mod[:, 8:16], 1.0, vec[:, nm:nm + DC], ALU.add, ALU.mult))
            norm("mix", xT, lambda c: gain[:, c:c + 1], shift=0)
            ahead(first_slot[stage_groups["qa"][0]] + 2)
            dve.wait_ge(sem("act_start"), 2)
            link(dve.tensor_scalar(tiny[:, 2], tiny[:, 1], 2.0, None, ALU.add))
            link(dve.reciprocal(tiny[:, 3], tiny[:, 2]))
            link(dve.tensor_tensor(tiny[:, 4], tiny[:, 1], tiny[:, 3], ALU.mult))
            link(dve.tensor_tensor(tiny[:, 5], tiny[:, 4], tiny[:, 4], ALU.mult))
            link(dve.tensor_scalar(tiny[:, 6], tiny[:, 5], 1.0 / 19, 1.0 / 17, ALU.mult, ALU.add))
            for d in (15, 13, 11, 9, 7, 5, 3, 1):
                link(dve.tensor_tensor(tiny[:, 7], tiny[:, 6], tiny[:, 5], ALU.mult))
                link(dve.tensor_scalar(tiny[:, 6], tiny[:, 7], 1.0 / d, None, ALU.add))
            link(dve.tensor_tensor(tiny[:, 7], tiny[:, 6], tiny[:, 4], ALU.mult))
            lam = vec[:, VROW["rnn_lambda"]:VROW["rnn_lambda"] + DC]
            link(dve.tensor_scalar(tiny[:, 2], lam, -1.0, 0.0, ALU.mult, ALU.max))
            link(dve.scalar_tensor_tensor(tiny[:, 3], tiny[:, 7], 2.0, tiny[:, 2], ALU.mult, ALU.add))
            link(dve.tensor_scalar(coef[:], tiny[:, 3], -8.0, None, ALU.mult))
            for stage in ("qa", "ka", "qc", "kc", "va", "vc"):
                for g in stage_groups[stage]:
                    ahead(first_slot[g] + 2)
            dve.wait_ge(sem("root_ready"), ROOTS.index("qk") + 1)
            dve.reciprocal(rt[:], rt[:]).then_inc(sem("qk_rs"), 1)
            names = ["qnorm_a"] * 4 + ["knorm_a"] * 2 + ["qnorm_c"] * 4 + ["knorm_c"] * 4
            dve.wait_ge(sem("act_read"), reads_at[stage_groups["kc"][-1]])
            for t in range(14):
                dve.wait_ge(sem("qk_spread"), t // 2 + 1)
                dve.scalar_tensor_tensor(qk[:, t], qk[:, t], col(names[t], 0), misc[:, (t // 2) % 4, (t % 2) * T:(t % 2 + 1) * T],
                                         ALU.mult, ALU.mult).then_inc(sem("qk_normed"), 1)

            def peak(h):
                b, s = h % 2, small[:, h % 2]
                dve.wait_ge(sem("att_scores"), h + 1)
                if h >= 2:
                    dve.wait_ge(sem("att_p"), 2 * (h - 1))
                dve.tensor_reduce(s[:, 0:1], misc[:, b, 0:P], AX_X, ALU.max).then_inc(sem("att_max"), 1)
                dve.tensor_reduce(s[:, 1:2], misc[:, b, P:384], AX_X, ALU.max).then_inc(sem("att_max"), 1)
                dve.wait_ge(sem("att_max"), 2 * h + 2)
                if h < 8:
                    dve.tensor_scalar(s[:, 2:4], s[:, 0:2], sinks[:, h:h + 1], -1.0, ALU.max, ALU.mult).then_inc(sem("att_negmax"), 1)
                else:
                    dve.tensor_scalar(s[:, 2:4], s[:, 0:2], -1.0, None, ALU.mult).then_inc(sem("att_negmax"), 1)

            def normalised(h):
                b, s = h % 2, small[:, h % 2]
                dve.wait_ge(sem("att_exp"), exps(h))
                if h < 8:
                    link(dve.tensor_tensor(s[:, 4:6], s[:, 4:6], s[:, 6:8], ALU.add))
                link(dve.reciprocal(s[:, 6:8], s[:, 4:6]))
                dve.tensor_scalar(s_buf[b][:, 0:P], s_buf[b][:, 0:P], s[:, 6:7], None, ALU.mult).then_inc(sem("att_p"), 1)
                dve.tensor_scalar(s_buf[b][:, P:384], s_buf[b][:, P:384], s[:, 7:8], None, ALU.mult).then_inc(sem("att_p"), 1)

            def out_low(i):
                chunk = i if i < 4 else 8 + i
                dve.wait_ge(sem("att_out_hi"), i + 1)
                low(opl[:, chunk], banks[:, i % 2, 0:T], oph[:, chunk], "att_out_lo")

            dve.wait_ge(sem("table_landed"), 48)
            peak(0)
            for h in range(NHEAD):
                if h + 1 < NHEAD:
                    peak(h + 1)
                normalised(h)
                if h % 2 == 1 and h >= 3:
                    out_low(h // 2 - 1)
                if h == 13:
                    ahead(first_slot[stage_groups["xr"][0]] + 1)
            out_low(7)
            for g in stage_groups["xr"]:
                ahead(first_slot[g] + 2)
            dve.wait_ge(sem("xr_padded"), 1)

            def gated(t):
                dve.wait_ge(sem("rnn_i"), t + 1)
                dve.tensor_tensor(work[:, t], work[:, t], xc[:, t % 2], ALU.mult).then_inc(sem("rnn_ix"), 1)

            for t in range(DC):
                x = xrp[:, t]
                if t % 2 == 0:
                    ahead(first_slot[stage_groups["yr"][t // 2]] + 2)
                    dve.wait_ge(sem("act_read"), reads_at[stage_groups["xr"][t // 2]])
                if t >= 2:
                    gated(t - 2)
                    dve.wait_ge(sem("rnn_ix"), t - 1)
                link(dve.tensor_scalar(xc[:, t % 2], x[:, 0:T], col("rnn_conv_w", t), col("rnn_conv_b", t), ALU.mult, ALU.add))
                for k in (1, 2, 3):
                    ins = dve.scalar_tensor_tensor(xc[:, t % 2], x[:, k:k + T], col("rnn_conv_w", DC * k + t), xc[:, t % 2],
                                                   ALU.mult, ALU.add)
                    if k < 3:
                        link(ins)
                ins.then_inc(sem("rnn_xc"), 1)
            gated(DC - 2)
            gated(DC - 1)
            dve.wait_ge(sem("act_read"), reads_at[stage_groups["yr"][-1]])
            for u in range(DC):
                dve.wait_ge(sem("rnn_a"), u + 1)
                w_ = wmul[u // 4][:, u % 4]
                link(dve.tensor_tensor(tmp2[:, u % 2], xrp[:, u, 3:3 + T], xrp[:, u, 3:3 + T], ALU.mult))
                dve.scalar_tensor_tensor(w_, tmp2[:, u % 2], 1.0, w_, ALU.add, ALU.mult).then_inc(sem("rnn_w"), 1)
            for half in range(2):
                q, wm = slice(4 * half, 4 * half + 4), wmul[half]
                dve.wait_ge(sem("rnn_mult"), half + 1)
                link(dve.memset(wm[:, :, 0:1], 1.0))
                link(dve.tensor_tensor(work[:, q, :], work[:, q, :], wm, ALU.mult))
                for t in range(4):
                    u = 4 * half + t
                    ins = dve.tensor_tensor_scan(wm[:, t], xrp[:, u, 3:3 + T], work[:, u], 0.0, ALU.mult, ALU.add)
                link(ins)
                dve.tensor_tensor(work[:, q, :], wm, yg[:, q, :], ALU.mult).then_inc(sem("rnn_ob"), 1)
            for half in range(2):
                q = slice(4 * half, 4 * half + 4)
                if half:
                    ahead(first_slot[stage_groups["g"][0]] + 1)
                dve.wait_ge(sem("rnn_ob_hi"), half + 1)
                low(opl[:, 4 + 4 * half:8 + 4 * half, :], work[:, q, :], oph[:, 4 + 4 * half:8 + 4 * half, :], "rnn_ob_lo")
            modulation(8, 24)
            gi = iter(stage_groups["g"])
            for j in range(4):
                for b in range(3):
                    ahead(first_slot[next(gi)] + 2)
                g = stage_groups["branch_ac"][j]
                last = first_slot[g]
                ahead(last + 2)
                dve.wait_ge(sem("slot_used"), split_no[last] + 1)
                dve.wait_ge(sem("act_read"), reads_at[stage_groups["g"][3 * j + 2]])
                ps = pair[:, pair_seq[g] % PAIRS]
                if j >= 2:
                    dve.wait_ge(sem("merged_hi"), j - 1)
                dve.tensor_tensor(mrg[:, j % 2], ps[:, :, 0:T], g_sig[:, j % 2, 0:2, :], ALU.mult).then_inc(sem("dve_chain"), 1)
                st["chain"] += 1
                dve.tensor_tensor(mrg2[:, j % 2], ps[:, :, T:2 * T], g_sig[:, j % 2, 4:6, :], ALU.mult).then_inc(sem("dve_read"), 1)
                dve.wait_ge(sem("dve_chain"), st["chain"])
                dve.wait_ge(sem("dve_read"), reads_at[g])
                link(dve.tensor_tensor(mrg[:, j % 2], mrg[:, j % 2], mrg2[:, j % 2], ALU.add))
                g = stage_groups["branch_b"][j]
                ps = group(g)
                dve.tensor_tensor(mrg2[:, j % 2], ps, g_sig[:, j % 2, 2:4, :], ALU.mult).then_inc(sem("dve_read"), 1)
                dve.wait_ge(sem("dve_read"), reads_at[g])
                dve.tensor_tensor(mrg[:, j % 2], mrg[:, j % 2], mrg2[:, j % 2], ALU.add).then_inc(sem("merged_f"), 1)
                dve.wait_ge(sem("merged_hi"), j + 1)
                low(opl[:, 16 + 2 * j:18 + 2 * j, :], mrg[:, j % 2], oph[:, 16 + 2 * j:18 + 2 * j, :], "merged_lo")
            for j, g in enumerate(stage_groups["w_out"]):
                add_modulated(g, j, 16)
            nf = VROW["norm_ffn"]
            link(dve.scalar_tensor_tensor(gain[:], mod[:, 32:40], 1.0, vec[:, nf:nf + DC], ALU.add, ALU.mult))
            norm("ffn", xT, lambda c: gain[:, c:c + 1], shift=24)
            ups = stage_groups["up"]
            for j in range(FC + 2):
                if j < FC:
                    ps = group(ups[j])
                    dve.wait_ge(sem("up_tap2"), 2 * (j + 1))
                    for k, back in ((1, 1), (0, 2)):
                        for m in range(2):
                            a = acc[:, j % 3, m]
                            last = k == 0 and m == 1
                            ins = dve.scalar_tensor_tensor(a[:, back:], ps[:, m, 0:T - back],
                                                           col("ffn_conv_w", 44 * k + 22 * m + j), a[:, back:], ALU.mult, ALU.add)
                            ins.then_inc(sem("dve_read" if last else "up_taps"), 1)
                            if k == 1 and m == 1:
                                dve.wait_ge(sem("up_taps"), 3 * j + 2)
                    dve.wait_ge(sem("dve_read"), reads_at[ups[j]])
                if 1 <= j <= FC:
                    i = j - 1
                    dve.wait_ge(sem("up_silu"), i + 1)
                    if i >= 3:
                        dve.wait_ge(sem("u_hi"), i - 2)
                    dve.tensor_tensor(uf[:, i % 3], sg[:, i % 3], acc[:, i % 3, 1], ALU.mult).then_inc(sem("u_ready"), 1)
                if j >= 2:
                    dve.wait_ge(sem("u_hi"), j - 1)
                    low(opl[:, j - 2], uf[:, (j - 2) % 3], oph[:, j - 2], "u_lo")
            for j, g in enumerate(stage_groups["down"]):
                add_modulated(g, j, 40)

            def add_plain(g, j):
                ps = group(g)
                dve.tensor_tensor(xT[:, 2 * j:2 * j + 2, :], ps, xT[:, 2 * j:2 * j + 2, :], ALU.add).then_inc(sem("dve_read"), 1)

            for l in range(2):
                norm(f"mix{l}", xT, lambda c: col("norm_mix_g_2", DC * l + c))
                dve.wait_ge(sem("mix_padded"), l + 1)
                for t, g in enumerate(stage_groups[f"mixa{l}"]):
                    ps = group(g)
                    dve.wait_ge(sem("ya_sig"), 3 * l + t + 1)
                    dve.tensor_tensor(yap[:, t, 30:30 + T], ps[:, 0], sgm[:, t % 2], ALU.mult).then_inc(sem("dve_read"), 1)
                dve.wait_ge(sem("dve_read"), reads_at[g])
                aw, ab = VROW["conv_a_w_2"] + 93 * l, VROW["conv_a_b_2"] + 3 * l
                taps = [(k, t) for k in range(TAPS_A) for t in range(3)]
                done = {"k": 0}

                def conv_a(n):
                    for k, t in taps[done["k"]:done["k"] + n]:
                        if k == 0:
                            ins = dve.tensor_scalar(y8[:, t], yap[:, t, 0:T], vec[:, aw + t:aw + t + 1], vec[:, ab + t:ab + t + 1],
                                                    ALU.mult, ALU.add)
                        else:
                            dve.wait_ge(sem("conv_taps"), 93 * l + 3 * k + t - 2)
                            ins = dve.scalar_tensor_tensor(y8[:, t], yap[:, t, k:k + T], vec[:, aw + 3 * k + t:aw + 3 * k + t + 1],
                                                           y8[:, t], ALU.mult, ALU.add)
                        ins.then_inc(sem("conv_taps"), 1)
                    done["k"] += n

                dve.wait_ge(sem("mem_rt"), l + 1)
                link(dve.reciprocal(tiny[:, 2, 0:2], tiny[:, 1, 0:2]))
                for i in range(TB):
                    dve.tensor_scalar(m_tok[:, i], m_tok[:, i], tiny[:, 2, i:i + 1], None, ALU.mult).then_inc(sem("mem_scaled"), 1)
                for stage in ("mix_bg", "mix_bgcg", "mix_cg"):
                    ahead(first_slot[stage_groups[f"{stage}{l}"][0]] + 2)
                    conv_a(9)
                mg = VROW["norm_mem_g_2"] + DC * l
                for c in range(DC):
                    dve.wait_ge(sem("mem_hi"), DC * l + c // 2 * 2 + 2)
                    dve.scalar_tensor_tensor(opl[:, c], misc[:, c // 2, (c % 2) * T:(c % 2 + 1) * T], vec[:, mg + c:mg + c + 1],
                                             oph[:, c].bitcast(F32), ALU.mult, ALU.subtract).then_inc(sem("mem_lo"), 1)
                g = stage_groups[f"mix_bin{l}"][0]
                ps = group(g)
                dve.wait_ge(sem("act_read"), reads_at[stage_groups[f"mix_cg{l}"][0]])
                dve.tensor_tensor(prod[:, 0:2, 2:2 + T], ps, cg[:, 0:2, :], ALU.mult).then_inc(sem("dve_read"), 1)
                conv_a(9)
                g = stage_groups[f"mix_binuv{l}"][0]
                ps = group(g)
                dve.wait_ge(sem("mix_v2"), l + 1)
                dve.tensor_tensor(prod[0:64, 2, 2:2 + T], ps[0:64, 0], cg[0:64, 2, :], ALU.mult).then_inc(sem("dve_read"), 1)
                for stage in ("mix_u", "mix_v"):
                    ahead(first_slot[stage_groups[f"{stage}{l}"][0]] + 2)
                    conv_a(9)

                def memory_low(stage, j):
                    ps = group(stage_groups[f"{stage}{l}"][j])
                    dve.wait_ge(sem("kvq_hi"), 12 * l + (j if stage == "xk" else 4 + j) + 1)
                    hi, lo = [b[:, 2 * j:2 * j + 2, :] for b in keys_at] if stage == "xk" else \
                        [b[:, :, j * 256:(j + 1) * 256] for b in values_at]
                    low(lo, ps, hi, "dve_read")

                dve.wait_ge(sem("means_summed"), 2 * l + 1)
                for t in range(3):
                    dve.scalar_tensor_tensor(vb[:, t], misc[:, 0, 0:T], -1.0 / 320, vb[:, t], ALU.mult, ALU.add)\
                        .then_inc(sem("centred"), 1)
                memory_low("xk", 0)
                conv_a(9)
                dve.wait_ge(sem("root_ready"), ROOTS.index(f"v{l}") + 1)
                link(dve.reciprocal(rt[:], rt[:]))
                for t in range(3):
                    ins = dve.scalar_tensor_tensor(vb[:, t], vb[:, t], col("ln_c_g_2", 2 * t + l), rt[:], ALU.mult, ALU.mult)
                link(ins)
                for t in range(3):
                    dve.tensor_scalar(vb[:, t], vb[:, t], col("ln_c_b_2", 2 * t + l), None, ALU.add).then_inc(sem("mix_v_normed"), 1)
                memory_low("xk", 1)
                conv_a(12)
                memory_low("xk", 2)
                conv_a(12)
                memory_low("xk", 3)
                conv_a(93 - done["k"])
                dve.wait_ge(sem("conv_taps"), 93 * (l + 1))
                bw = lambda k, t: col("conv_b_w_2", 6 * t + 3 * l + k)
                dve.wait_ge(sem("dve_read"), reads_at[stage_groups[f"mix_binuv{l}"][0]])
                dve.wait_ge(sem("mix_bg2"), l + 1)
                for t in range(3):
                    p = slice(0, 128) if t < 2 else slice(0, 64)
                    link(dve.tensor_scalar(vcb[p, t], prod[p, t, 0:T], bw(0, t)[p], None, ALU.mult))
                    for k in (1, 2):
                        link(dve.scalar_tensor_tensor(vcb[p, t], prod[p, t, k:k + T], bw(k, t)[p], vcb[p, t], ALU.mult, ALU.add))
                    dve.tensor_tensor(y8[p, 3 + t], y8[p, 3 + t], vcb[p, t], ALU.mult).then_inc(sem("b_done"), 1)
                dve.wait_ge(sem("c_mixed"), l + 1)
                dve.wait_ge(sem("gb_landed"), 80 * (l + 1))
                for t in range(3):
                    p = slice(0, 128) if t else slice(64, 128)
                    ps = misc[p, 2 + t // 2, (t % 2) * T:(t % 2 + 1) * T].rearrange("p (i s) -> p i s", i=TB)
                    tmp = vb[p, t].rearrange("p (i s) -> p i s", i=TB)
                    link(dve.tensor_tensor(tmp, ps, gb[p, t, :].unsqueeze(1).to_broadcast([p.stop - p.start, TB, P]), ALU.add))
                    dve.tensor_tensor(y8[p, 5 + t], y8[p, 5 + t], vb[p, t], ALU.mult).then_inc(sem("c_done"), 1)
                dve.wait_ge(sem("means_summed"), 2 * l + 2)
                for t in range(3):
                    dve.scalar_tensor_tensor(y8[:, t], misc[:, 0, 0:T], -1.0 / 384, y8[:, t], ALU.mult, ALU.add)\
                        .then_inc(sem("centred"), 1)
                memory_low("xv", 0)
                dve.wait_ge(sem("root_ready"), ROOTS.index(f"a{l}") + 1)
                link(dve.reciprocal(rt[:], rt[:]))
                for t in range(3):
                    dve.scalar_tensor_tensor(y8[:, t], y8[:, t], col("ln_a_g_2", 3 * l + t), rt[:], ALU.mult, ALU.mult)\
                        .then_inc(sem("a_scaled"), 1)
                memory_low("xv", 1)
                dve.wait_ge(sem("root_ready"), ROOTS.index(f"y{l}") + 1)
                dve.reciprocal(rt[:], rt[:]).then_inc(sem("y_rs"), 1)
                memory_low("xv", 2)
                for c in range(DC):
                    dve.wait_ge(sem("y_spread"), 4 * l + c // 2 + 1)
                    dve.scalar_tensor_tensor(work[:, c], y8[:, c], col("mix_out_g_2", DC * l + c),
                                             misc[:, c // 2, (c % 2) * T:(c % 2 + 1) * T], ALU.mult, ALU.mult).then_inc(sem("y_scaled"), 1)
                for c in range(DC):
                    dve.wait_ge(sem("y_hi"), DC * l + c + 1)
                    low(hl[:, c], work[:, c], hh[:, c], "y_lo")
                memory_low("xv", 3)
                for j, g in enumerate(stage_groups[f"mixout{l}"]):
                    add_plain(g, j)
                norm(f"x{l}", xT, lambda c: col("norm_x_g_2", DC * l + c))
                for j, g in enumerate(stage_groups[f"xq{l}"]):
                    ps = group(g)
                    dve.wait_ge(sem("kvq_hi"), 12 * l + 8 + j + 1)
                    low(queries[1][:, 2 * j:2 * j + 2, :], ps, queries[0][:, 2 * j:2 * j + 2, :], "dve_read")
                ahead(first_slot[stage_groups[f"xo{l}"][0]] + 2)

                def x_max(h):
                    b = h % 2
                    dve.wait_ge(sem("x_scores"), 4 * l + h + 1)
                    link(dve.tensor_reduce(small[:, b, 0:2], misc[:, b, :].rearrange("p (i m) -> p i m", i=TB), AX_X, ALU.max))
                    dve.tensor_scalar(small[:, b, 2:4], small[:, b, 0:2], -1.0 / 16, None, ALU.mult).then_inc(sem("x_negmax"), 1)

                def x_out_low(h):
                    dve.wait_ge(sem("xo_hi"), 4 * l + h + 1)
                    low(hl[:, 2 * h:2 * h + 2, :], x_bank(l, h).rearrange("p (a b) -> p a b", a=2), hh[:, 2 * h:2 * h + 2, :],
                        "xo_lo")

                x_max(0)
                for h in range(4):
                    if h + 1 < 4:
                        x_max(h + 1)
                    b = h % 2
                    dve.wait_ge(sem("x_exp"), 2 * (4 * l + h + 1))
                    link(dve.reciprocal(small[:, b, 6:8], small[:, b, 4:6]))
                    for i in range(TB):
                        dve.tensor_scalar(xp[:, b, i], xp[:, b, i], small[:, b, 6 + i:7 + i], None, ALU.mult).then_inc(sem("x_p"), 1)
                    dve.wait_ge(sem("x_pt_sb"), 4 * l + h + 1)
                    low(queries[1][:, 2 * h:2 * h + 2, :], misc[:, 2 + h % 2, :].rearrange("p (a b) -> p a b", a=2),
                        queries[0][:, 2 * h:2 * h + 2, :], "x_pt_lo")
                    if h >= 1:
                        x_out_low(h - 1)
                x_out_low(3)
                for j, g in enumerate(stage_groups[f"xo{l}"]):
                    add_plain(g, j)
                norm(f"ffn{l}", xT, lambda c: col("norm_ffn_g_2", DC * l + c))
                if l == 0:
                    ups2 = stage_groups["up2"]
                    for j in range(FC + 1):
                        if j < FC:
                            ps = group(ups2[j])
                            dve.wait_ge(sem("up2_silu"), j + 1)
                            if j >= 3:
                                dve.wait_ge(sem("u2_lo"), j - 2)
                            dve.tensor_tensor(uf[:, j % 3], ps[:, 1], sg[:, j % 3], ALU.mult).then_inc(sem("dve_read"), 1)
                        if j >= 1:
                            dve.wait_ge(sem("u2_hi"), j)
                            low(opl[:, j - 1], uf[:, (j - 1) % 3], oph[:, j - 1], "u2_lo")
                    for j, g in enumerate(stage_groups["down2"]):
                        add_plain(g, j)

            ahead(n_dense - 1)
            dve.wait_ge(sem("moe_consts"), 3)
            dve.wait_ge(sem("logits_done"), 1)
            link(dve.tensor_copy(logit[:], misc[:, 1, 0:TB * NE].rearrange("p (i e) -> p i e", i=TB)))
            for i in range(TB):
                link(dve.max(best[:, i], logit[:, i]))
                link(dve.max_index(besti[:, i], best[:, i], logit[:, i]))
            dve.tensor_tensor(topw[:, :, 0], best[:, :, 1], best[:, :, 0], ALU.subtract).then_inc(sem("top_gap"), 1)
            link(dve.tensor_copy(topw[:, :, 2:4], besti[:, :, 0:2]))
            for i in range(TB):
                for k in range(2):
                    ins = dve.tensor_scalar(pick[:, k, i], iota[:, 0:NE], topw[:, i, 2 + k:3 + k], None, ALU.is_equal)
            link(ins)
            dve.wait_ge(sem("top_exp"), 1)
            link(dve.tensor_scalar(topw[:, :, 2], topw[:, :, 1], 1.0, None, ALU.add))
            link(dve.reciprocal(topw[:, :, 3], topw[:, :, 2]))
            link(dve.tensor_tensor(topw[:, :, 2], topw[:, :, 1], topw[:, :, 3], ALU.mult))
            for i in range(TB):
                link(dve.tensor_scalar(comb[:, i], pick[:, 0, i], topw[:, i, 3:4], None, ALU.mult))
                link(dve.scalar_tensor_tensor(comb[:, i], pick[:, 1, i], topw[:, i, 2:3], comb[:, i], ALU.mult, ALU.add))
            dve.tensor_tensor(pick[:, 0], pick[:, 0], pick[:, 1], ALU.add).then_inc(sem("picked"), 1)
            dve.wait_ge(sem("picked"), 1)
            dve.wait_ge(sem("ranked"), 1)
            link(dve.memset(rankm[:], -1e4))
            link(dve.scalar_tensor_tensor(rankm[:, :, 0:NE], misc[:, 0, 0:TB * NE].rearrange("p (i e) -> p i e", i=TB), 1.0,
                                          pick[:, 0], ALU.add, ALU.mult))
            link(dve.tensor_scalar(rankm[:, :, 0:NE], rankm[:, :, 0:NE], -1.0, None, ALU.add))
            link(dve.tensor_reduce(small[:, 0, 0:1], misc[:, 0, 16:16 + NE], AX_X, ALU.max))
            link(dve.tensor_scalar(small[:, 0, 1:2], small[:, 0, 0:1], float(P), None, ALU.is_gt))
            dve.tensor_copy(flag[0:1, 0:1], small[0:1, 0, 1:2]).then_inc(sem("overflow_known"), 1)
            dve.memset(ye, 0.0).then_inc(sem("m_yc"), 1)
            dve.memset(small[:, 1, 0:1], 0.0).then_inc(sem("m_c"), 1)
            dve.memset(small[:, 1, 1:2], 0.0).then_inc(sem("m_mul"), 2)
            dve.memset(small[:, 1, 2:3], 0.0).then_inc(sem("m_added"), 4)

            def moe_lo(E, k):
                r, q = (n_dense + k) % RAW, (n_split + k) % SPLIT
                dve.wait_ge(sem("hi_ready"), E * MOE_SLOTS + (n_split + k + 1))
                dve.tensor_tensor(wlo[:, q, :], raw[:, r, :], whi[:, q, :].bitcast(F32), ALU.subtract).then_inc(sem("lo_ready"), 1)

            def placed(dst, e, weighted, name):
                for i in range(TB):
                    if weighted:
                        ins = dve.tensor_scalar(dst[:, i], iota, rankm[:, i, bass.ds(e, 1)], comb[:, i, bass.ds(e, 1)],
                                                ALU.is_equal, ALU.mult)
                    else:
                        ins = dve.tensor_scalar(dst[:, i], iota, rankm[:, i, bass.ds(e, 1)], None, ALU.is_equal)
                ins.then_inc(sem(name), 1)

            def added(S):
                for r in range(4):
                    dve.wait_ge(sem("m_s"), S * 4 + (r + 1))
                    dve.tensor_tensor(xT[:, 2 * r:2 * r + 2, :], banks[:, r, :].rearrange("p (a b) -> p a b", a=2),
                                      xT[:, 2 * r:2 * r + 2, :], ALU.add).then_inc(sem("m_added"), 1)

            def moe_expert(e, u, p):
                E, Q = e + NE * p, e + (NE + 1) * p
                st["k"] = 2

                def upto(k):
                    while st["k"] <= k:
                        moe_lo(E, st["k"])
                        st["k"] += 1

                def hidden_lo(j):
                    dve.wait_ge(sem("m_hhi"), E * JE + (j + 1))
                    low(h_lo[j % 2], misc[:, 1 if j == JE - 1 else 0, :], h_hi[j % 2], "m_hlo")

                for j in range(JE):
                    upto(gate_last(j) + 2)
                    if j >= 1:
                        hidden_lo(j - 1)
                    if j == 2:
                        placed(place_w, e, True, "m_gw")
                    if j == 5:
                        placed(place, e + 1, False, "m_gt")
                    upto(gate_last(j) + 4)
                    dve.wait_ge(sem("slot_used"), E * MOE_SLOTS + (n_split + gate_last(j) + 3))
                    dve.wait_ge(sem("m_sil"), E * JE + (j + 1))
                    dve.tensor_tensor(sh[:, j % 2, :], pair[:, j % 2, 1, :], sil[:, j % 2], ALU.mult).then_inc(sem("m_mul"), 1)
                upto(MOE_SLOTS - 1)
                for half in range(2):
                    dve.wait_ge(sem("m_xhi"), Q * 2 + (3 + half))
                    low(xg_lo[1 - u][:, half * 512:(half + 1) * 512], misc[:, 1 - half, :],
                        xg_hi[1 - u][:, half * 512:(half + 1) * 512], "m_xlo")
                hidden_lo(JE - 1)
                added(Q)
                upto(MOE_SLOTS + 1)

            def moe_pass(p):
                if p:
                    dve.tensor_scalar(rankm[:, :, 0:NE], rankm[:, :, 0:NE], -float(P), None, ALU.add).then_inc(sem("pass_ready"), 1)
                    dve.wait_ge(sem("pass_ready"), 2)
                dve.memset(comb_t[:, 1], 0.0).then_inc(sem("pass_ready"), 1)
                dve.wait_ge(sem("pass_ready"), 1 + 2 * p)
                placed(place, 0, False, "m_gt")
                for half in range(2):
                    dve.wait_ge(sem("m_xhi"), 2 * (NE + 1) * p + half + 1)
                    low(xg_lo[0][:, half * 512:(half + 1) * 512], misc[:, 1 - half, :], xg_hi[0][:, half * 512:(half + 1) * 512], "m_xlo")
                with dve.Fori(0, NE // 2) as i:
                    for u in range(2):
                        moe_expert(2 * i + u, u, p)
                added((NE + 1) * p + NE)

            moe_lo(0, 0)
            moe_lo(0, 1)
            dve.wait_ge(sem("hn_turned"), 4)
            moe_pass(0)
            over = dve.value_load(flag[0:1, 0:1], min_val=0, max_val=1)
            with dve.If(over > 0):
                moe_pass(1)
                dve.wait_ge(sem("m_added"), 8 * (NE + 1) + 4)
            dve.wait_ge(sem("m_added"), 4 * (NE + 1) + 4)
            dve.memset(small[:, 1, 3:4], 0.0).then_inc(sem("moe_added"), 1)
            dve.wait_ge(sem("fin_act"), 3)
            link(dve.reciprocal(rt[:], rt[:]))
            for c in range(DC):
                dve.scalar_tensor_tensor(work[:, c], xT[:, c], col("norm_final_g_2", c), rt[:], ALU.mult, ALU.mult)\
                    .then_inc(sem("fin_scaled"), 1)


_INS = ['x', 'c', 'w_mod', 'b_mod', 'norm_mix', 'norm_ffn', 'w_in', 'qnorm_a', 'knorm_a', 'sinks', 'rnn_conv_w',
        'rnn_conv_b', 'rnn_gate_a_w', 'rnn_gate_a_b', 'rnn_gate_x_w', 'rnn_gate_x_b', 'rnn_lambda', 'qnorm_c',
        'knorm_c', 'rel_bias', 'w_branch', 'w_out', 'w_up', 'ffn_conv_w', 'ffn_conv_b', 'w_down', 'mem_2',
        'norm_mix_g_2', 'w_in_2', 'conv_a_w_2', 'conv_a_b_2', 'ln_a_g_2', 'ln_a_b_2', 'conv_b_w_2', 'ln_c_g_2',
        'ln_c_b_2', 'gmlp_ws_2', 'gmlp_b_2', 'mix_out_g_2', 'w_mix_out_2', 'norm_x_g_2', 'norm_mem_g_2', 'w_xq_2',
        'w_xkv_2', 'w_xo_2', 'norm_ffn_g_2', 'ffn_w_gate_2', 'ffn_w_up_2', 'ffn_w_down_2', 'moe_router_2',
        'moe_w_gate_2', 'moe_w_up_2', 'moe_w_down_2', 'norm_final_g_2']


def lay_out(nc, inputs):
    arrays, w = {}, {}
    for name in _INS:
        a = np.ascontiguousarray(inputs[name])
        arrays[f"in_{name}_dram"] = a
        w[name] = nc.dram_tensor(f"in_{name}_dram", a.shape, mybir.dt.from_np(a.dtype), kind="ExternalInput").ap()
    arrays["bucket_onehot_dram"] = bucket_onehot()
    onehot = nc.dram_tensor("bucket_onehot_dram", (32, T), F32, kind="ExternalInput").ap()
    out = nc.dram_tensor("out_0_dram", (1, T, D), F32, kind="ExternalOutput").ap()
    bias_dram = nc.dram_tensor("bias_rows", (NHEAD, 512), F32).ap()
    build_program(nc, w, onehot, out, bias_dram)
    return arrays


def kernel(**inputs):
    import concourse.bacc as _bacc
    from concourse.bass_utils import run_bass_kernel_spmd as _run

    nc = _bacc.Bacc("TRN2", target_bir_lowering=False, num_devices=1)
    arrays = lay_out(nc, inputs)
    r = _run(nc, [arrays], core_ids=[0])
    return r.results[0]["out_0_dram"]
```
